# Optimizing a Trainium2 kernel written in Bass

```python
import math
import jax, jax.numpy as jnp
from jax import lax
import numpy as np

D_MODEL = 1024
BATCH = 1
SEQ = 512
DEPTH = 1

SSM_WIDTH = D_MODEL // 2
SSM_GROUP = 16
SSM_GROUPS = SSM_WIDTH // SSM_GROUP
SSM_STATE = 64
SSM_CHUNK_MAX = 512
DT_MIN = 1e-3
DT_MAX = 1e-1
ATTN_HEADS = 8
HEAD_DIM = 64
ATTN_WIDTH = ATTN_HEADS * HEAD_DIM
IDX_HEADS = 8
IDX_DIM = 64
IDX_SCALE = (IDX_HEADS * IDX_DIM) ** -0.5
TOPK_MAX = 256
Q_BLOCK = 128
RMS_EPS = 1e-6

IN_WIDTHS = (
    SSM_WIDTH,
    SSM_WIDTH,
    ATTN_WIDTH,
    HEAD_DIM,
    HEAD_DIM,
    ATTN_WIDTH,
    IDX_HEADS * IDX_DIM,
    IDX_DIM,
    IDX_HEADS,
    D_MODEL,
    D_MODEL,
)
IN_COLS = sum(IN_WIDTHS)
IN_SPLITS = tuple(int(s) for s in np.cumsum(IN_WIDTHS)[:-1])


def rms_norm(x, g):
    x32 = x.astype(jnp.float32)
    y = x32 * lax.rsqrt(jnp.mean(x32 * x32, axis=-1, keepdims=True) + RMS_EPS)
    return (y * g.astype(jnp.float32)).astype(x.dtype)

def _complex_affine_combine(e1, e2):
    a1r, a1i, b1r, b1i = e1
    a2r, a2i, b2r, b2i = e2
    return (a1r * a2r - a1i * a2i,
            a1r * a2i + a1i * a2r,
            a2r * b1r - a2i * b1i + b2r,
            a2r * b1i + a2i * b1r + b2i)

def s5_mixer(u, a_re, a_im, b_re, b_im, c_re, c_im, d_skip, log_dt):
    bsz, seq_len, _ = u.shape
    f32 = jnp.float32
    ar, ai = a_re.astype(f32), a_im.astype(f32)
    dt = jnp.exp(log_dt.astype(f32))[:, None]
    mag = jnp.exp(ar * dt)
    abar_r, abar_i = mag * jnp.cos(ai * dt), mag * jnp.sin(ai * dt)
    den = ar * ar + ai * ai
    nr = abar_r - 1.0
    cr = (nr * ar + abar_i * ai) / den
    ci = (abar_i * ar - nr * ai) / den
    br, bi = b_re.astype(f32), b_im.astype(f32)
    bb_r = cr[..., None] * br - ci[..., None] * bi
    bb_i = cr[..., None] * bi + ci[..., None] * br
    cre, cim = c_re.astype(f32), c_im.astype(f32)

    chunk = math.gcd(seq_len, SSM_CHUNK_MAX)
    n_chunks = seq_len // chunk
    ug = u.astype(f32).reshape(bsz, n_chunks, chunk, SSM_GROUPS, SSM_GROUP)
    ug = ug.transpose(1, 0, 2, 3, 4)

    def chunk_step(h0, u_c):
        h0r, h0i = h0
        bu_r = jnp.einsum('btgp,gnp->btgn', u_c, bb_r)
        bu_i = jnp.einsum('btgp,gnp->btgn', u_c, bb_i)
        a_r = jnp.broadcast_to(abar_r, bu_r.shape)
        a_i = jnp.broadcast_to(abar_i, bu_i.shape)
        cum_r, cum_i, hl_r, hl_i = lax.associative_scan(
            _complex_affine_combine, (a_r, a_i, bu_r, bu_i), axis=1)
        h_r = hl_r + cum_r * h0r[:, None] - cum_i * h0i[:, None]
        h_i = hl_i + cum_r * h0i[:, None] + cum_i * h0r[:, None]
        y = (jnp.einsum('btgn,gpn->btgp', h_r, cre)
             - jnp.einsum('btgn,gpn->btgp', h_i, cim))
        return (h_r[:, -1], h_i[:, -1]), y

    h_init = (jnp.zeros((bsz, SSM_GROUPS, SSM_STATE), f32),
              jnp.zeros((bsz, SSM_GROUPS, SSM_STATE), f32))
    _, y = lax.scan(chunk_step, h_init, ug)
    y = y.transpose(1, 0, 2, 3, 4).reshape(bsz, seq_len, SSM_WIDTH)
    y = y + d_skip.astype(f32) * u.astype(f32)
    return y.astype(u.dtype)

def dsa_mixer(q, k, v, q_idx, k_idx, w_idx):
    bsz, seq_len = q.shape[0], q.shape[1]
    f32 = jnp.float32
    top_k = min(TOPK_MAX, seq_len // 4)
    n_blocks = seq_len // Q_BLOCK
    key_pos = jnp.arange(seq_len)
    k_idx32 = k_idx.astype(f32)
    attn_scale = HEAD_DIM ** -0.5

    def to_blocks(t):
        return t.reshape((bsz, n_blocks, Q_BLOCK) + t.shape[2:]).swapaxes(0, 1)

    def block(args):
        blk, qb, qib, wb = args
        q_pos = blk * Q_BLOCK + jnp.arange(Q_BLOCK)
        causal = key_pos[None, :] <= q_pos[:, None]
        s = jax.nn.relu(jnp.einsum('bqhd,bkd->bqhk', qib.astype(f32), k_idx32)) * IDX_SCALE
        score = jnp.einsum('bqh,bqhk->bqk', wb.astype(f32), s)
        score = jnp.where(causal[None], score, -jnp.inf)
        _, sel = lax.top_k(score, top_k)
        valid = sel <= q_pos[None, :, None]
        k_sel = jax.vmap(lambda kk, ii: kk[ii])(k, sel)
        v_sel = jax.vmap(lambda vv, ii: vv[ii])(v, sel)
        logits = jnp.einsum('bqhd,bqkd->bqhk', qb.astype(f32), k_sel.astype(f32)) * attn_scale
        logits = jnp.where(valid[:, :, None, :], logits, -jnp.inf)
        p = jax.nn.softmax(logits, axis=-1)
        o = jnp.einsum('bqhk,bqkd->bqhd', p, v_sel.astype(f32))
        return o.astype(qb.dtype)

    out = lax.map(block, (jnp.arange(n_blocks), to_blocks(q), to_blocks(q_idx), to_blocks(w_idx)))
    return out.swapaxes(0, 1).reshape(bsz, seq_len, ATTN_WIDTH)

def hybrid_layer(x, c, norm_g, w_mod, b_mod, w_in, a_re, a_im, b_re, b_im, c_re, c_im,
                 d_skip, log_dt, w_glu, b_glu, w_a_o, w_b_o, w_out):
    bsz, seq_len, _ = x.shape
    mod = jax.nn.silu(c) @ w_mod + b_mod
    shift, scale, gate = jnp.split(mod, 3, axis=-1)
    h = rms_norm(x, norm_g) * (1 + scale[:, None]) + shift[:, None]
    proj = h @ w_in
    xa, za, q, k, v, zb, qi, ki, wi, ga, gb = jnp.split(proj, IN_SPLITS, axis=-1)

    ya = jax.nn.gelu(s5_mixer(xa, a_re, a_im, b_re, b_im, c_re, c_im, d_skip, log_dt))
    g = ya @ w_glu + b_glu
    ya = g[..., :SSM_WIDTH] * jax.nn.sigmoid(g[..., SSM_WIDTH:])
    ya = (ya * jax.nn.silu(za)) @ w_a_o

    yb = dsa_mixer(q.reshape(bsz, seq_len, ATTN_HEADS, HEAD_DIM), k, v,
                   qi.reshape(bsz, seq_len, IDX_HEADS, IDX_DIM), ki, wi)
    yb = (yb * jax.nn.silu(zb)) @ w_b_o

    merged = jax.nn.sigmoid(ga) * ya + jax.nn.sigmoid(gb) * yb
    return x + gate[:, None] * (merged @ w_out)

def first_inputs(seed: int = 0) -> dict:
    key = jax.random.key(seed)
    ks = jax.random.split(key, 20)
    f32 = jnp.float32
    G, N, P = SSM_GROUPS, SSM_STATE, SSM_GROUP

    def nrm(k, shape, std):
        return jax.random.normal(k, shape, f32) * std

    n_idx = jnp.arange(N, dtype=f32)
    return {
        "x": nrm(ks[0], (BATCH, SEQ, D_MODEL), 1.0),
        "c": nrm(ks[1], (BATCH, D_MODEL), 1.0),
        "norm_g": 1.0 + nrm(ks[2], (DEPTH, D_MODEL), 0.02),
        "w_mod": nrm(ks[3], (DEPTH, D_MODEL, 3 * D_MODEL), 0.5 * D_MODEL ** -0.5),
        "b_mod": nrm(ks[4], (DEPTH, 3 * D_MODEL), 0.01),
        "w_in": nrm(ks[5], (DEPTH, D_MODEL, IN_COLS), D_MODEL ** -0.5),
        "a_re": -0.5 + nrm(ks[6], (DEPTH, G, N), 0.01),
        "a_im": math.pi * n_idx + nrm(ks[7], (DEPTH, G, N), 0.01),
        "b_re": nrm(ks[8], (DEPTH, G, N, P), (2 * P) ** -0.5),
        "b_im": nrm(ks[9], (DEPTH, G, N, P), (2 * P) ** -0.5),
        "c_re": nrm(ks[10], (DEPTH, G, P, N), N ** -0.5),
        "c_im": nrm(ks[11], (DEPTH, G, P, N), N ** -0.5),
        "d_skip": nrm(ks[12], (DEPTH, SSM_WIDTH), 1.0),
        "log_dt": jax.random.uniform(ks[13], (DEPTH, G), f32,
                                     minval=math.log(DT_MIN), maxval=math.log(DT_MAX)),
        "w_glu": nrm(ks[14], (DEPTH, SSM_WIDTH, 2 * SSM_WIDTH), SSM_WIDTH ** -0.5),
        "b_glu": nrm(ks[15], (DEPTH, 2 * SSM_WIDTH), 0.01),
        "w_a_o": nrm(ks[16], (DEPTH, SSM_WIDTH, D_MODEL), SSM_WIDTH ** -0.5),
        "w_b_o": nrm(ks[17], (DEPTH, ATTN_WIDTH, D_MODEL), ATTN_WIDTH ** -0.5),
        "w_out": nrm(ks[18], (DEPTH, D_MODEL, D_MODEL), D_MODEL ** -0.5),
        "final_g": 1.0 + nrm(ks[19], (D_MODEL,), 0.02),
    }

def first_block(x, c, norm_g, w_mod, b_mod, w_in, a_re, a_im, b_re, b_im, c_re, c_im,
              d_skip, log_dt, w_glu, b_glu, w_a_o, w_b_o, w_out, final_g):
    for l in range(DEPTH):
        x = hybrid_layer(x, c, norm_g[l], w_mod[l], b_mod[l], w_in[l], a_re[l], a_im[l],
                         b_re[l], b_im[l], c_re[l], c_im[l], d_skip[l], log_dt[l],
                         w_glu[l], b_glu[l], w_a_o[l], w_b_o[l], w_out[l])
    return rms_norm(x, final_g)


N_HEADS = 16
HEAD_DIM_2 = D_MODEL // N_HEADS
D_ATTN = N_HEADS * HEAD_DIM_2
BLOCK_Q = 128
SB_SCALE = HEAD_DIM_2 ** -0.5
POOL_WINDOWS = (2, 4, 8, 16)
N_POOL_GROUPS = len(POOL_WINDOWS)
D_POOL = D_MODEL
POOL_GROUP_DIM = D_POOL // N_POOL_GROUPS
SPLITS = (D_ATTN, D_ATTN, D_ATTN, D_ATTN, D_POOL, D_POOL, D_MODEL, D_MODEL)
IN_COLS_2 = sum(SPLITS)
EPS = 1e-6


def rms_norm_2(x, gain):
    xf = x.astype(jnp.float32)
    y = xf * lax.rsqrt(jnp.mean(xf * xf, axis=-1, keepdims=True) + EPS)
    return (y * gain.astype(jnp.float32)).astype(x.dtype)

def stick_breaking_attention(q, k, v):
    S = q.shape[2]
    outs = []
    for i in range(S // BLOCK_Q):
        q0, q1 = i * BLOCK_Q, (i + 1) * BLOCK_Q
        qb = q[:, :, q0:q1]
        kb = k[:, :, :q1]
        vb = v[:, :, :q1]
        z = jnp.einsum('bhqd,bhkd->bhqk', qb, kb).astype(jnp.float32) * SB_SCALE
        q_pos = jnp.arange(q0, q1)[:, None]
        k_pos = jnp.arange(q1)[None, :]
        mask = k_pos < q_pos
        log_1m_beta = jnp.where(mask, -jax.nn.softplus(z), 0.0)
        suffix = lax.cumsum(log_1m_beta, axis=3, reverse=True) - log_1m_beta
        w = jnp.where(mask, jnp.exp(jax.nn.log_sigmoid(z) + suffix), 0.0)
        outs.append(jnp.einsum('bhqk,bhkd->bhqd', w.astype(vb.dtype), vb))
    return jnp.concatenate(outs, axis=2)

def multiscale_causal_pool(u, pool_w, pool_scale):
    B, S, _ = u.shape
    uf = u.astype(jnp.float32)
    pos_count = jnp.arange(S) + 1
    diffs = []
    for g, win in enumerate(POOL_WINDOWS):
        ug = uf[:, :, g * POOL_GROUP_DIM:(g + 1) * POOL_GROUP_DIM]
        cs = jnp.cumsum(ug, axis=1)
        cs_shift = jnp.pad(cs, ((0, 0), (win, 0), (0, 0)))[:, :S]
        count = jnp.minimum(pos_count, win).astype(jnp.float32)[None, :, None]
        diffs.append((cs - cs_shift) / count - ug)
    d = jnp.stack(diffs, axis=2).astype(u.dtype)
    mixed = jnp.einsum('bsgc,gcd->bsgd', d, pool_w).reshape(B, S, D_POOL)
    return mixed * pool_scale

def hybrid_layer_2(x, c, norm_gain, w_ada, b_ada, w_in, pool_w, pool_scale,
                 w_branch_a, w_branch_b, w_out):
    B, S, D = x.shape
    mod = jax.nn.silu(c) @ w_ada + b_ada
    shift, scale, gate = jnp.split(mod, 3, axis=-1)
    h = rms_norm_2(x, norm_gain) * (1.0 + scale[:, None, :]) + shift[:, None, :]

    proj = h @ w_in
    offs = np.cumsum(SPLITS)[:-1].tolist()
    q, k, v, z_a, u, z_b, m_a, m_b = jnp.split(proj, offs, axis=-1)

    to_heads = lambda t: t.reshape(B, S, N_HEADS, HEAD_DIM_2).transpose(0, 2, 1, 3)
    attn = stick_breaking_attention(to_heads(q), to_heads(k), to_heads(v))
    attn = attn.transpose(0, 2, 1, 3).reshape(B, S, D_ATTN)
    p_a = (attn * jax.nn.silu(z_a)) @ w_branch_a

    pooled = multiscale_causal_pool(u, pool_w, pool_scale)
    p_b = (pooled * jax.nn.silu(z_b)) @ w_branch_b

    merged = jax.nn.sigmoid(m_a) * p_a + jax.nn.sigmoid(m_b) * p_b
    out = merged @ w_out
    return x + gate[:, None, :] * out

def second_inputs(seed: int = 0) -> dict:
    key = jax.random.key(seed)
    ks = jax.random.split(key, 13)
    f32 = jnp.float32
    nrm = lambda k, shape, s: jax.random.normal(k, shape, f32) * s
    return {
        "x": nrm(ks[0], (BATCH, SEQ, D_MODEL), 1.0),
        "c": nrm(ks[1], (BATCH, D_MODEL), 1.0),
        "norm_gain": 1.0 + nrm(ks[2], (DEPTH, D_MODEL), 0.05),
        "w_ada": nrm(ks[3], (DEPTH, D_MODEL, 3 * D_MODEL), 0.5 * D_MODEL ** -0.5),
        "b_ada": nrm(ks[4], (DEPTH, 3 * D_MODEL), 0.01),
        "w_in": nrm(ks[5], (DEPTH, D_MODEL, IN_COLS_2), D_MODEL ** -0.5),
        "pool_w": nrm(ks[6], (DEPTH, N_POOL_GROUPS, POOL_GROUP_DIM, POOL_GROUP_DIM), POOL_GROUP_DIM ** -0.5),
        "pool_scale": 1.0 + nrm(ks[7], (DEPTH, D_POOL), 0.1),
        "w_branch_a": nrm(ks[8], (DEPTH, D_ATTN, D_MODEL), D_ATTN ** -0.5),
        "w_branch_b": nrm(ks[9], (DEPTH, D_POOL, D_MODEL), D_POOL ** -0.5),
        "w_out": nrm(ks[10], (DEPTH, D_MODEL, D_MODEL), D_MODEL ** -0.5),
        "final_gain": 1.0 + nrm(ks[11], (D_MODEL,), 0.05),
    }

def second_block(x, c, norm_gain, w_ada, b_ada, w_in, pool_w, pool_scale,
              w_branch_a, w_branch_b, w_out, final_gain):
    for l in range(DEPTH):
        x = hybrid_layer_2(x, c, norm_gain[l], w_ada[l], b_ada[l], w_in[l], pool_w[l],
                         pool_scale[l], w_branch_a[l], w_branch_b[l], w_out[l])
    return rms_norm_2(x, final_gain)


def setup_inputs(seed=0):
    out = dict(first_inputs(seed))
    for name, value in second_inputs(seed + 1).items():
        if name != "x":
            out[name + "_2"] = value
    return out


def reference(
    x, c, norm_g, w_mod, b_mod, w_in, a_re, a_im, b_re, b_im, c_re, c_im, d_skip, log_dt, w_glu,
    b_glu, w_a_o, w_b_o, w_out, final_g, c_2, norm_gain_2, w_ada_2, b_ada_2, w_in_2, pool_w_2,
    pool_scale_2, w_branch_a_2, w_branch_b_2, w_out_2, final_gain_2,
):
    x = first_block(
        x, c, norm_g, w_mod, b_mod, w_in, a_re, a_im, b_re, b_im, c_re, c_im, d_skip, log_dt,
        w_glu, b_glu, w_a_o, w_b_o, w_out, final_g,
    )
    return second_block(
        x, c_2, norm_gain_2, w_ada_2, b_ada_2, w_in_2, pool_w_2, pool_scale_2, w_branch_a_2,
        w_branch_b_2, w_out_2, final_gain_2,
    )


_drawn_inputs = setup_inputs


def setup_inputs(seed=0):
    import zlib

    import numpy as np

    out = dict(_drawn_inputs(seed))
    spreads = {}
    factors = {'norm_g': 8.0,
     'b_mod': 8.0,
     'a_re': 64.0,
     'a_im': 64.0,
     'b_re': 64.0,
     'b_im': 64.0,
     'c_re': 64.0,
     'c_im': 64.0,
     'log_dt': 64.0,
     'b_glu': 30.366,
     'final_g': 2.806,
     'norm_gain_2': 5.691,
     'b_ada_2': 8.0,
     'pool_scale_2': 5.416}
    for name, (base, spread) in spreads.items():
        noise = np.random.default_rng([zlib.crc32(name.encode()), seed]).standard_normal(out[name].shape)
        drawn = base * np.exp(spread * noise) if base else spread * noise
        out[name] = __import__('jax').numpy.asarray(drawn.astype(out[name].dtype))
    for name, factor in factors.items():
        out[name] = (out[name] * factor).astype(out[name].dtype)
    return out
```

```python
import concourse.bass as bass
from concourse import mybir
from contextlib import ExitStack
import math


class Item:

    def __init__(self, fixed, trip=None, per=0):
        self.fixed, self.trip, self.per = fixed, trip, per

    def __add__(self, k):
        return Item(self.fixed + k, self.trip, self.per)

    def value(self, add=0):
        return self.fixed + add + (0 if self.trip is None else self.trip * self.per)

    def turns(self, ring, times=1, add=0):
        return (self.fixed // ring) * times + add + (0 if self.trip is None else self.trip * (self.per // ring * times))

    def slot(self, ring):
        return self.fixed % ring


class Steps:

    def __init__(self, engine, sem):
        self.engine, self.sem, self.base, self.k = engine, sem, 0, 0

    def do(self, instruction):
        instruction.then_inc(self.sem, 1)
        self.k += 1

    def settle(self):
        self.engine.wait_ge(self.sem, self.base + self.k)

    def link(self, instruction):
        self.do(instruction)
        self.settle()

    def begin_loop(self):
        self.start, self.k = self.base + self.k, 0

    def begin_trip(self, trip, per):
        self.base, self.k, self.per = self.start + trip * per, 0, per

    def end_loop(self, trips):
        assert self.k == self.per, (self.k, self.per)
        self.base, self.k = self.start + trips * self.per, 0


def hybrid_two_layers(nc, x, c, norm_g, w_mod, b_mod, w_in, a_re, a_im, b_re, b_im, c_re, c_im, d_skip, log_dt,
                      w_glu, b_glu, w_a_o, w_b_o, w_out, final_g, c_2, norm_gain_2, w_ada_2, b_ada_2, w_in_2,
                      pool_w_2, pool_scale_2, w_branch_a_2, w_branch_b_2, w_out_2, final_gain_2, out):
    fp32, fp32r, i32 = mybir.dt.float32, mybir.dt.float32r, mybir.dt.int32
    ALU, ACT, AX = mybir.AluOpType, mybir.ActivationFunctionType, mybir.AxisListType

    P = 128
    S, D = x.shape[1], x.shape[2]
    TT, FT = S // P, D // P
    DH = 64
    G, N, GP = b_re.shape[1], b_re.shape[2], b_re.shape[3]
    ST = G * N // P
    L = P // GP
    NCH = S // L
    TOPK, H1, H2 = 128, 8, 16
    IDX_SCALE = float(H1 * DH) ** -0.5
    EPS = 1e-6
    NEG, TAKEN = -1e30, -3e38
    WINDOWS = (2, 4, 8, 16)

    XA, KI, KV, QI, ZA, ZB, Q1, GLU, GATE, WO = 0, 4, 5, 6, 10, 14, 18, 22, 30, 62
    L2, MA, POOLW, MB, WO2, END = 70, 118, 134, 142, 158, 166
    NMOD = 3 * FT
    C_XA, C_ZA, C_Q, C_K, C_ZB, C_QI, C_KI, C_GA, C_GB = 0, 512, 1024, 1536, 1664, 2176, 2688, 2760, 3784

    def by_rows(w):
        return w.rearrange("(k p) n -> p k n", p=P)

    w_mod1, w_mod2 = by_rows(w_mod[0]), by_rows(w_ada_2[0])
    w_in1, w_in2 = by_rows(w_in[0]), by_rows(w_in_2[0])
    glu_w, ao_w, bo_w, out_w1 = by_rows(w_glu[0]), by_rows(w_a_o[0]), by_rows(w_b_o[0]), by_rows(w_out[0])
    pa_w, pb_w, out_w2 = by_rows(w_branch_a_2[0]), by_rows(w_branch_b_2[0]), by_rows(w_out_2[0])
    pool_w = pool_w_2[0].rearrange("g (k p) n -> p g k n", p=P)
    x_v = x[0].rearrange("(t p) d -> p t d", p=P)
    out_v = out[0].rearrange("(t p) d -> p t d", p=P)

    def rows(v):
        return v.rearrange("(r c) -> r c", c=P)

    ctx = ExitStack()
    with ctx:
        def sb(name, shape, dt=fp32):
            return ctx.enter_context(nc.sbuf_tensor(name, shape, dt))

        def sem(name):
            return ctx.enter_context(nc.semaphore(name))

        x_tok = sb("x_tok", [P, TT, D])
        AH, AL = sb("AH", [P, FT, S], fp32r), sb("AL", [P, FT, S], fp32r)
        BH, BL = sb("BH", [P, FT, S], fp32r), sb("BL", [P, FT, S], fp32r)
        raw = sb("raw", [P, 4, FT * P])
        WH, WL = sb("WH", [P, 2, FT * P], fp32r), sb("WL", [P, 2, FT * P], fp32r)
        tmpf = sb("tmpf", [P, 2, S])
        vcol, vcol2 = sb("vcol", [P, P]), sb("vcol2", [P, P])
        ident = sb("ident", [P, P])
        tri1, tri2 = sb("tri1", [P, P]), sb("tri2", [P, P])
        silc, mod1, mod2, gs = sb("silc", [P, 3, FT]), sb("mod1", [P, NMOD]), sb("mod2", [P, NMOD]), sb("gs", [P, 2, FT])
        stat, diag = sb("stat", [P, 8, TT]), sb("diag", [P, TT, P])
        vtok, wtok, m8 = sb("vtok", [P, TT, DH]), sb("wtok", [P, TT, H1]), sb("m8", [P, 3, 8])
        hs = sb("hs", [P, 8, TT])
        rc = sb("rc", [P, 16])
        arena = sb("arena", [P, 21284])
        pp = sb("pp", [P, 24, ST])
        ppi = sb("ppi", [P, 2, ST], i32)
        sc = sb("sc", [P, 2, 2, ST])
        PS = ctx.enter_context(nc.psum_tensor("PS", [P, 8, 512], fp32))
        Z0, Z1, Z2, T0, T1, M0 = 2, 3, 4, 5, 6, 7

        def at(start, *dims, parts=P):
            n = 1
            for d in dims:
                n *= d
            v = arena[0:parts, start:start + n]
            if len(dims) == 1:
                return v
            names = "abcde"[:len(dims)]
            return v.rearrange(f"p ({' '.join(names)}) -> p {' '.join(names)}",
                               **{k: d for k, d in zip(names, dims)})

        E = at(0, 2, ST, L + 1, GP)
        Cin = at(4608, 2, 4, 2, N)
        vrow = at(6144, 2, P)
        Bin = at(5632, 2, ST, GP)
        Dt = at(4608, G, L, GP)
        Kraw = at(8704, G, P, parts=GP)
        U = at(8704, G, NCH)
        X = at(10752, L, L, GP, parts=NCH)
        Hs = at(10752, NCH + 1, 2, ST)
        G1T = at(12832, ST, 2, P)
        GB = at(16928, 2, ST, L, GP)
        xaT = at(16928, 4, S)
        BU = at(18976, ST, 2, NCH)
        Y = at(18976, L, P, parts=NCH)
        kiw, kv, qi_s = at(12832, S), at(13344, S), at(13856, S)
        rl, score = at(14368, 1280), at(15648, 1280)
        work = at(20000, 1280)
        sza, szb = at(0, 4, S), at(2048, 4, S)
        ya2 = at(4096, 4, S)
        q_s, lg = at(6656, 2, S), at(7680, 1280)
        pT, o_s = at(8960, 10, P), at(10240, TT, P)
        gates, parts_ab = at(12832, 2, S), at(13856, 2, S)
        merged1 = at(16928, FT, S)
        gain = at(0, D)
        uT, szb2 = at(0, FT, S), at(4096, FT, S)
        q2, k2, v2, v2tok = at(8192, S), at(8704, S), at(9216, S), at(9728, TT, P)
        beta, om, Pw = at(10240, 1280), at(11520, 1280), at(12800, 1284)
        wT, sza2, o2 = at(14084, 10, P), at(15364, S), at(15876, TT, P)
        zeros = at(16388, S)
        mod_ring = at(6144, 4, FT * P)
        part_a, merged2 = at(8192, FT, S), at(12288, FT, S)
        wide, gates2, prod2 = at(16384, 2, S), at(17408, S), at(17920, S)
        junk = tmpf[:, :, :].rearrange("p a b -> p (a b)")

        (consts, rows_zero, rows_in, x_in, b_in, c_in, gain_in, cols_t, c_t, gb_t, gb_c, k_t, k_c, silc_ok, mod_done,
         mod_ok, sumsq, root, diag_ok, ht, hv, hh, hl, raw_free_, h_ready, l_ready, tile_done, xa_ok, gb_ok, e_ok, dt_zero,
         dt_in) = [sem(n) for n in (
             "consts rows_zero rows_in x_in b_in c_in gain_in cols_t c_t gb_t gb_c k_t k_c silc_ok mod_done mod_ok sumsq "
             "root diag_ok ht hv hh hl raw_free h_ready l_ready tile_done xa_ok gb_ok e_ok dt_zero dt_in").split()]
        raw_in = [sem(f"raw_in{i}") for i in range(4)]
        mod_in = [sem(f"mod_in{i}") for i in range(4)]
        p_free = [sem(f"p_free{i}") for i in range(2)]
        (pe_s, act_s, dve_s, pool_s) = [sem(n) for n in ("pe_step", "act_step", "dve_step", "pool_step")]
        (xt, xc, ut, uc, but, buc, scanned, yt, yc, y2t, ya_ok, sin_in, sin_ok, cols_ok, gate_sig, sig_read) = [
            sem(n) for n in ("xt xc ut uc but buc scanned yt yc y2t ya_ok sin_in sin_ok cols_ok gate_sig "
                             "sig_read").split()]
        (ki_c, ki_dup, k_c1, k_dup, ki_t, wtok_ok, v_t, vtok_ok, qi_c, idx_s, idx_r, idx_w, amask_ok) = [
            sem(n) for n in "ki_c ki_dup k_c1 k_dup ki_t wtok_ok v_t vtok_ok qi_c idx_s idx_r idx_w amask_ok".split()]
        (q_c, z_ready, z_read, nmax_ok, probs_ok, t_ready, t_copied, o_ready, o_copied, feats_t, feats_c, yb_v, yb_h,
         yb_l, ya2_ok, ya2_h, ya2_l, mg_ok, mg_h, mg_l, wo_v, wo_t, wo_add, x1_ok, out_done, z_gates) = [
            sem(n) for n in ("q_c z_ready z_read nmax_ok probs_ok t_ready t_copied o_ready o_copied feats_t feats_c yb_v "
                             "yb_h yb_l ya2_ok ya2_h ya2_l mg_ok mg_h mg_l wo_v wo_t wo_add x1_ok out_done z_gates"
                             ).split()]
        (v2_t, v2_c, d_ok, d_h, d_l, pw_v, pw_h, pw_l, y2b_ok, head2_m, ld_rows, mod2_read, ms_ok, sig_c, y_v, gelu_ok,
         yh, gate2_sig, part_a_ok, mg2_ok, mod_gate) = [
            sem(n) for n in ("v2_t v2_c d_ok d_h d_l pw_v pw_h pw_l y2b_ok head2_m ld_rows mod2_read ms_ok sig_c y_v "
                             "gelu_ok yh gate2_sig part_a_ok mg2_ok mod_gate").split()]

        def bank(b):
            return PS[:, b, :]

        V_G1, V_BM1, V_C1, V_BG, V_DS, V_C2, V_G2, V_BM2, V_PS, V_AR = 0, 8, 32, 40, 48, 52, 60, 68, 92, 100
        SEGS = ((3, 0, Z0, 0), (2, 512, Z1, 0), (0, 896, Z1, 384), (1, 1024, Z2, 0))
        BLOCKS = [(q, c0 // P + kb, kb) for q, c0, _, _ in SEGS for kb in range(q + 1)]
        T_GROUPS = ((0, 4), (4, 8), (8, 10))

        def weight_source(n):
            def cols(w, col, kt=FT):
                return w[:, 0:kt, col:col + P], kt
            if n < KI:
                return cols(w_in1, C_XA + n * P)
            if n < QI:
                return cols(w_in1, (C_KI, C_K)[n - KI])
            if n < ZA:
                return cols(w_in1, C_QI + (n - QI) * P)
            if n < ZB:
                return cols(w_in1, C_ZA + (n - ZA) * P)
            if n < Q1:
                return cols(w_in1, C_ZB + (n - ZB) * P)
            if n < GLU:
                return cols(w_in1, C_Q + (n - Q1) * P)
            if n < GATE:
                return cols(glu_w, ((n - GLU) // 2 + 4 * ((n - GLU) % 2)) * P, 4)
            if n < L2:
                return cols(out_w1, (n - WO) * P)
            if n < MA:
                assert False
            if n < MB:
                g, h = (n - POOLW) // 2, (n - POOLW) % 2
                return pool_w[:, g, :, h * P:(h + 1) * P], 2
            return cols(out_w2, (n - WO2) * P)

        def raw_of(n):
            return n + NMOD

        block = ctx.enter_context(nc.Block())

        @block.sync
        def _(sp):
            sp.wait_ge(rows_zero, 2)
            for base, v in ((V_G1, norm_g[0]), (V_BM1, b_mod[0]), (V_C1, c[0]), (V_BG, b_glu[0]), (V_DS, d_skip[0]),
                            (V_C2, c_2[0]), (V_G2, norm_gain_2[0]), (V_BM2, b_ada_2[0]), (V_PS, pool_scale_2[0])):
                n = v.shape[0] // P
                sp.dma_start(vrow[base:base + n, 0, :], rows(v)).then_inc(rows_in, 16)
            for part, v in ((0, a_re), (1, a_im)):
                first = V_AR if part == 0 else 0
                sp.dma_start(vrow[first:first + ST, part, :], v[0].rearrange("(t g) n -> t (g n)", g=2)).then_inc(rows_in, 16)
            sp.dma_start(hs[32:48, 0, 0:2], log_dt[0].rearrange("(t g) -> t g", g=2)).then_inc(rows_in, 16)
            for part, v in ((0, c_re), (1, c_im)):
                for dup in range(2):
                    sp.dma_start(Cin[:, part, :, dup, :],
                                 v[0].rearrange("(f g) p n -> (g p) f n", f=4)).then_inc(c_in, 16)
            for part, v in ((0, b_re), (1, b_im)):
                for half in range(2):
                    sp.dma_start(Bin[half * N:(half + 1) * N, part, :, :],
                                 v[0].rearrange("(t g) n p -> g n t p", g=2)[half]).then_inc(b_in, 16)
            sp.dma_start(x_tok[:, :, :], x_v).then_inc(x_in, 16)

            def load_mod(m, r, w, before):
                if before is not None:
                    sp.wait_ge(*before)
                col = (m % NMOD) * P
                sp.dma_start(raw[:, r % 4, :].rearrange("p (k c) -> p k c", c=P), w[:, :, col:col + P])\
                    .then_inc(raw_in[r % 4], 16)

            def load(r, src, kt):
                sp.dma_start(raw[:, r.slot(4), 0:kt * P].rearrange("p (k c) -> p k c", c=P), src)\
                    .then_inc(raw_in[r.slot(4)], 16)

            users = []
            for m in range(NMOD):
                load_mod(m, m, w_mod1, users[m - 4] if m >= 4 else None)
                users.append((mod_done, m + 1))

            def load_tile(n):
                sp.wait_ge(*users[-4])
                load(Item(raw_of(n)), *weight_source(n))
                users.append((l_ready, n + 1))

            for n in range(GATE):
                load_tile(n)
            with sp.Fori(1, FT // 2 + 1) as i:
                for jj in range(2):
                    for k, (w, col, kt) in enumerate(((w_in1, C_GA, 8), (w_in1, C_GB, 8), (ao_w, 0, 4), (bo_w, 0, 4))):
                        n = Item(GATE + 4 * (jj - 2) + k, i, 8)
                        at_col = i * (2 * P) + (col + (jj - 2) * P)
                        sp.wait_ge(l_ready, n.value(-3))
                        load(n + NMOD, w[:, 0:kt, bass.ds(at_col, P)], kt)
            sp.wait_ge(feats_c, 4)
            sp.wait_ge(ya2_l, 1)
            for m in range(NMOD, 2 * NMOD):
                if m >= NMOD + 4:
                    sp.wait_ge(mod_done, m - 3)
                sp.dma_start(mod_ring[:, m % 4, :].rearrange("p (k c) -> p k c", c=P),
                             w_mod2[:, :, (m - NMOD) * P:(m - NMOD + 1) * P]).then_inc(mod_in[m % 4], 16)
                if m % 3 == 2:
                    n = WO + (m - NMOD) // 3
                    sp.wait_ge(l_ready, n - 3)
                    load(Item(raw_of(n)), *weight_source(n))
            with sp.Fori(1, FT // 2 + 1) as i:
                for jj in range(2):
                    for k, s in enumerate((0, 1, 2, 3, 4, 5)):
                        n = Item(L2 + 6 * (jj - 2) + k, i, 12)
                        at_col = i * (2 * P) + (s * D + (jj - 2) * P)
                        sp.wait_ge(l_ready, n.value(-3))
                        load(n + NMOD, w_in2[:, :, bass.ds(at_col, P)], FT)
            with sp.Fori(1, FT // 2 + 1) as i:
                for jj in range(2):
                    for k, (w, col) in enumerate(((w_in2, 6 * D), (pa_w, 0))):
                        n = Item(MA + 2 * (jj - 2) + k, i, 4)
                        at_col = i * (2 * P) + (col + (jj - 2) * P)
                        sp.wait_ge(l_ready, n.value(-3))
                        load(n + NMOD, w[:, :, bass.ds(at_col, P)], FT)
            for n in range(POOLW, MB):
                sp.wait_ge(l_ready, n - 3)
                load(Item(raw_of(n)), *weight_source(n))
            with sp.Fori(1, FT // 2 + 1) as i:
                for jj in range(2):
                    for k, (w, col) in enumerate(((w_in2, 7 * D), (pb_w, 0))):
                        n = Item(MB + 2 * (jj - 2) + k, i, 4)
                        at_col = i * (2 * P) + (col + (jj - 2) * P)
                        sp.wait_ge(l_ready, n.value(-3))
                        load(n + NMOD, w[:, :, bass.ds(at_col, P)], FT)
            for n in range(WO2, END):
                sp.wait_ge(l_ready, n - 3)
                load(Item(raw_of(n)), *weight_source(n))
            for t in range(TT):
                sp.wait_ge(x1_ok, TT + t + 1)
                sp.dma_start(out_v[:, t, :], x_tok[:, t, :]).then_inc(out_done, 16)
            sp.wait_ge(out_done, 16 * TT)

        @block.gpsimd
        def _(pool):
            steps = Steps(pool, pool_s)
            steps.do(nc.gpsimd.memset(ident[:, :], 0.0))
            steps.do(nc.gpsimd.memset(tri1[:, :], 0.0))
            steps.do(nc.gpsimd.memset(tri2[:, :], 0.0))
            steps.do(nc.gpsimd.memset(wtok[:, :, :], 0.0))
            for t in range(16):
                steps.do(nc.gpsimd.memset(rc[:, t:t + 1], 1.0 / (t + 1)))
            steps.settle()
            steps.do(nc.gpsimd.affine_select(out=ident[:, :], in_=ident[:, :], compare_op=ALU.not_equal, fill=1.0, base=0,
                                             pattern=[[-1, P]], channel_multiplier=1))
            steps.do(nc.gpsimd.affine_select(out=tri1[:, :], in_=tri1[:, :], compare_op=ALU.is_ge, fill=NEG, base=0,
                                             pattern=[[-1, P]], channel_multiplier=1))
            steps.do(nc.gpsimd.affine_select(out=tri2[:, :], in_=tri2[:, :], compare_op=ALU.is_gt, fill=NEG, base=0,
                                             pattern=[[-1, P]], channel_multiplier=1))
            steps.settle()
            nc.gpsimd.memset(pp[:, 23, :], 0.0).then_inc(consts, 1)

            def low(n, kt):
                s, r = n.slot(2), (n + NMOD).slot(4)
                pool.wait_ge(h_ready, n.value(1))
                nc.gpsimd.tensor_tensor(WL[:, s, 0:kt * P], raw[:, r, 0:kt * P], WH[:, s, 0:kt * P].bitcast(fp32),
                                        ALU.subtract).then_inc(l_ready, 1)

            for n in range(GATE):
                low(Item(n), weight_source(n)[1])
            with pool.Fori(0, FT // 2) as i:
                for k in range(8):
                    low(Item(GATE + k, i, 8), 8 if k % 4 < 2 else 4)
            for n in range(WO, L2):
                low(Item(n), FT)
            with pool.Fori(0, FT // 2) as i:
                for k in range(12):
                    low(Item(L2 + k, i, 12), FT)
            with pool.Fori(0, FT // 2) as i:
                for k in range(4):
                    low(Item(MA + k, i, 4), FT)
            for n in range(POOLW, MB):
                low(Item(n), 2)
            with pool.Fori(0, FT // 2) as i:
                for k in range(4):
                    low(Item(MB + k, i, 4), FT)
            for n in range(WO2, END):
                low(Item(n), FT)

        @block.tensor
        def _(pe):
            def product(n, hi, lo, kt, k0=0):
                s = n.slot(2)
                pe.wait_ge(l_ready, n.value(1))
                if n.trip is not None or n.fixed >= 2:
                    pe.wait_ge(p_free[s], n.turns(2))
                for k in range(kt):
                    w_hi, w_lo = WH[:, s, k * P:(k + 1) * P], WL[:, s, k * P:(k + 1) * P]
                    nc.tensor.matmul(bank(s), w_hi, hi[:, k0 + k, :], start=(k == 0), stop=False)
                    nc.tensor.matmul(bank(s), w_hi, lo[:, k0 + k, :], start=False, stop=False)
                    last = nc.tensor.matmul(bank(s), w_lo, hi[:, k0 + k, :], start=False, stop=(k == kt - 1))
                last.then_inc(tile_done, 1)

            def taken_out(n):
                pe.wait_ge(p_free[n.slot(2)], n.turns(2, add=1))

            def modulation(m):
                ring, came = (raw, raw_in) if m < NMOD else (mod_ring, mod_in)
                col = m % NMOD
                pe.wait_ge(came[m % 4], 16 * (m % NMOD // 4 + 1))
                for k in range(FT):
                    last = nc.tensor.matmul(PS[:, M0, 256 + col:257 + col], ring[:, m % 4, k * P:(k + 1) * P],
                                            silc[:, m // NMOD, k:k + 1], start=(k == 0), stop=(k == FT - 1))
                last.then_inc(mod_done, 1)

            def normed_features(layer):
                pe.wait_ge(diag_ok, layer + 1)
                for f in range(FT):
                    if f >= 2:
                        pe.wait_ge(hv, FT * layer + f - 1)
                    for t in range(TT):
                        last = nc.tensor.matmul(PS[:, Z0 + f % 2, t * P:(t + 1) * P], x_tok[:, t, f * P:(f + 1) * P],
                                                diag[:, t, :], start=True, stop=True)
                    last.then_inc(ht, 1)

            def attend_scores(hd, base_q, base_k, h):
                for q, _, b, c in SEGS:
                    last = nc.tensor.matmul(PS[:, b, c:c + (q + 1) * P], base_q[h * DH:(h + 1) * DH, q * P:(q + 1) * P],
                                            base_k[h * DH:(h + 1) * DH, 0:(q + 1) * P], start=True, stop=True)
                last.then_inc(z_ready, 1)

            def attend_values(hd, h, probs, wt, vals):
                pe.wait_ge(probs_ok, hd.value(1))
                for g, (lo, hi) in enumerate(T_GROUPS):
                    if hd.trip is not None or 3 * hd.fixed + g >= 2:
                        pe.wait_ge(t_copied, Item(3 * hd.fixed + g, hd.trip, 3 * hd.per).value(-1))
                    b = T0 + (3 * hd.fixed + g) % 2
                    for n in range(lo, hi):
                        last = nc.tensor.transpose(PS[:, b, (n - lo) * P:(n - lo + 1) * P], probs[:, n * P:(n + 1) * P],
                                                   ident[:, :])
                    last.then_inc(t_ready, 1)
                if hd.trip is not None or hd.fixed >= 1:
                    pe.wait_ge(o_copied, hd.value())
                pe.wait_ge(t_copied, Item(3 * hd.fixed, hd.trip, 3 * hd.per).value(3))
                for q, n, kb in BLOCKS:
                    last = nc.tensor.matmul(PS[:, M0, q * DH:(q + 1) * DH], wt[:, n, :], vals(kb),
                                            start=(kb == 0), stop=(kb == q))
                last.then_inc(o_ready, 1)

            def pair_features(hd, o):
                pe.wait_ge(o_copied, hd.value(1))
                for t in range(TT):
                    last = nc.tensor.transpose(PS[:, M0, t * P:(t + 1) * P], o[:, t, :], ident[:, :])
                last.then_inc(feats_t, 1)

            def out_transposes(j):
                n = Item((WO if j < FT else WO2 - FT) + j)
                taken_out(n)
                if j >= 2:
                    pe.wait_ge(wo_add, j - 1)
                for t in range(TT):
                    last = nc.tensor.transpose(PS[:, T0 + j % 2, t * P:(t + 1) * P], tmpf[:, j % 2, t * P:(t + 1) * P],
                                               ident[:, :])
                last.then_inc(wo_t, 1)

            pe.wait_ge(consts, 1)
            pe.wait_ge(rows_in, 16 * 11)
            pe.wait_ge(ld_rows, 1)
            for part in range(2):
                last = nc.tensor.transpose(PS[:, M0, part * P:(part + 1) * P], vrow[:, part, :], ident[:, :])
            last.then_inc(cols_t, 1)
            pe.wait_ge(c_in, 64)
            for part in range(2):
                for f in range(4):
                    last = nc.tensor.transpose(PS[:, Z0 + part, f * P:(f + 1) * P],
                                               Cin[:, part, f, :, :].rearrange("p a b -> p (a b)"), ident[:, :])
            last.then_inc(c_t, 1)
            pe.wait_ge(silc_ok, 1)
            for m in range(NMOD):
                modulation(m)
            pe.wait_ge(gb_ok, 1)
            for r in range(8):
                if r >= 2:
                    pe.wait_ge(gb_c, r - 1)
                for k in range(4):
                    t, ri = 2 * r + k // 2, k % 2
                    last = nc.tensor.transpose(PS[:, T0 + r % 2, k * P:(k + 1) * P],
                                               GB[:, ri, t, :, :].rearrange("p a b -> p (a b)"), ident[:, :])
                last.then_inc(gb_t, 1)
            pe.wait_ge(e_ok, 1)
            for r in range(8):
                if r >= 2:
                    pe.wait_ge(k_c, r - 1)
                for k in range(4):
                    t, half = 4 * (r // 2) + k, (r % 2) * N
                    for ri in range(2):
                        last = nc.tensor.matmul(PS[0:GP, Z0 + r % 2, k * P:(k + 1) * P], GB[half:half + N, ri, t, 0, :],
                                                E[half:half + N, ri, t, 0:L, :].rearrange("p a b -> p (a b)"),
                                                start=(ri == 0), stop=(ri == 1))
                last.then_inc(k_t, 1)

            pe.wait_ge(k_c, 8)
            normed_features(0)
            pe.wait_ge(hl, FT)
            for n in range(XA, KI):
                product(Item(n), AH, AL, FT)
            for f in range(4):
                taken_out(Item(XA + f))
                if f >= 1:
                    pe.wait_ge(uc, f)
                    pe.wait_ge(buc, f)
                steps_of = xaT[:, f, :].rearrange("p (c j) -> p c j", j=L)
                for s in range(L):
                    last = nc.tensor.transpose(PS[0:NCH, T1 + s // 4, (s % 4) * P:(s % 4 + 1) * P],
                                               steps_of[:, :, L - 1 - s], ident[:, :])
                last.then_inc(xt, 1)
                pe.wait_ge(xc, 2 * f + 2)
                for g in range(L):
                    last = nc.tensor.transpose(PS[:, T1, g * NCH:(g + 1) * NCH], X[:, g, :, :].rearrange("p a b -> p (a b)"),
                                               ident[0:NCH, 0:NCH])
                last.then_inc(ut, 1)
                pe.wait_ge(uc, f + 1)
                for t in range(4):
                    for ri in range(2):
                        for half in range(2):
                            last = nc.tensor.matmul(
                                PS[half * N:(half + 1) * N, M0, (2 * t + ri) * NCH:(2 * t + ri + 1) * NCH],
                                G1T[:, 4 * f + t, ri, half * N:(half + 1) * N], U[:, 2 * (4 * f + t) + half, :],
                                start=True, stop=True)
                last.then_inc(but, 1)
            pe.wait_ge(buc, 4)
            product(Item(KI), AH, AL, FT)
            product(Item(KV), AH, AL, FT)
            taken_out(Item(KI))
            for t in range(TT):
                last = nc.tensor.transpose(PS[:, M0, t * P:(t + 1) * P], kiw[:, t * P:(t + 1) * P], ident[:, :])
            last.then_inc(ki_t, 1)
            product(Item(QI), AH, AL, FT)
            taken_out(Item(KV))
            pe.wait_ge(wtok_ok, 1)
            for t in range(TT):
                last = nc.tensor.transpose(PS[:, M0, t * P:(t + 1) * P], kv[:, t * P:(t + 1) * P], ident[:, :])
            last.then_inc(v_t, 1)
            pe.wait_ge(ki_dup, 16)
            for j in range(4):
                if j:
                    product(Item(QI + j), AH, AL, FT)
                taken_out(Item(QI + j))
                for h in range(2):
                    if 2 * j + h:
                        pe.wait_ge(idx_r, 2 * j + h)
                    for q, _, b, c in SEGS:
                        if q:
                            last = nc.tensor.matmul(PS[:, b, c:c + (q + 1) * P],
                                                    qi_s[h * DH:(h + 1) * DH, q * P:(q + 1) * P],
                                                    kiw[h * DH:(h + 1) * DH, 0:(q + 1) * P], start=True, stop=True)
                    last.then_inc(idx_s, 1)
            pe.wait_ge(scanned, 1)
            pe.wait_ge(dt_in, 128)
            pe.wait_ge(idx_r, H1)
            for f in range(4):
                for half4 in range(2):
                    if f:
                        pe.wait_ge(yc, 2 * f + half4 - 1)
                    for k in range(4):
                        t, half = 4 * f + k, half4 * N
                        g = 2 * t + half4
                        o = PS[0:NCH, Z0 + half4, k * P:(k + 1) * P]
                        for ri in range(2):
                            nc.tensor.matmul(o, Hs[half:half + N, 0:NCH, ri, t],
                                             E[half:half + N, ri, t, 1:L + 1, :].rearrange("p a b -> p (a b)"),
                                             start=(ri == 0), stop=False)
                        last = nc.tensor.matmul(o, U[:, g, :], Dt[:, g, :, :].rearrange("p a b -> p (a b)"),
                                                start=False, stop=True)
                    last.then_inc(yt, 1)
                pe.wait_ge(yc, 2 * f + 2)
                if f:
                    pe.wait_ge(y_v, f)
                for s in range(L):
                    last = nc.tensor.transpose(PS[:, T0, s * NCH:(s + 1) * NCH], Y[:, s, :], ident[0:NCH, 0:NCH])
                last.then_inc(y2t, 1)
            for n in range(ZA, Q1):
                product(Item(n), AH, AL, FT)
            product(Item(Q1), AH, AL, FT)
            pe.wait_ge(k_dup, 16)
            for j in range(4):
                taken_out(Item(Q1 + j))
                for h in range(2):
                    hd = Item(2 * j + h)
                    if hd.fixed:
                        pe.wait_ge(z_read, hd.fixed)
                    attend_scores(hd, q_s[:, j % 2, :], kv, h)
                    if h == 0 and j < 3:
                        product(Item(Q1 + j + 1), AH, AL, FT)
                    pe.wait_ge(feats_c, j)
                    attend_values(hd, h, lg, pT, lambda kb: vtok[:, kb, :])
                pair_features(Item(2 * j + 1), o_s)
            pe.wait_ge(ya_ok, 4)
            for n in range(GLU, GATE):
                product(Item(n), BH, BL, 4)
            with pe.Fori(0, FT // 2) as i:
                for jj in range(2):
                    n = Item(GATE + 4 * jj, i, 8)
                    product(n, AH, AL, FT)
                    product(n + 1, AH, AL, FT)
                    pe.wait_ge(ya2_l, 1)
                    product(n + 2, BH, BL, 4)
                    pe.wait_ge(yb_l, 4)
                    product(n + 3, BH, BL, 4, k0=4)
            pe.wait_ge(silc_ok, 2)
            pe.wait_ge(feats_c, 4)
            for j in range(FT + 1):
                if j < FT:
                    for k in range(3):
                        modulation(NMOD + 3 * j + k)
                    if j == 0:
                        pe.wait_ge(mg_l, FT)
                    product(Item(WO + j), AH, AL, FT)
                if j:
                    out_transposes(j - 1)

            pe.wait_ge(mod2_read, 1)
            normed_features(1)
            pe.wait_ge(hl, 2 * FT)
            with pe.Fori(0, FT // 2) as i:
                for jj in range(2):
                    n = Item(L2 + 6 * jj, i, 12)
                    pair = Item(jj, i, 2)
                    for k in range(3):
                        product(n + k, AH, AL, FT)
                    taken_out(n)
                    taken_out(n + 1)
                    for h in range(2):
                        hd = Item(H1 + 2 * jj + h, i, 4)
                        pe.wait_ge(z_gates, hd.value(-H1))
                        attend_scores(hd, q2, k2, h)
                        if h == 0:
                            taken_out(n + 2)
                            pe.wait_ge(feats_c, pair.value(4))
                            for t in range(TT):
                                last = nc.tensor.transpose(PS[:, M0, t * P:(t + 1) * P], v2[:, t * P:(t + 1) * P],
                                                           ident[:, :])
                            last.then_inc(v2_t, 1)
                            product(n + 3, AH, AL, FT)
                            pe.wait_ge(v2_c, pair.value(1))
                        else:
                            product(n + 4, AH, AL, FT)
                        attend_values(hd, h, beta, wT, lambda kb: v2tok[:, kb, h * DH:(h + 1) * DH])
                    pair_features(Item(H1 + 2 * jj + 1, i, 4), o2)
                    product(n + 5, AH, AL, FT)
            pe.wait_ge(y2b_ok, FT)
            with pe.Fori(0, FT // 2) as i:
                for jj in range(2):
                    n = Item(MA + 2 * jj, i, 4)
                    product(n, AH, AL, FT)
                    product(n + 1, BH, BL, FT)
            pe.wait_ge(d_l, FT)
            for n in range(POOLW, MB):
                product(Item(n), BH, BL, 2, k0=2 * ((n - POOLW) // 2))
            with pe.Fori(0, FT // 2) as i:
                for jj in range(2):
                    n = Item(MB + 2 * jj, i, 4)
                    product(n, AH, AL, FT)
                    pe.wait_ge(pw_l, FT)
                    product(n + 1, BH, BL, FT)
            pe.wait_ge(mg_l, 2 * FT)
            for j in range(FT + 1):
                if j < FT:
                    product(Item(WO2 + j), AH, AL, FT)
                if j:
                    out_transposes(FT + j - 1)

        @block.scalar
        def _(act):
            def high(n, kt):
                s, r = n.slot(2), n + NMOD
                act.wait_ge(raw_in[r.slot(4)], r.turns(4, 16, 16))
                if n.trip is not None or n.fixed >= 2:
                    act.wait_ge(tile_done, n.value(-1))
                nc.scalar.activation(WH[:, s, 0:kt * P], raw[:, r.slot(4), 0:kt * P], ACT.Copy).then_inc(h_ready, 1)

            def kt_of(n):
                return weight_source(n)[1]

            def squares(s):
                for t in range(TT):
                    if s or t:
                        act.wait_ge(sumsq, 4 * s + t)
                    if s in (1, 3):
                        act.wait_ge(wo_add, FT * (s // 2 + 1))
                    if s == 2:
                        act.wait_ge(x1_ok, t + 1)
                    nc.scalar.activation(junk, x_tok[:, t, :], ACT.Square,
                                         accum_out=stat[:, 0, t:t + 1]).then_inc(sumsq, 1)
                act.wait_ge(ms_ok, s + 1)
                nc.scalar.activation(stat[:, 2, :], stat[:, 1, :], ACT.Sqrt).then_inc(root, 1)

            def features(layer):
                act.wait_ge(mod_ok, layer + 1)
                m = (mod1, mod2)[layer]
                for f in range(FT):
                    n = FT * layer + f
                    act.wait_ge(ht, n + 1)
                    if f >= 2:
                        act.wait_ge(hl, n - 1)
                    nc.scalar.activation(tmpf[:, f % 2, :], bank(Z0 + f % 2), ACT.Identity, bias=m[:, f:f + 1],
                                         scale=gs[:, layer, f:f + 1]).then_inc(hv, 1)
                    act.wait_ge(hv, n + 1)
                    nc.scalar.activation(AH[:, f, :], tmpf[:, f % 2, :], ACT.Copy).then_inc(hh, 1)

            def copy_out(n, dst):
                act.wait_ge(tile_done, n.value(1))
                nc.scalar.activation(dst, bank(n.slot(2)), ACT.Copy).then_inc(p_free[n.slot(2)], 1)

            def copy_gate(n):
                act.wait_ge(tile_done, n.value(1))
                nc.scalar.activation(gates2, bank(0), ACT.Sigmoid).then_inc(p_free[0], 1)

            def t_copies(hd, wt):
                act.wait_ge(o_ready, hd.value())
                for g, (lo, hi) in enumerate(T_GROUPS):
                    tg = Item(3 * hd.fixed + g, hd.trip, 3 * hd.per)
                    act.wait_ge(t_ready, tg.value(1))
                    nc.scalar.activation(wt[:, lo:hi, :].rearrange("p a b -> p (a b)"),
                                         PS[:, T0 + tg.slot(2), 0:(hi - lo) * P], ACT.Copy).then_inc(t_copied, 1)

            act.wait_ge(cols_ok, 1)
            for k, v in enumerate((V_C1, V_C2)):
                nc.scalar.activation(silc[:, k, :], vcol[:, v:v + FT], ACT.Sigmoid).then_inc(sig_c, 1)
            act.wait_ge(x_in, 16)
            squares(0)
            act.wait_ge(sin_in, 1)
            for k in range(2):
                nc.scalar.activation(pp[:, 12 + k, :], pp[:, 10 + k, :], ACT.Sin).then_inc(sin_ok, 1)
            for r in range(8):
                act.wait_ge(gb_t, r + 1)
                nc.scalar.activation(G1T[:, 2 * r:2 * r + 2, :, :].rearrange("p a b c -> p (a b c)"), bank(T0 + r % 2),
                                     ACT.Copy).then_inc(gb_c, 1)
            for r in range(8):
                act.wait_ge(k_t, r + 1)
                nc.scalar.activation(Kraw[:, 8 * (r // 2) + r % 2:8 * (r // 2) + 8:2, :],
                                     PS[0:GP, Z0 + r % 2, :].rearrange("p (a b) -> p a b", b=P), ACT.Copy).then_inc(k_c, 1)
            act.wait_ge(k_c, 8)
            act.wait_ge(dt_zero, 1)
            for j in range(L):
                d = L - 1 - j
                act.dma_start(Dt[d * GP:(d + 1) * GP, :, j:L, :].rearrange("p a b c -> p a (b c)"),
                              Kraw[:, :, 0:(L - j) * GP]).then_inc(dt_in, 16)
            high(Item(0), FT)
            high(Item(1), FT)
            features(0)
            for n in range(XA, KI):
                copy_out(Item(n), xaT[:, n, :])
                high(Item(n + 2), FT)
            act.wait_ge(dt_in, 16 * L)
            for f in range(4):
                act.wait_ge(xt, f + 1)
                if f:
                    act.wait_ge(ut, f)
                for k in range(2):
                    nc.scalar.activation(X[:, :, 4 * k:4 * k + 4, :],
                                         PS[0:NCH, T1 + k, :].rearrange("p (s g c) -> p g s c", s=4, g=L), ACT.Copy).then_inc(xc, 1)
                act.wait_ge(ut, f + 1)
                nc.scalar.activation(U[:, L * f:L * f + L, :].rearrange("p a b -> p (a b)"), bank(T1),
                                     ACT.Copy).then_inc(uc, 1)
                act.wait_ge(but, f + 1)
                nc.scalar.activation(BU[:, 4 * f:4 * f + 4, :, :].rearrange("p a b c -> p (a b c)"), bank(M0),
                                     ACT.Copy).then_inc(buc, 1)
            copy_out(Item(KI), kiw)
            high(Item(KI + 2), FT)
            act.wait_ge(ki_t, 1)
            nc.scalar.activation(wtok[:, :, :], bank(M0).rearrange("p (t f) -> p t f", f=P)[:, :, DH:DH + H1],
                                 ACT.Copy).then_inc(wtok_ok, 1)
            act.dma_start(kiw[DH:P, :], kiw[0:DH, :]).then_inc(ki_dup, 16)
            copy_out(Item(KV), kv)
            high(Item(KV + 2), FT)
            act.wait_ge(v_t, 1)
            nc.scalar.activation(vtok[:, :, :], bank(M0).rearrange("p (t f) -> p t f", f=P)[:, :, DH:P],
                                 ACT.Copy).then_inc(vtok_ok, 1)
            act.dma_start(kv[DH:P, :], kv[0:DH, :]).then_inc(k_dup, 16)
            for j in range(4):
                if j:
                    act.wait_ge(idx_s, 2 * j)
                copy_out(Item(QI + j), qi_s)
                high(Item(QI + j + 2), FT)
                for h in range(2 * j, 2 * j + 2):
                    act.wait_ge(idx_s, h + 1)
                    if h:
                        act.wait_ge(idx_w, h)
                    for q, c0, b, c in SEGS:
                        if q:
                            last = nc.scalar.activation(rl[:, c0:c0 + (q + 1) * P], PS[:, b, c:c + (q + 1) * P],
                                                        ACT.Relu, scale=IDX_SCALE)
                    last.then_inc(idx_r, 1)
            for f in range(4):
                for half4 in range(2):
                    act.wait_ge(yt, 2 * f + half4 + 1)
                    if f and half4 == 0:
                        act.wait_ge(y2t, f)
                    nc.scalar.activation(
                        Y.rearrange("p i (k h c) -> p i k h c", h=2, c=GP)[:, :, :, half4, :],
                        PS[0:NCH, Z0 + half4, :].rearrange("p (g i c) -> p i g c", g=4, i=L), ACT.Copy).then_inc(yc, 1)
                act.wait_ge(y_v, f + 1)
                nc.scalar.activation(tmpf[:, f % 2, :], tmpf[:, f % 2, :], ACT.Gelu_apprx_tanh).then_inc(gelu_ok, 1)
                act.wait_ge(gelu_ok, f + 1)
                nc.scalar.activation(BH[:, f, :], tmpf[:, f % 2, :], ACT.Copy).then_inc(yh, 1)
            for n in range(ZA, Q1):
                act.wait_ge(tile_done, n + 1)
                if n >= ZA + 2:
                    act.wait_ge(p_free[n % 2], n // 2)
                act.wait_ge(ya_ok, 4)
                nc.scalar.activation(tmpf[:, n % 2, :], bank(n % 2), ACT.Sigmoid).then_inc(gate_sig, 1)
                high(Item(n + 2), FT)
            copy_out(Item(Q1), q_s[:, 0, :])
            high(Item(Q1 + 2), FT)
            for j in range(4):
                for h in range(2):
                    hd = Item(2 * j + h)
                    act.wait_ge(nmax_ok, hd.value(1))
                    for q, c0, _, _ in SEGS:
                        seg = lg[:, c0:c0 + (q + 1) * P]
                        last = nc.scalar.activation(seg, seg, ACT.Exp, bias=hs[:, 1, q:q + 1], scale=DH ** -0.5,
                                                    accum_out=hs[:, 2, q:q + 1])
                    last.then_inc(probs_ok, 1)
                    if h == 0 and j < 3:
                        copy_out(Item(Q1 + j + 1), q_s[:, (j + 1) % 2, :])
                        high(Item(Q1 + j + 3), kt_of(Q1 + j + 3))
                    t_copies(hd, pT)
            for j in range(4):
                n = GLU + 2 * j
                act.wait_ge(tile_done, n + 2)
                if j == 0:
                    act.wait_ge(o_copied, H1)
                else:
                    act.wait_ge(p_free[0], n // 2)
                nc.scalar.activation(gates[:, 1, :], bank(1), ACT.Sigmoid,
                                     bias=vcol[:, V_BG + 4 + j:V_BG + 5 + j]).then_inc(p_free[1], 1)
                high(Item(n + 2), 4 if n + 2 < GATE else 8)
                high(Item(n + 3), 4 if n + 3 < GATE else 8)
            act.wait_ge(ya2_ok, 4)
            nc.scalar.activation(BH[:, 0:4, :].rearrange("p a b -> p (a b)"), ya2.rearrange("p a b -> p (a b)"),
                                 ACT.Copy).then_inc(ya2_h, 1)
            with act.Fori(0, FT // 2) as i:
                for jj in range(2):
                    n = Item(GATE + 4 * jj, i, 8)
                    for k in range(4):
                        high(n + k + 2, (4, 4, 8, 8)[k])
                        if k < 2:
                            act.wait_ge(p_free[k], (n + k).turns(2))
                            act.wait_ge(tile_done, (n + k).value(1))
                            nc.scalar.activation(gates[:, k, :], bank(k), ACT.Sigmoid).then_inc(p_free[k], 1)
            act.wait_ge(mg_ok, FT)
            for f in range(FT):
                nc.scalar.activation(AH[:, f, :], merged1[:, f, :], ACT.Copy).then_inc(mg_h, 1)
            act.dma_start(gain, final_g.rearrange("(o n) -> o n", o=1).broadcast_to([P, D])).then_inc(gain_in, 16)

            def out_tile(n, j, m):
                act.wait_ge(tile_done, n + 1)
                if j % FT >= 2:
                    act.wait_ge(wo_t, j - 1)
                nc.scalar.activation(tmpf[:, j % 2, :], bank(n % 2), ACT.Identity,
                                     scale=m[:, 16 + j % FT:17 + j % FT]).then_inc(p_free[n % 2], 1)

            act.wait_ge(mg_l, FT)
            for j in range(FT):
                high(Item(WO + j + 2), FT)
                out_tile(WO + j, j, mod1)
            squares(1)
            squares(2)
            features(1)
            with act.Fori(0, FT // 2) as i:
                for jj in range(2):
                    n, pair = Item(L2 + 6 * jj, i, 12), Item(jj, i, 2)

                    def gates_of(h):
                        hd = Item(H1 + 2 * jj + h, i, 4)
                        act.wait_ge(head2_m, hd.value(1 - H1))
                        act.wait_ge(t_ready, Item(3 * hd.fixed, i, 12).value())
                        act.wait_ge(probs_ok, hd.value())
                        for dst, scale in ((beta, DH ** -0.5), (om, -DH ** -0.5)):
                            for col, b, width in ((0, Z0, 512), (512, Z1, 512), (1024, Z2, 256)):
                                last = nc.scalar.activation(dst[:, col:col + width], PS[:, b, 0:width], ACT.Sigmoid,
                                                            scale=scale)
                        last.then_inc(z_gates, 1)

                    high(n + 2, FT)
                    act.wait_ge(z_ready, Item(H1 + 2 * jj, i, 4).value())
                    copy_out(n, q2)
                    high(n + 3, FT)
                    copy_out(n + 1, k2)
                    high(n + 4, FT)
                    copy_out(n + 2, v2)
                    gates_of(0)
                    act.wait_ge(v2_t, pair.value(1))
                    act.wait_ge(o_ready, Item(H1 + 2 * jj, i, 4).value())
                    nc.scalar.activation(v2tok.rearrange("p a b -> p (a b)"), bank(M0), ACT.Copy).then_inc(v2_c, 1)
                    high(n + 5, FT)
                    act.wait_ge(tile_done, (n + 3).value(1))
                    nc.scalar.activation(sza2, bank(1), ACT.Sigmoid).then_inc(gate2_sig, 1)
                    t_copies(Item(H1 + 2 * jj, i, 4), wT)
                    gates_of(1)
                    high(n + 6, FT)
                    t_copies(Item(H1 + 2 * jj + 1, i, 4), wT)
                    high(n + 7, FT)
                    act.wait_ge(tile_done, (n + 5).value(1))
                    act.wait_ge(y2b_ok, pair.value(1))
                    nc.scalar.activation(tmpf[:, 0, :], bank(1), ACT.Sigmoid).then_inc(gate2_sig, 1)
            with act.Fori(0, FT // 2) as i:
                for jj in range(2):
                    n = Item(MA + 2 * jj, i, 4)
                    high(n + 2, FT)
                    act.wait_ge(p_free[1], n.turns(2))
                    copy_gate(n)
                    high(n + 3, FT)
            act.wait_ge(d_ok, FT)
            for f in range(FT):
                nc.scalar.activation(BH[:, f, :], uT[:, f, :], ACT.Copy).then_inc(d_h, 1)
            for g in range(4):
                n = POOLW + 2 * g
                high(Item(n + 2), kt_of(n + 2) if n + 2 < MB else FT)
                act.wait_ge(tile_done, n + 2)
                for k in range(2):
                    act.wait_ge(pw_l, 2 * g)
                    nc.scalar.activation(wide[:, k, :], bank(k), ACT.Identity,
                                         scale=vcol[:, V_PS + 2 * g + k:V_PS + 2 * g + k + 1]).then_inc(p_free[k], 1)
                high(Item(n + 3), kt_of(n + 3) if n + 3 < MB else FT)
                for k in range(2):
                    act.wait_ge(pw_v, 2 * g + k + 1)
                    nc.scalar.activation(BH[:, 2 * g + k, :], wide[:, k, :], ACT.Copy).then_inc(pw_h, 1)
            with act.Fori(0, FT // 2) as i:
                for jj in range(2):
                    n = Item(MB + 2 * jj, i, 4)
                    high(n + 2, FT)
                    act.wait_ge(p_free[1], n.turns(2))
                    copy_gate(n)
                    high(n + 3, FT)
            act.wait_ge(mg2_ok, FT)
            for f in range(FT):
                nc.scalar.activation(AH[:, f, :], merged2[:, f, :], ACT.Copy).then_inc(mg_h, 1)
            act.dma_start(gain, final_gain_2.rearrange("(o n) -> o n", o=1).broadcast_to([P, D])).then_inc(gain_in, 16)
            for j in range(FT):
                if WO2 + j + 2 < END:
                    high(Item(WO2 + j + 2), FT)
                out_tile(WO2 + j, FT + j, mod2)
            squares(3)

        @block.vector
        def _(dve):
            steps = Steps(dve, dve_s)
            link, do = steps.link, steps.do
            tt, ts, stt = nc.vector.tensor_tensor, nc.vector.tensor_scalar, nc.vector.scalar_tensor_tensor

            def col(k):
                return pp[:, k, :]

            nc.vector.memset(vrow[:, :, :], 0.0).then_inc(rows_zero, 1)
            nc.vector.memset(hs[:, 0, :], 0.0).then_inc(rows_zero, 1)
            link(nc.vector.memset(sc[:, :, :, :], 0.0))
            dve.wait_ge(rows_in, 16 * 12)
            ts(vrow[32:48, 1, :].rearrange("p (g n) -> p g n", g=2), hs[32:48, 0, 0:2].unsqueeze(2).broadcast_to([ST, 2, N]),
               1.0, None, ALU.mult).then_inc(ld_rows, 1)
            dve.wait_ge(cols_t, 1)
            do(nc.vector.tensor_copy(vcol2[:, :], PS[:, M0, P:2 * P]))
            nc.vector.tensor_copy(vcol[:, :], PS[:, M0, 0:P]).then_inc(cols_ok, 1)
            dve.wait_ge(cols_ok, 1)
            steps.settle()
            dve.wait_ge(sig_c, 2)
            for k, v in enumerate((V_C1, V_C2)):
                tt(silc[:, k, :], silc[:, k, :], vcol[:, v:v + FT], ALU.mult).then_inc(silc_ok, 1)

            def scales(s, gains):
                dve.wait_ge(sumsq, 4 * s + 4)
                ts(stat[:, 1, :], stat[:, 0, :], 1.0 / D, EPS, ALU.mult, ALU.add).then_inc(ms_ok, 1)
                dve.wait_ge(root, s + 1)
                link(nc.vector.reciprocal(stat[:, 3, :], stat[:, 2, :]))
                if not gains:
                    for t in range(TT):
                        last = ts(diag[:, t, :], ident[:, :], stat[:, 3, t:t + 1], None, ALU.mult)
                        if t < TT - 1:
                            do(last)
                    last.then_inc(diag_ok, 1)
                else:
                    dve.wait_ge(gain_in, 16 * gains)
                    for t in range(TT):
                        stt(x_tok[:, t, :], x_tok[:, t, :], stat[:, 3, t:t + 1], gain, ALU.mult, ALU.mult)\
                            .then_inc(x1_ok, 1)

            def exponential(out_, in_):
                x_, k_, r_, p_, k1 = (col(n) for n in range(16, 21))
                link(ts(x_, in_, -174.0, 88.0, ALU.max, ALU.min))
                link(ts(k_, x_, 1.0 / math.log(2.0), 12582912.0, ALU.mult, ALU.add))
                link(ts(k_, k_, 12582912.0, None, ALU.subtract))
                link(stt(r_, k_, -0.693359375, x_, ALU.mult, ALU.add))
                link(stt(r_, k_, 2.12194440e-4, r_, ALU.mult, ALU.add))
                link(ts(p_, r_, 1.0 / math.factorial(8), None, ALU.mult))
                for n in range(7, 0, -1):
                    link(stt(p_, p_, 1.0 / math.factorial(n), r_, ALU.add, ALU.mult))
                link(ts(p_, p_, 1.0, None, ALU.add))
                link(ts(k1, k_, -126.0, None, ALU.max))
                link(tt(k_, k_, k1, ALU.subtract))
                for n, k in enumerate((k1, k_)):
                    link(ts(ppi[:, n, :], k, 127.0, None, ALU.add))
                    link(ts(ppi[:, n, :], ppi[:, n, :], 23, None, ALU.logical_shift_left))
                    link(tt(p_, p_, ppi[:, n, :].bitcast(fp32), ALU.mult))
                link(ts(out_, p_, 1.0, None, ALU.mult))

            ar, ai, ld = vcol[:, V_AR:V_AR + ST], vcol2[:, 0:ST], vcol2[:, 32:32 + ST]
            scales(0, 0)
            exponential(col(0), ld)
            link(tt(col(1), ar, col(0), ALU.mult))
            exponential(col(2), col(1))
            link(tt(col(3), ai, col(0), ALU.mult))
            C1 = 6.28125
            C2 = round((2 * math.pi - C1) * 2 ** 20) / 2 ** 20
            C3 = 2 * math.pi - C1 - C2
            link(ts(col(4), col(3), 1.0 / (2 * math.pi), 12582912.0, ALU.mult, ALU.add))
            link(ts(col(4), col(4), 12582912.0, None, ALU.subtract))
            for cc in (C1, C2, C3):
                link(stt(col(3), col(4), -cc, col(3), ALU.mult, ALU.add))
            link(ts(col(10), col(3), 3.1415925, -3.1415925, ALU.min, ALU.max))
            ts(col(11), col(10), 0.5, None, ALU.mult).then_inc(sin_in, 1)
            dve.wait_ge(sin_ok, 2)
            link(tt(col(7), col(13), col(13), ALU.mult))
            link(ts(col(7), col(7), -2.0, 1.0, ALU.mult, ALU.add))
            link(tt(col(5), col(2), col(7), ALU.mult))
            link(tt(col(6), col(2), col(12), ALU.mult))
            link(tt(col(16), ar, ar, ALU.mult))
            link(tt(col(17), ai, ai, ALU.mult))
            link(tt(col(16), col(16), col(17), ALU.add))
            link(nc.vector.reciprocal(col(16), col(16)))
            link(ts(col(17), col(5), 1.0, None, ALU.subtract))
            link(tt(col(18), col(17), ar, ALU.mult))
            link(tt(col(19), col(6), ai, ALU.mult))
            link(tt(col(18), col(18), col(19), ALU.add))
            link(tt(col(8), col(18), col(16), ALU.mult))
            link(tt(col(18), col(6), ar, ALU.mult))
            link(tt(col(19), col(17), ai, ALU.mult))
            link(tt(col(18), col(18), col(19), ALU.subtract))
            link(tt(col(9), col(18), col(16), ALU.mult))
            link(ts(col(13), col(6), -1.0, None, ALU.mult))
            link(ts(col(14), col(6), 1.0, None, ALU.mult))
            link(ts(col(15), col(6), -1.0, None, ALU.mult))
            link(ts(col(20), col(9), -1.0, None, ALU.mult))
            link(ts(col(21), col(9), 1.0, None, ALU.mult))

            prod = [tmpf[:, k, :].rearrange("p (a b c) -> p a b c", a=2, b=ST) for k in range(2)]

            def wide_of(v, twice):
                v = v.unsqueeze(1) if twice else v
                return v.unsqueeze(3).broadcast_to([P, 2, ST, GP])

            def complex_times(out_, in_, swapped, re, im):
                link(tt(prod[0], in_, wide_of(re, True), ALU.mult))
                link(tt(prod[1], swapped, wide_of(im, False), ALU.mult))
                link(tt(out_, prod[0], prod[1], ALU.add))

            dve.wait_ge(b_in, 64)
            complex_times(GB[:, :, :, 0, :], Bin, Bin[:, ::-1, :, :], col(8), pp[:, 20:22, :])
            for d in range(1, L):
                before = GB[:, :, :, d - 1, :]
                complex_times(GB[:, :, :, d, :], before, before[:, ::-1, :, :], col(5), pp[:, 13:15, :])
            nc.vector.memset(pp[:, 22, :], 0.0).then_inc(gb_ok, 1)
            dve.wait_ge(c_t, 1)
            for part in range(2):
                for half in range(2):
                    v = PS[half * N:(half + 1) * N, Z0 + part, :].rearrange("p (t g c) -> p t g c", g=2, c=GP)
                    link(ts(E[half * N:(half + 1) * N, part, :, 0, :], v[:, :, half, :], 1.0 - 2.0 * part, None, ALU.mult))
            nc.vector.memset(Dt[:, :, :, :], 0.0).then_inc(dt_zero, 1)
            for k in range(L):
                before = E[:, :, :, k, :]
                complex_times(E[:, :, :, k + 1, :], before, before[:, ::-1, :, :], col(5), pp[:, 14:16, :])
            nc.vector.memset(pp[:, 22, :], 0.0).then_inc(e_ok, 1)
            for _ in range(3):
                link(tt(col(16), col(5), col(5), ALU.mult))
                link(tt(col(17), col(6), col(6), ALU.mult))
                link(tt(col(18), col(5), col(6), ALU.mult))
                link(tt(col(5), col(16), col(17), ALU.subtract))
                link(ts(col(6), col(18), 2.0, None, ALU.mult))
            link(ts(col(14), col(6), 1.0, None, ALU.mult))
            link(ts(col(15), col(6), -1.0, None, ALU.mult))

            def modulations(layer):
                m, base, g = ((mod1, V_BM1, V_G1), (mod2, V_BM2, V_G2))[layer]
                dve.wait_ge(mod_done, NMOD * (layer + 1))
                if layer:
                    tt(m[:, :], PS[:, M0, 256:256 + NMOD], vcol[:, base:base + NMOD], ALU.add).then_inc(mod2_read, 1)
                    dve.wait_ge(mod2_read, 1)
                else:
                    link(tt(m[:, :], PS[:, M0, 256:256 + NMOD], vcol[:, base:base + NMOD], ALU.add))
                stt(gs[:, layer, :], m[:, FT:2 * FT], 1.0, vcol[:, g:g + FT], ALU.add, ALU.mult).then_inc(mod_ok, 1)

            def low_features(layer):
                for f in range(FT):
                    dve.wait_ge(hh, FT * layer + f + 1)
                    tt(AL[:, f, :], tmpf[:, f % 2, :], AH[:, f, :].bitcast(fp32), ALU.subtract).then_inc(hl, 1)

            modulations(0)
            low_features(0)
            dve.wait_ge(buc, 4)
            link(nc.vector.memset(score, 0.0))
            for q, c0, _, _ in SEGS:
                do(nc.vector.tensor_copy(score[:, c0 + q * P:c0 + (q + 1) * P], tri1[:, :]))
            steps.settle()
            link(nc.vector.memset(Hs[:, 0, :, :], 0.0))

            def scan(first, last_):
                steps.begin_loop()
                with dve.Fori(first, last_) as ch:
                    steps.base, steps.k, steps.per = steps.start + (ch - first) * 4, 0, 4
                    now = Hs[:, bass.ds(ch, 1), :, :].rearrange("p a r t -> p (a r) t")
                    link(tt(sc[:, 0, :, :], now, col(5).unsqueeze(1).broadcast_to([P, 2, ST]), ALU.mult))
                    link(tt(sc[:, 1, ::-1, :], now, pp[:, 14:16, :], ALU.mult))
                    link(tt(sc[:, 0, :, :], sc[:, 0, :, :], sc[:, 1, :, :], ALU.add))
                    link(tt(Hs[:, bass.ds(ch + 1, 1), :, :].rearrange("p a r t -> p (a r) t"), sc[:, 0, :, :],
                            BU[:, :, :, bass.ds(ch, 1)].rearrange("p t r a -> p (r a) t"), ALU.add))
                steps.end_loop(last_ - first)

            per_head = NCH // H1
            for h in range(H1):
                scan(h * per_head, (h + 1) * per_head)
                dve.wait_ge(wtok_ok, 1)
                dve.wait_ge(idx_r, h + 1)
                for q, c0, _, _ in SEGS:
                    if q:
                        seg = slice(c0, c0 + (q + 1) * P)
                        last = stt(score[:, seg], rl[:, seg], wtok[:, q, h:h + 1], score[:, seg], ALU.mult, ALU.add)
                        if q > 1:
                            do(last)
                last.then_inc(idx_w, 1)
            nc.vector.memset(pp[:, 22, :], 0.0).then_inc(scanned, 1)
            dve.wait_ge(idx_w, H1)
            for f in range(4):
                dve.wait_ge(y2t, f + 1)
                if f >= 2:
                    dve.wait_ge(yh, f - 1)
                    dve.wait_ge(ya_ok, f - 1)
                stt(tmpf[:, f % 2, :].rearrange("p (c i) -> p c i", i=L), xaT[:, f, :].rearrange("p (c i) -> p c i", i=L),
                    vcol[:, V_DS + f:V_DS + f + 1], bank(T0).rearrange("p (i c) -> p c i", i=L), ALU.mult, ALU.add)\
                    .then_inc(y_v, 1)
                dve.wait_ge(yh, f + 1)
                tt(BL[:, f, :], tmpf[:, f % 2, :], BH[:, f, :].bitcast(fp32), ALU.subtract).then_inc(ya_ok, 1)

            rounds = [(r, q, c0) for r in range(TOPK // 8) for q, c0, _, _ in SEGS if q]

            def take(r, q, c0):
                seg = slice(c0, c0 + (q + 1) * P)
                src = score[:, seg] if r == 0 else work[:, seg]
                link(nc.vector.max(m8[:, q - 1, :], src))
                link(nc.vector.match_replace(work[:, seg], m8[:, q - 1, :], src, TAKEN))

            for n in range(ZA, Q1):
                for k in range(6):
                    take(*rounds[6 * (n - ZA) + k])
                dve.wait_ge(gate_sig, n - ZA + 1)
                dst = sza[:, n - ZA, :] if n < ZB else szb[:, n - ZB, :]
                tt(dst, bank(n % 2), tmpf[:, n % 2, :], ALU.mult).then_inc(p_free[n % 2], 1)
            for q, c0, _, _ in SEGS:
                if q:
                    seg = slice(c0, c0 + (q + 1) * P)
                    last = ts(score[:, seg], work[:, seg], TAKEN / 2, NEG, ALU.is_gt, ALU.mult)
                    do(last)
            steps.settle()
            amask = score

            for j in range(4):
                for h in range(2):
                    hd = 2 * j + h
                    dve.wait_ge(z_ready, hd + 1)
                    for q, c0, b, cb in SEGS:
                        w = (q + 1) * P
                        last = nc.vector.tensor_tensor_reduce(lg[:, c0:c0 + w], PS[:, b, cb:cb + w], amask[:, c0:c0 + w],
                                                              1.0, -3e38, ALU.add, ALU.max, hs[:, 0, q:q + 1])
                        if q != 1:
                            do(last)
                    last.then_inc(z_read, 1)
                    dve.wait_ge(z_read, hd + 1)
                    steps.settle()
                    ts(hs[:, 1, :], hs[:, 0, :], -DH ** -0.5, None, ALU.mult).then_inc(nmax_ok, 1)
                    dve.wait_ge(probs_ok, hd + 1)
                    link(nc.vector.reciprocal(hs[:, 3, :], hs[:, 2, :]))
                    if hd >= 2 and h == 0:
                        dve.wait_ge(feats_t, j)
                    dve.wait_ge(o_ready, hd + 1)
                    for q in range(TT):
                        last = ts(o_s[:, q, h * DH:(h + 1) * DH], PS[:, M0, q * DH:(q + 1) * DH],
                                  hs[:, 3, q:q + 1], None, ALU.mult)
                        if q < TT - 1:
                            do(last)
                    last.then_inc(o_copied, 1)
                dve.wait_ge(feats_t, j + 1)
                tt(tmpf[:, 0, :], bank(M0), szb[:, j, :], ALU.mult).then_inc(feats_c, 1)
                dve.wait_ge(feats_c, j + 1)
                link(ts(BH[:, 4 + j, :], tmpf[:, 0, :], 1.0, None, ALU.mult))
                tt(BL[:, 4 + j, :], tmpf[:, 0, :], BH[:, 4 + j, :].bitcast(fp32), ALU.subtract).then_inc(yb_l, 1)
            for j in range(4):
                dve.wait_ge(tile_done, GLU + 2 * j + 2)
                dve.wait_ge(p_free[1], (GLU + 2 * j + 1) // 2 + 1)
                if j:
                    dve.wait_ge(ya2_ok, j)
                stt(parts_ab[:, 0, :], bank(0), vcol[:, V_BG + j:V_BG + j + 1], gates[:, 1, :], ALU.add, ALU.mult)\
                    .then_inc(p_free[0], 1)
                dve.wait_ge(p_free[0], (GLU + 2 * j) // 2 + 1)
                tt(ya2[:, j, :], parts_ab[:, 0, :], sza[:, j, :], ALU.mult).then_inc(ya2_ok, 1)
            dve.wait_ge(ya2_h, 1)
            tt(BL[:, 0:4, :], ya2, BH[:, 0:4, :].bitcast(fp32), ALU.subtract).then_inc(ya2_l, 1)
            with dve.Fori(0, FT // 2) as i:
                for jj in range(2):
                    n = Item(GATE + 4 * jj, i, 8)
                    for k in range(2):
                        dve.wait_ge(p_free[k], (n + k).turns(2, add=1))
                        dve.wait_ge(tile_done, (n + 2 + k).value(1))
                        tt(parts_ab[:, k, :], bank(k), gates[:, k, :], ALU.mult).then_inc(p_free[k], 1)
                    for k in range(2):
                        dve.wait_ge(p_free[k], (n + 2 + k).turns(2, add=1))
                    tt(merged1[:, bass.ds(i * 2 + jj, 1), :].rearrange("p a b -> p (a b)"), parts_ab[:, 0, :],
                       parts_ab[:, 1, :], ALU.add).then_inc(mg_ok, 1)
                    dve.wait_ge(mg_ok, Item(jj, i, 2).value(1))

            def low_merged(layer, m):
                for f in range(FT):
                    dve.wait_ge(mg_h, FT * layer + f + 1)
                    tt(AL[:, f, :], m[:, f, :], AH[:, f, :].bitcast(fp32), ALU.subtract).then_inc(mg_l, 1)

            def add_outputs(layer):
                for j in range(FT):
                    dve.wait_ge(wo_t, FT * layer + j + 1)
                    v = x_tok[:, :, j * P:(j + 1) * P]
                    tt(v, v, bank(T0 + j % 2).rearrange("p (t c) -> p t c", t=TT), ALU.add).then_inc(wo_add, 1)

            low_merged(0, merged1)
            add_outputs(0)
            scales(1, 1)
            modulations(1)
            scales(2, 0)
            low_features(1)
            link(nc.vector.memset(zeros, 0.0))
            link(nc.vector.memset(Pw, 1.0))
            starts = {3: 0, 2: 513, 0: 898, 1: 1027}
            steps.begin_loop()
            with dve.Fori(0, FT // 2) as i:
                steps.begin_trip(i, 2 * (2 * 10 + 1))
                for jj in range(2):
                    n, pair = Item(L2 + 6 * jj, i, 12), Item(jj, i, 2)

                    def head(h):
                        hd = Item(H1 + 2 * jj + h, i, 4)
                        dve.wait_ge(z_ready, hd.value(1))
                        for q, _, b, cb in SEGS:
                            v = PS[:, b, cb + q * P:cb + (q + 1) * P]
                            last = tt(v, v, tri2[:, :], ALU.add)
                            if q != 1:
                                do(last)
                        last.then_inc(head2_m, 1)
                        dve.wait_ge(z_gates, hd.value(1 - H1))
                        dve.wait_ge(probs_ok, hd.value())
                        for q, c0, _, _ in SEGS:
                            w, s0 = (q + 1) * P, starts[q]
                            do(nc.vector.tensor_tensor_scan(Pw[:, s0:s0 + w][:, ::-1], om[:, c0:c0 + w][:, ::-1],
                                                            zeros[:, 0:w], 1.0, ALU.mult, ALU.add))
                        steps.settle()
                        for q, c0, _, _ in SEGS:
                            w, s0 = (q + 1) * P, starts[q]
                            last = tt(beta[:, c0:c0 + w], beta[:, c0:c0 + w], Pw[:, s0 + 1:s0 + 1 + w], ALU.mult)
                            if q != 1:
                                do(last)
                        last.then_inc(probs_ok, 1)

                    def outputs(h):
                        hd = Item(H1 + 2 * jj + h, i, 4)
                        if h == 0:
                            dve.wait_ge(feats_t, pair.value(4))
                        dve.wait_ge(o_ready, hd.value(1))
                        nc.vector.tensor_copy(o2[:, :, h * DH:(h + 1) * DH],
                                              PS[:, M0, 0:TT * DH].rearrange("p (t c) -> p t c", t=TT))\
                            .then_inc(o_copied, 1)

                    head(0)
                    dve.wait_ge(gate2_sig, Item(2 * jj, i, 4).value(1))
                    tt(sza2, bank(1), sza2, ALU.mult).then_inc(p_free[1], 1)
                    outputs(0)
                    head(1)
                    dve.wait_ge(tile_done, (n + 4).value(1))
                    ts(uT[:, bass.ds(i * 2 + jj, 1), :].rearrange("p a b -> p (a b)"), bank(0), 1.0, None, ALU.mult)\
                        .then_inc(p_free[0], 1)
                    outputs(1)
                    dve.wait_ge(feats_t, pair.value(5))
                    tt(tmpf[:, 1, :], bank(M0), sza2, ALU.mult).then_inc(feats_c, 1)
                    dve.wait_ge(feats_c, pair.value(5))
                    high = BH[:, bass.ds(i * 2 + jj, 1), :].rearrange("p a b -> p (a b)")
                    link(ts(high, tmpf[:, 1, :], 1.0, None, ALU.mult))
                    tt(BL[:, bass.ds(i * 2 + jj, 1), :].rearrange("p a b -> p (a b)"), tmpf[:, 1, :], high.bitcast(fp32),
                       ALU.subtract).then_inc(y2b_ok, 1)
                    dve.wait_ge(y2b_ok, pair.value(1))
                    dve.wait_ge(gate2_sig, Item(2 * jj, i, 4).value(2))
                    tt(szb2[:, bass.ds(i * 2 + jj, 1), :].rearrange("p a b -> p (a b)"), bank(1), tmpf[:, 0, :],
                       ALU.mult).then_inc(p_free[1], 1)
            steps.end_loop(FT // 2)
            with dve.Fori(0, FT // 2) as i:
                for jj in range(2):
                    n = Item(MA + 2 * jj, i, 4)
                    dve.wait_ge(p_free[0], n.turns(2, add=1))
                    dve.wait_ge(tile_done, (n + 1).value(1))
                    tt(part_a[:, bass.ds(i * 2 + jj, 1), :].rearrange("p a b -> p (a b)"), bank(1), gates2, ALU.mult)\
                        .then_inc(p_free[1], 1)
            dve.wait_ge(p_free[1], (MA + 15) // 2 + 1)
            dve.wait_ge(p_free[0], (L2 + 46) // 2 + 1)
            for f in range(FT):
                g, win = f // 2, WINDOWS[f // 2]
                src, width = uT[:, f, :], 1
                for s in range(g + 1):
                    dst = wide[:, s % 2, :]
                    do(ts(dst[:, 0:width], src[:, 0:width], 1.0, None, ALU.mult))
                    link(tt(dst[:, width:S], src[:, width:S], src[:, 0:S - width], ALU.add))
                    src, width = dst, 2 * width
                link(tt(src[:, 0:win], src[:, 0:win], rc[:, 0:win], ALU.mult))
                do(tt(uT[:, f, 0:win], src[:, 0:win], uT[:, f, 0:win], ALU.subtract))
                stt(uT[:, f, win:S], src[:, win:S], 1.0 / win, uT[:, f, win:S], ALU.mult, ALU.subtract).then_inc(d_ok, 1)
                dve.wait_ge(d_ok, f + 1)
            for f in range(FT):
                dve.wait_ge(d_h, f + 1)
                tt(BL[:, f, :], uT[:, f, :], BH[:, f, :].bitcast(fp32), ALU.subtract).then_inc(d_l, 1)
            for f in range(FT):
                dve.wait_ge(p_free[f % 2], (POOLW + f) // 2 + 1)
                tt(wide[:, f % 2, :], wide[:, f % 2, :], szb2[:, f, :], ALU.mult).then_inc(pw_v, 1)
                dve.wait_ge(pw_h, f + 1)
                tt(BL[:, f, :], wide[:, f % 2, :], BH[:, f, :].bitcast(fp32), ALU.subtract).then_inc(pw_l, 1)
            with dve.Fori(0, FT // 2) as i:
                for jj in range(2):
                    n = Item(MB + 2 * jj, i, 4)
                    dve.wait_ge(p_free[0], n.turns(2, add=1))
                    dve.wait_ge(tile_done, (n + 1).value(1))
                    tt(prod2, bank(1), gates2, ALU.mult).then_inc(p_free[1], 1)
                    dve.wait_ge(p_free[1], (n + 1).turns(2, add=1))
                    tt(merged2[:, bass.ds(i * 2 + jj, 1), :].rearrange("p a b -> p (a b)"),
                       part_a[:, bass.ds(i * 2 + jj, 1), :].rearrange("p a b -> p (a b)"), prod2, ALU.add)\
                        .then_inc(mg2_ok, 1)
                    dve.wait_ge(mg2_ok, Item(jj, i, 2).value(1))
            low_merged(1, merged2)
            add_outputs(1)
            scales(3, 2)


_INS = ["x", "c", "norm_g", "w_mod", "b_mod", "w_in", "a_re", "a_im", "b_re", "b_im", "c_re", "c_im", "d_skip",
        "log_dt", "w_glu", "b_glu", "w_a_o", "w_b_o", "w_out", "final_g", "c_2", "norm_gain_2", "w_ada_2", "b_ada_2",
        "w_in_2", "pool_w_2", "pool_scale_2", "w_branch_a_2", "w_branch_b_2", "w_out_2", "final_gain_2"]
_OUTS = [((1, 512, 1024), "float32")]


def kernel(**inputs):
    import numpy as _np
    import concourse.bacc as _bacc
    from concourse import mybir as _mybir
    from concourse.bass_utils import run_bass_kernel_spmd as _run

    nc = _bacc.Bacc("TRN2", target_bir_lowering=False, num_devices=1)
    arrays, args = {}, []
    for name in _INS:
        a = _np.ascontiguousarray(inputs[name])
        arrays[f"in_{name}_dram"] = a
        args.append(nc.dram_tensor(f"in_{name}_dram", a.shape, _mybir.dt.from_np(a.dtype), kind="ExternalInput").ap())
    for i, (shape, dtype) in enumerate(_OUTS):
        dt = _mybir.dt.from_np(_np.dtype(dtype))
        args.append(nc.dram_tensor(f"out_{i}_dram", shape, dt, kind="ExternalOutput").ap())
    hybrid_two_layers(nc, *args)
    r = _run(nc, [arrays], core_ids=[0])
    got = tuple(r.results[0][f"out_{i}_dram"] for i in range(len(_OUTS)))
    return got[0]
```

```python
import concourse.bass as bass
from concourse import mybir
from contextlib import ExitStack
import math


class Item:

    def __init__(self, fixed, trip=None, per=0):
        self.fixed, self.trip, self.per = fixed, trip, per

    def __add__(self, k):
        return Item(self.fixed + k, self.trip, self.per)

    def value(self, add=0):
        return self.fixed + add + (0 if self.trip is None else self.trip * self.per)

    def turns(self, ring, times=1, add=0):
        return (self.fixed // ring) * times + add + (0 if self.trip is None else self.trip * (self.per // ring * times))

    def slot(self, ring):
        return self.fixed % ring


class Steps:

    def __init__(self, engine, sem):
        self.engine, self.sem, self.base, self.k = engine, sem, 0, 0

    def do(self, instruction):
        instruction.then_inc(self.sem, 1)
        self.k += 1

    def settle(self):
        self.engine.wait_ge(self.sem, self.base + self.k)

    def link(self, instruction):
        self.do(instruction)
        self.settle()

    def begin_loop(self):
        self.start, self.k = self.base + self.k, 0

    def begin_trip(self, trip, per):
        self.base, self.k, self.per = self.start + trip * per, 0, per

    def end_loop(self, trips):
        assert self.k == self.per, (self.k, self.per)
        self.base, self.k = self.start + trips * self.per, 0


def hybrid_two_layers(nc, x, c, norm_g, w_mod, b_mod, w_in, a_re, a_im, b_re, b_im, c_re, c_im, d_skip, log_dt,
                      w_glu, b_glu, w_a_o, w_b_o, w_out, final_g, c_2, norm_gain_2, w_ada_2, b_ada_2, w_in_2,
                      pool_w_2, pool_scale_2, w_branch_a_2, w_branch_b_2, w_out_2, final_gain_2, out):
    fp32, fp32r, i32 = mybir.dt.float32, mybir.dt.float32r, mybir.dt.int32
    ALU, ACT, AX = mybir.AluOpType, mybir.ActivationFunctionType, mybir.AxisListType

    P = 128
    S, D = x.shape[1], x.shape[2]
    TT, FT = S // P, D // P
    DH = 64
    G, N, GP = b_re.shape[1], b_re.shape[2], b_re.shape[3]
    ST = G * N // P
    L = P // GP
    NCH = S // L
    TOPK, H1, H2 = 128, 8, 16
    IDX_SCALE = float(H1 * DH) ** -0.5
    EPS = 1e-6
    NEG, TAKEN = -1e30, -3e38
    WINDOWS = (2, 4, 8, 16)

    XA, KI, KV, QI, ZA, ZB, Q1, GATE, WO = 0, 4, 5, 6, 10, 14, 18, 30, 62
    Q_TILES, GLU_TILES = (18, 19, 22, 25), (20, 23, 26, 28)
    L2, MA, POOLW, MB, WO2, END = 70, 118, 134, 142, 158, 166
    NMOD = 3 * FT
    C_XA, C_ZA, C_Q, C_K, C_ZB, C_QI, C_KI, C_GA, C_GB = 0, 512, 1024, 1536, 1664, 2176, 2688, 2760, 3784

    def by_rows(w):
        return w.rearrange("(k p) n -> p k n", p=P)

    w_mod1, w_mod2 = by_rows(w_mod[0]), by_rows(w_ada_2[0])
    w_in1, w_in2 = by_rows(w_in[0]), by_rows(w_in_2[0])
    glu_w, ao_w, bo_w, out_w1 = by_rows(w_glu[0]), by_rows(w_a_o[0]), by_rows(w_b_o[0]), by_rows(w_out[0])
    pa_w, pb_w, out_w2 = by_rows(w_branch_a_2[0]), by_rows(w_branch_b_2[0]), by_rows(w_out_2[0])
    pool_w = pool_w_2[0].rearrange("g (k p) n -> p g k n", p=P)
    x_v = x[0].rearrange("(t p) d -> p t d", p=P)
    out_v = out[0].rearrange("(t p) d -> p t d", p=P)

    def rows(v):
        return v.rearrange("(r c) -> r c", c=P)

    ctx = ExitStack()
    with ctx:
        def sb(name, shape, dt=fp32):
            return ctx.enter_context(nc.sbuf_tensor(name, shape, dt))

        def sem(name):
            return ctx.enter_context(nc.semaphore(name))

        x_tok = sb("x_tok", [P, TT, D])
        AH, AL = sb("AH", [P, FT, S], fp32r), sb("AL", [P, FT, S], fp32r)
        BH, BL = sb("BH", [P, FT, S], fp32r), sb("BL", [P, FT, S], fp32r)
        raw = sb("raw", [P, 2, FT * P])
        WH, WL = sb("WH", [P, 4, FT * P], fp32r), sb("WL", [P, 2, FT * P], fp32r)
        tmpf = sb("tmpf", [P, 2, S])
        vcol, vcol2 = sb("vcol", [P, P]), sb("vcol2", [P, P])
        ident = sb("ident", [P, P])
        tri1, tri2 = sb("tri1", [P, P]), sb("tri2", [P, P])
        silc, mod1, mod2, gs = sb("silc", [P, 2, FT]), sb("mod1", [P, NMOD]), sb("mod2", [P, NMOD]), sb("gs", [P, 2, FT])
        stat, diag = sb("stat", [P, 4, TT]), sb("diag", [P, TT, P])
        vtok, wtok, m8 = sb("vtok", [P, TT, DH]), sb("wtok", [P, TT, H1]), sb("m8", [P, 3, 8])
        hs = sb("hs", [P, 8, TT])
        ones = sb("ones", [P, 2])
        arena = sb("arena", [P, 21284])
        pp = sb("pp", [P, 24, ST])
        ppi = sb("ppi", [P, 2, ST], i32)
        sc = sb("sc", [P, 2, 2, ST])
        PS = ctx.enter_context(nc.psum_tensor("PS", [P, 8, 512], fp32))
        Z0, Z1, Z2, T0, T1, M0 = 2, 3, 4, 5, 6, 7

        def at(start, *dims, parts=P):
            n = 1
            for d in dims:
                n *= d
            v = arena[0:parts, start:start + n]
            if len(dims) == 1:
                return v
            names = "abcde"[:len(dims)]
            return v.rearrange(f"p ({' '.join(names)}) -> p {' '.join(names)}",
                               **{k: d for k, d in zip(names, dims)})

        E = at(0, 2, ST, L + 1, GP)
        Cin = at(4608, 2, 4, 2, N)
        vrow = at(6144, 2, P)
        Bin = at(5632, 2, ST, GP)
        prod_b, prod_c = at(6400, 2, 512), at(7424, 2, 512)
        mod_sum1 = at(12832, 3 * D)
        Dt = at(4608, G, L, GP)
        mod_ring1 = [at(8704 + k * D, D) for k in range(4)]
        Kraw = at(8704, G, P, parts=GP)
        U = at(8704, G, NCH)
        X = at(10752, L, L, GP, parts=NCH)
        Hs = at(10752, NCH + 1, 2, ST)
        G1T = at(12832, ST, 2, P)
        GB = at(16928, 2, ST, L, GP)
        xaT = at(16928, 4, S)
        BU = at(18976, ST, 2, NCH)
        Y = at(18976, L, P, parts=NCH)
        kiw, kv, qi_s = at(12832, S), at(13344, S), at(13856, S)
        rl, score = at(14368, 1280), at(15648, 1280)
        work = at(20000, 1280)
        sza, szb = at(0, 4, S), at(2048, 4, S)
        ya2, glu_gate, glu_part = at(16928, 4, S), at(14368, S), at(14880, S)
        q_s, lg = at(6656, 2, S), (at(7680, 1280), at(4096, 1280))
        pT, o_s = at(8960, 10, P), at(10240, TT, P)
        gates, parts_ab = at(12832, 2, S), at(13856, 2, S)
        merged1 = at(16928, FT, S)
        gain = at(0, D)
        uT, szb2 = at(0, FT, S), at(4096, FT, S)
        q2, k2, v2, v2tok = at(8192, S), at(8704, S), at(9216, S), at(9728, TT, P)
        beta, om = (at(10240, 1280), at(16900, 1280)), (at(11520, 1280), at(18180, 1280))
        Pw = at(12800, 1284)
        wT, sza2, o2 = at(14084, 10, P), at(15364, S), at(15876, TT, P)
        zeros = at(16388, S)
        mod_sum2, mod_ring = at(6656, 3 * D), (at(10752, D), at(11776, D), at(9728, D))
        shifts, inv_win, inv_count = at(19460, 4, 4), at(19476, 4), at(19480, 4, 16)
        PAD = WINDOWS[-1] // 2
        part_a, merged2 = at(8192, FT, S), at(12288, FT, S)
        wide, gates2, prod2 = at(16384, 2, S), at(17408, S), at(17920, S)
        padded = at(18432 + 1112, 2, PAD + S)
        junk = tmpf[:, :, :].rearrange("p a b -> p (a b)")

        (consts, rows_zero, rows_in, x_in, b_in, c_in, gain_in, cols_t, c_t, gb_t, gb_c, k_t, k_c, silc_ok, mod_done,
         mod_ok, sumsq, root, diag_ok, ht, hv, hh, hl, raw_free_, h_ready, l_ready, tile_done, xa_ok, gb_ok, e_ok, dt_zero,
         dt_in) = [sem(n) for n in (
             "consts rows_zero rows_in x_in b_in c_in gain_in cols_t c_t gb_t gb_c k_t k_c silc_ok mod_done mod_ok sumsq "
             "root diag_ok ht hv hh hl raw_free h_ready l_ready tile_done xa_ok gb_ok e_ok dt_zero dt_in").split()]
        raw_in = [sem(f"raw_in{i}") for i in range(2)]
        mod1_in = [sem(f"mod1_in{i}") for i in range(4)]
        mod_in = [sem(f"mod_in{i}") for i in range(3)]
        p_free = [sem(f"p_free{i}") for i in range(2)]
        (pe_s, act_s, dve_s, pool_s) = [sem(n) for n in ("pe_step", "act_step", "dve_step", "pool_step")]
        (xt, xc, ut, uc, but, buc, scanned, yt, yc, y2t, ya_ok, sin_in, sin_ok, cols_ok, gate_sig, param_ok, mod_used, tables) = [
            sem(n) for n in ("xt xc ut uc but buc scanned yt yc y2t ya_ok sin_in sin_ok cols_ok gate_sig "
                             "param_ok mod_used tables").split()]
        (ki_c, ki_dup, k_c1, k_dup, ki_t, wtok_ok, v_t, vtok_ok, qi_c, idx_s, idx_r, idx_w, amask_ok) = [
            sem(n) for n in "ki_c ki_dup k_c1 k_dup ki_t wtok_ok v_t vtok_ok qi_c idx_s idx_r idx_w amask_ok".split()]
        (q_c, z_ready, z_read, nmax_ok, probs_ok, t_ready, t_copied, o_ready, o_copied, feats_t, feats_c, yb_v, yb_h,
         yb_l, ya2_ok, ya2_h, ya2_l, mg_ok, mg_h, mg_l, wo_v, wo_t, wo_add, x1_ok, out_done, z_gates) = [
            sem(n) for n in ("q_c z_ready z_read nmax_ok probs_ok t_ready t_copied o_ready o_copied feats_t feats_c yb_v "
                             "yb_h yb_l ya2_ok ya2_h ya2_l mg_ok mg_h mg_l wo_v wo_t wo_add x1_ok out_done z_gates"
                             ).split()]
        (v2_t, v2_c, d_ok, d_h, d_l, pw_v, pw_h, pw_l, y2b_ok, head2_m, ld_rows, mod2_read, ms_ok, sig_c, y_v, gelu_ok,
         yh, gate2_sig, part_a_ok, mg2_ok, mod_gate) = [
            sem(n) for n in ("v2_t v2_c d_ok d_h d_l pw_v pw_h pw_l y2b_ok head2_m ld_rows mod2_read ms_ok sig_c y_v "
                             "gelu_ok yh gate2_sig part_a_ok mg2_ok mod_gate").split()]

        def bank(b):
            return PS[:, b, :]

        V_G1, V_BM1, V_C1, V_BG, V_DS, V_C2, V_G2, V_BM2, V_PS, V_AR = 0, 8, 32, 40, 48, 52, 60, 68, 92, 100
        SEGS = ((3, 0, Z0, 0), (2, 512, Z1, 0), (0, 896, Z1, 384), (1, 1024, Z2, 0))
        BLOCKS = [(q, c0 // P + kb, kb) for q, c0, _, _ in SEGS for kb in range(q + 1)]
        T_GROUPS = ((0, 4), (4, 8), (8, 10))

        def weight_source(n):
            def cols(w, col, kt=FT):
                return w[:, 0:kt, col:col + P], kt
            if n < KI:
                return cols(w_in1, C_XA + n * P)
            if n < QI:
                return cols(w_in1, (C_KI, C_K)[n - KI])
            if n < ZA:
                return cols(w_in1, C_QI + (n - QI) * P)
            if n < ZB:
                return cols(w_in1, C_ZA + (n - ZA) * P)
            if n < Q1:
                return cols(w_in1, C_ZB + (n - ZB) * P)
            if n in Q_TILES:
                return cols(w_in1, C_Q + Q_TILES.index(n) * P)
            if n < GATE:
                gate = n not in GLU_TILES
                return cols(glu_w, (GLU_TILES.index(n - gate) + 4 * gate) * P, 4)
            if n < L2:
                return cols(out_w1, (n - WO) * P)
            if n < MA:
                assert False
            if n < MB:
                g, h = (n - POOLW) // 2, (n - POOLW) % 2
                return pool_w[:, g, :, h * P:(h + 1) * P], 2
            return cols(out_w2, (n - WO2) * P)

        block = ctx.enter_context(nc.Block())

        @block.sync
        def _(sp):
            sp.wait_ge(rows_zero, 2)
            for base, v in ((V_G1, norm_g[0]), (V_BM1, b_mod[0]), (V_C1, c[0]), (V_BG, b_glu[0]), (V_DS, d_skip[0]),
                            (V_C2, c_2[0]), (V_G2, norm_gain_2[0]), (V_BM2, b_ada_2[0]), (V_PS, pool_scale_2[0])):
                n = v.shape[0] // P
                sp.dma_start(vrow[base:base + n, 0, :], rows(v)).then_inc(rows_in, 16)
            for part, v in ((0, a_re), (1, a_im)):
                first = V_AR if part == 0 else 0
                sp.dma_start(vrow[first:first + ST, part, :], v[0].rearrange("(t g) n -> t (g n)", g=2)).then_inc(rows_in, 16)
            sp.dma_start(hs[32:48, 0, 0:2], log_dt[0].rearrange("(t g) -> t g", g=2)).then_inc(rows_in, 16)
            for part, v in ((0, c_re), (1, c_im)):
                for dup in range(2):
                    sp.dma_start(Cin[:, part, :, dup, :],
                                 v[0].rearrange("(f g) p n -> (g p) f n", f=4)).then_inc(c_in, 16)
            for part, v in ((0, b_re), (1, b_im)):
                for half in range(2):
                    sp.dma_start(Bin[half * N:(half + 1) * N, part, :, :],
                                 v[0].rearrange("(t g) n p -> g n t p", g=2)[half]).then_inc(b_in, 16)
            sp.dma_start(x_tok[:, :, :], x_v).then_inc(x_in, 16)

            def load(r, src, kt):
                sp.dma_start(raw[:, r.slot(2), 0:kt * P].rearrange("p (k c) -> p k c", c=P), src)\
                    .then_inc(raw_in[r.slot(2)], 16)

            for m in range(NMOD):
                if m >= 4:
                    sp.wait_ge(mod_used, m - 3)
                sp.dma_start(mod_ring1[m % 4], w_mod1[:, m // 3, (m % 3) * D:(m % 3 + 1) * D]).then_inc(mod1_in[m % 4], 16)
            for n in range(GATE):
                if n >= 2:
                    sp.wait_ge(l_ready, n - 1)
                load(Item(n), *weight_source(n))
            with sp.Fori(1, FT // 2 + 1) as i:
                for jj in range(2):
                    for k, (w, col, kt) in enumerate(((w_in1, C_GA, 8), (w_in1, C_GB, 8), (ao_w, 0, 4), (bo_w, 0, 4))):
                        n = Item(GATE + 4 * (jj - 2) + k, i, 8)
                        at_col = i * (2 * P) + (col + (jj - 2) * P)
                        sp.wait_ge(l_ready, n.value(-1))
                        load(n, w[:, 0:kt, bass.ds(at_col, P)], kt)
                        if k < 3:
                            m = Item(NMOD + 3 * (jj - 2) + k, i, 6)
                            at_row = i * 2 + (jj - 2)
                            sp.wait_ge(mod_used, m.value(-2))
                            if k == 2:
                                sp.wait_ge(feats_c, 4)
                            sp.dma_start(mod_ring[k], w_mod2[:, bass.ds(at_row, 1), k * D:(k + 1) * D]
                                         .rearrange("p a n -> p (a n)")).then_inc(mod_in[k], 16)
            for n in range(WO, L2):
                sp.wait_ge(l_ready, n - 1)
                load(Item(n), *weight_source(n))
            with sp.Fori(1, FT // 2 + 1) as i:
                for jj in range(2):
                    for k, s in enumerate((0, 1, 2, 3, 4, 5)):
                        n = Item(L2 + 6 * (jj - 2) + k, i, 12)
                        at_col = i * (2 * P) + (s * D + (jj - 2) * P)
                        sp.wait_ge(l_ready, n.value(-1))
                        load(n, w_in2[:, :, bass.ds(at_col, P)], FT)
            with sp.Fori(1, FT // 2 + 1) as i:
                for jj in range(2):
                    for k, (w, col) in enumerate(((w_in2, 6 * D), (pa_w, 0))):
                        n = Item(MA + 2 * (jj - 2) + k, i, 4)
                        at_col = i * (2 * P) + (col + (jj - 2) * P)
                        sp.wait_ge(l_ready, n.value(-1))
                        load(n, w[:, :, bass.ds(at_col, P)], FT)
            for n in range(POOLW, MB):
                sp.wait_ge(l_ready, n - 1)
                load(Item(n), *weight_source(n))
            with sp.Fori(1, FT // 2 + 1) as i:
                for jj in range(2):
                    for k, (w, col) in enumerate(((w_in2, 7 * D), (pb_w, 0))):
                        n = Item(MB + 2 * (jj - 2) + k, i, 4)
                        at_col = i * (2 * P) + (col + (jj - 2) * P)
                        sp.wait_ge(l_ready, n.value(-1))
                        load(n, w[:, :, bass.ds(at_col, P)], FT)
            for n in range(WO2, END):
                sp.wait_ge(l_ready, n - 1)
                load(Item(n), *weight_source(n))
            for t in range(TT):
                sp.wait_ge(x1_ok, TT + t + 1)
                sp.dma_start(out_v[:, t, :], x_tok[:, t, :]).then_inc(out_done, 16)
            sp.wait_ge(out_done, 16 * TT)

        @block.gpsimd
        def _(pool):
            steps = Steps(pool, pool_s)
            steps.do(nc.gpsimd.memset(ident[:, :], 0.0))
            steps.do(nc.gpsimd.memset(tri1[:, :], 0.0))
            steps.do(nc.gpsimd.memset(tri2[:, :], 0.0))
            steps.do(nc.gpsimd.memset(wtok[:, :, :], 0.0))
            steps.do(nc.gpsimd.memset(ones[:, :], 1.0))
            steps.settle()
            steps.do(nc.gpsimd.affine_select(out=ident[:, :], in_=ident[:, :], compare_op=ALU.not_equal, fill=1.0, base=0,
                                             pattern=[[-1, P]], channel_multiplier=1))
            steps.do(nc.gpsimd.affine_select(out=tri1[:, :], in_=tri1[:, :], compare_op=ALU.is_ge, fill=NEG, base=0,
                                             pattern=[[-1, P]], channel_multiplier=1))
            steps.do(nc.gpsimd.affine_select(out=tri2[:, :], in_=tri2[:, :], compare_op=ALU.is_gt, fill=NEG, base=0,
                                             pattern=[[-1, P]], channel_multiplier=1))
            steps.settle()
            nc.gpsimd.memset(pp[:, 23, :], 0.0).then_inc(consts, 1)

            def low(n, kt):
                r, h = n.slot(2), n.slot(4)
                pool.wait_ge(h_ready, n.value(1))
                if n.trip is not None or n.fixed >= 2:
                    pool.wait_ge(tile_done, n.value(-1))
                nc.gpsimd.tensor_tensor(WL[:, r, 0:kt * P], raw[:, r, 0:kt * P], WH[:, h, 0:kt * P].bitcast(fp32),
                                        ALU.subtract).then_inc(l_ready, 1)

            pprod = [prod_b[:, k, :].rearrange("p (a b c) -> p a b c", a=2, b=ST) for k in range(2)]

            def times(out_, in_, re, im):
                for o, i, v in ((pprod[0], in_, re.unsqueeze(1)), (pprod[1], in_[:, ::-1, :, :], im)):
                    steps.do(nc.gpsimd.tensor_tensor(o, i, v.unsqueeze(3).broadcast_to([P, 2, ST, GP]), ALU.mult))
                steps.settle()
                steps.link(nc.gpsimd.tensor_tensor(out_, pprod[0], pprod[1], ALU.add))

            pool.wait_ge(param_ok, 1)
            pool.wait_ge(b_in, 64)
            times(GB[:, :, :, 0, :], Bin, pp[:, 8, :], pp[:, 20:22, :])
            for d in range(1, L):
                times(GB[:, :, :, d, :], GB[:, :, :, d - 1, :], pp[:, 5, :], pp[:, 13:15, :])
            nc.gpsimd.memset(pp[:, 23, :], 0.0).then_inc(gb_ok, 1)

            for n in range(GATE):
                low(Item(n), weight_source(n)[1])
            with pool.Fori(0, FT // 2) as i:
                for k in range(8):
                    low(Item(GATE + k, i, 8), 8 if k % 4 < 2 else 4)
            for n in range(WO, L2):
                low(Item(n), FT)
            pool.wait_ge(mg_l, FT)
            steps.do(nc.gpsimd.memset(shifts, 1.0))
            for g, win in enumerate(WINDOWS):
                steps.do(nc.gpsimd.memset(inv_win[:, g:g + 1], 1.0 / win))
                steps.do(nc.gpsimd.memset(inv_count[:, g, :], 1.0 / win))
            steps.settle()
            for g in range(3):
                steps.do(nc.gpsimd.memset(shifts[:, g, g + 1:4], 0.0))
            for t in range(WINDOWS[-1] - 1):
                first = next(g for g, win in enumerate(WINDOWS) if win > t)
                steps.do(nc.gpsimd.memset(inv_count[:, first:4, t], 1.0 / (t + 1)))
            steps.settle()
            for k in range(2):
                nc.gpsimd.memset(padded[:, k, 0:PAD], 0.0).then_inc(tables, 1)
            with pool.Fori(0, FT // 2) as i:
                for k in range(12):
                    low(Item(L2 + k, i, 12), FT)
            with pool.Fori(0, FT // 2) as i:
                for k in range(4):
                    low(Item(MA + k, i, 4), FT)
            for n in range(POOLW, MB):
                low(Item(n), 2)
            with pool.Fori(0, FT // 2) as i:
                for k in range(4):
                    low(Item(MB + k, i, 4), FT)
            for n in range(WO2, END):
                low(Item(n), FT)

        @block.tensor
        def _(pe):
            def product(n, hi, lo, kt, k0=0, ready=None):
                s = n.slot(2)
                pe.wait_ge(l_ready, n.value(1))
                if n.trip is not None or n.fixed >= 2:
                    pe.wait_ge(p_free[s], n.turns(2))
                for k in range(kt):
                    if ready:
                        pe.wait_ge(ready[0], ready[1] + k)
                    w_hi, w_lo = WH[:, n.slot(4), k * P:(k + 1) * P], WL[:, s, k * P:(k + 1) * P]
                    nc.tensor.matmul(bank(s), w_hi, hi[:, k0 + k, :], start=(k == 0), stop=False)
                    nc.tensor.matmul(bank(s), w_hi, lo[:, k0 + k, :], start=False, stop=False)
                    last = nc.tensor.matmul(bank(s), w_lo, hi[:, k0 + k, :], start=False, stop=(k == kt - 1))
                last.then_inc(tile_done, 1)

            def taken_out(n):
                pe.wait_ge(p_free[n.slot(2)], n.turns(2, add=1))

            def modulation(layer):
                pe.wait_ge(mod_used, NMOD * (layer + 1))
                sums = (mod_sum1, mod_sum2)[layer]
                for m in range(NMOD):
                    last = nc.tensor.matmul(PS[:, M0, 256 + m:257 + m], sums[:, m * P:(m + 1) * P], ones[:, 0:1],
                                            start=True, stop=True)
                last.then_inc(mod_done, 1)

            def normed_features(layer):
                pe.wait_ge(diag_ok, layer + 1)
                for f in range(FT):
                    if f >= 2:
                        pe.wait_ge(hv, FT * layer + f - 1)
                    for t in range(TT):
                        last = nc.tensor.matmul(PS[:, Z0 + f % 2, t * P:(t + 1) * P], x_tok[:, t, f * P:(f + 1) * P],
                                                diag[:, t, :], start=True, stop=True)
                    last.then_inc(ht, 1)

            def attend_scores(hd, base_q, base_k, h):
                for q, _, b, c in SEGS:
                    last = nc.tensor.matmul(PS[:, b, c:c + (q + 1) * P], base_q[h * DH:(h + 1) * DH, q * P:(q + 1) * P],
                                            base_k[h * DH:(h + 1) * DH, 0:(q + 1) * P], start=True, stop=True)
                last.then_inc(z_ready, 1)

            def attend_values(hd, h, probs, wt, vals):
                pe.wait_ge(probs_ok, hd.value(1))
                for g, (lo, hi) in enumerate(T_GROUPS):
                    if hd.trip is not None or 3 * hd.fixed + g >= 2:
                        pe.wait_ge(t_copied, Item(3 * hd.fixed + g, hd.trip, 3 * hd.per).value(-1))
                    b = T0 + (3 * hd.fixed + g) % 2
                    for n in range(lo, hi):
                        last = nc.tensor.transpose(PS[:, b, (n - lo) * P:(n - lo + 1) * P], probs[:, n * P:(n + 1) * P],
                                                   ident[:, :])
                    last.then_inc(t_ready, 1)
                if hd.trip is not None or hd.fixed >= 1:
                    pe.wait_ge(o_copied, hd.value())
                pe.wait_ge(t_copied, Item(3 * hd.fixed, hd.trip, 3 * hd.per).value(3))
                for q, n, kb in BLOCKS:
                    last = nc.tensor.matmul(PS[:, M0, q * DH:(q + 1) * DH], wt[:, n, :], vals(kb),
                                            start=(kb == 0), stop=(kb == q))
                last.then_inc(o_ready, 1)

            def pair_features(hd, o):
                pe.wait_ge(o_copied, hd.value(1))
                for t in range(TT):
                    last = nc.tensor.transpose(PS[:, M0, t * P:(t + 1) * P], o[:, t, :], ident[:, :])
                last.then_inc(feats_t, 1)

            def out_transposes(j):
                n = Item((WO if j < FT else WO2 - FT) + j)
                taken_out(n)
                if j >= 2:
                    pe.wait_ge(wo_add, j - 1)
                for t in range(TT):
                    last = nc.tensor.transpose(PS[:, T0 + j % 2, t * P:(t + 1) * P], tmpf[:, j % 2, t * P:(t + 1) * P],
                                               ident[:, :])
                last.then_inc(wo_t, 1)

            pe.wait_ge(consts, 1)
            pe.wait_ge(rows_in, 16 * 11)
            pe.wait_ge(ld_rows, 1)
            for part in range(2):
                last = nc.tensor.transpose(PS[:, M0, part * P:(part + 1) * P], vrow[:, part, :], ident[:, :])
            last.then_inc(cols_t, 1)
            pe.wait_ge(c_in, 64)
            for part in range(2):
                for f in range(4):
                    last = nc.tensor.transpose(PS[:, Z0 + part, f * P:(f + 1) * P],
                                               Cin[:, part, f, :, :].rearrange("p a b -> p (a b)"), ident[:, :])
            last.then_inc(c_t, 1)
            pe.wait_ge(cols_ok, 1)
            modulation(0)
            normed_features(0)
            pe.wait_ge(hl, FT)
            for n in (XA, XA + 1):
                product(Item(n), AH, AL, FT)
            pe.wait_ge(gb_ok, 1)
            for r in range(8):
                if r >= 2:
                    pe.wait_ge(gb_c, r - 1)
                for k in range(4):
                    t, ri = 2 * r + k // 2, k % 2
                    last = nc.tensor.transpose(PS[:, T0 + r % 2, k * P:(k + 1) * P],
                                               GB[:, ri, t, :, :].rearrange("p a b -> p (a b)"), ident[:, :])
                last.then_inc(gb_t, 1)
            pe.wait_ge(e_ok, 1)
            for r in range(8):
                if r >= 2:
                    pe.wait_ge(k_c, r - 1)
                for k in range(4):
                    t, half = 4 * (r // 2) + k, (r % 2) * N
                    for ri in range(2):
                        last = nc.tensor.matmul(PS[0:GP, Z0 + r % 2, k * P:(k + 1) * P], GB[half:half + N, ri, t, 0, :],
                                                E[half:half + N, ri, t, 0:L, :].rearrange("p a b -> p (a b)"),
                                                start=(ri == 0), stop=(ri == 1))
                last.then_inc(k_t, 1)

            product(Item(XA + 2), AH, AL, FT)
            for f in range(4):
                if f:
                    product(Item(XA + 2 + f), AH, AL, FT)
                taken_out(Item(XA + f))
                if f >= 1:
                    pe.wait_ge(uc, f)
                    pe.wait_ge(buc, f)
                steps_of = xaT[:, f, :].rearrange("p (c j) -> p c j", j=L)
                for s in range(L):
                    last = nc.tensor.transpose(PS[0:NCH, T1 + s // 4, (s % 4) * P:(s % 4 + 1) * P],
                                               steps_of[:, :, L - 1 - s], ident[:, :])
                last.then_inc(xt, 1)
                pe.wait_ge(xc, 2 * f + 2)
                for g in range(L):
                    last = nc.tensor.transpose(PS[:, T1, g * NCH:(g + 1) * NCH], X[:, g, :, :].rearrange("p a b -> p (a b)"),
                                               ident[0:NCH, 0:NCH])
                last.then_inc(ut, 1)
                pe.wait_ge(uc, f + 1)
                for t in range(4):
                    for ri in range(2):
                        for half in range(2):
                            last = nc.tensor.matmul(
                                PS[half * N:(half + 1) * N, M0, (2 * t + ri) * NCH:(2 * t + ri + 1) * NCH],
                                G1T[:, 4 * f + t, ri, half * N:(half + 1) * N], U[:, 2 * (4 * f + t) + half, :],
                                start=True, stop=True)
                last.then_inc(but, 1)
            pe.wait_ge(buc, 4)
            taken_out(Item(KI))
            for t in range(TT):
                last = nc.tensor.transpose(PS[:, M0, t * P:(t + 1) * P], kiw[:, t * P:(t + 1) * P], ident[:, :])
            last.then_inc(ki_t, 1)
            product(Item(QI), AH, AL, FT)
            taken_out(Item(KV))
            pe.wait_ge(wtok_ok, 1)
            for t in range(TT):
                last = nc.tensor.transpose(PS[:, M0, t * P:(t + 1) * P], kv[:, t * P:(t + 1) * P], ident[:, :])
            last.then_inc(v_t, 1)
            pe.wait_ge(ki_dup, 16)
            for j in range(4):
                if j:
                    product(Item(QI + j), AH, AL, FT)
                taken_out(Item(QI + j))
                for h in range(2):
                    if 2 * j + h:
                        pe.wait_ge(idx_r, 2 * j + h)
                    for q, _, b, c in SEGS:
                        if q:
                            last = nc.tensor.matmul(PS[:, b, c:c + (q + 1) * P],
                                                    qi_s[h * DH:(h + 1) * DH, q * P:(q + 1) * P],
                                                    kiw[h * DH:(h + 1) * DH, 0:(q + 1) * P], start=True, stop=True)
                    last.then_inc(idx_s, 1)
            pe.wait_ge(scanned, 1)
            pe.wait_ge(dt_in, 128)
            pe.wait_ge(idx_r, H1)
            for f in range(4):
                for half4 in range(2):
                    if f:
                        pe.wait_ge(yc, 2 * f + half4 - 1)
                    for k in range(4):
                        t, half = 4 * f + k, half4 * N
                        g = 2 * t + half4
                        o = PS[0:NCH, Z0 + half4, k * P:(k + 1) * P]
                        for ri in range(2):
                            nc.tensor.matmul(o, Hs[half:half + N, 0:NCH, ri, t],
                                             E[half:half + N, ri, t, 1:L + 1, :].rearrange("p a b -> p (a b)"),
                                             start=(ri == 0), stop=False)
                        last = nc.tensor.matmul(o, U[:, g, :], Dt[:, g, :, :].rearrange("p a b -> p (a b)"),
                                                start=False, stop=True)
                    last.then_inc(yt, 1)
                pe.wait_ge(yc, 2 * f + 2)
                if f:
                    pe.wait_ge(y_v, f)
                for s in range(L):
                    last = nc.tensor.transpose(PS[:, T0, s * NCH:(s + 1) * NCH], Y[:, s, :], ident[0:NCH, 0:NCH])
                last.then_inc(y2t, 1)
            for n in range(ZA, Q1):
                product(Item(n), AH, AL, FT)
            product(Item(Q1), AH, AL, FT)
            pe.wait_ge(ya_ok, 4)
            pe.wait_ge(k_dup, 16)
            taken_out(Item(Q1))
            attend_scores(Item(0), q_s[:, 0, :], kv, 0)
            for j in range(4):
                for h in range(2):
                    hd = Item(2 * j + h)
                    if hd.fixed < H1 - 1:
                        if h == 1:
                            taken_out(Item(Q_TILES[j + 1]))
                        pe.wait_ge(z_read, hd.fixed + 1)
                        attend_scores(hd + 1, q_s[:, (hd.fixed + 1) // 2 % 2, :], kv, 1 - h)
                    if h == 1:
                        product(Item(GLU_TILES[j]), BH, BL, 4)
                        product(Item(GLU_TILES[j] + 1), BH, BL, 4)
                    elif j < 3:
                        product(Item(Q_TILES[j + 1]), AH, AL, FT)
                    pe.wait_ge(feats_c, j)
                    attend_values(hd, h, lg[h], pT, lambda kb: vtok[:, kb, :])
                pair_features(Item(2 * j + 1), o_s)
            with pe.Fori(0, FT // 2) as i:
                for jj in range(2):
                    n = Item(GATE + 4 * jj, i, 8)
                    product(n, AH, AL, FT)
                    product(n + 1, AH, AL, FT)
                    pe.wait_ge(ya2_l, 1)
                    product(n + 2, BH, BL, 4)
                    pe.wait_ge(yb_l, 4)
                    product(n + 3, BH, BL, 4, k0=4)
            pe.wait_ge(feats_c, 4)
            modulation(1)
            for j in range(FT + 1):
                if j < FT:
                    product(Item(WO + j), AH, AL, FT, ready=(mg_l, 1) if j == 0 else None)
                if j:
                    out_transposes(j - 1)

            pe.wait_ge(mod2_read, 1)
            normed_features(1)
            pe.wait_ge(hl, 2 * FT)
            with pe.Fori(0, FT // 2) as i:
                for jj in range(2):
                    n = Item(L2 + 6 * jj, i, 12)
                    pair = Item(jj, i, 2)
                    first, second = Item(H1 + 2 * jj, i, 4), Item(H1 + 2 * jj + 1, i, 4)
                    for k in range(3):
                        product(n + k, AH, AL, FT)
                    taken_out(n)
                    taken_out(n + 1)
                    attend_scores(first, q2, k2, 0)
                    taken_out(n + 2)
                    pe.wait_ge(feats_c, pair.value(4))
                    for t in range(TT):
                        last = nc.tensor.transpose(PS[:, M0, t * P:(t + 1) * P], v2[:, t * P:(t + 1) * P], ident[:, :])
                    last.then_inc(v2_t, 1)
                    product(n + 3, AH, AL, FT)
                    pe.wait_ge(z_gates, first.value(1 - H1))
                    attend_scores(second, q2, k2, 1)
                    product(n + 4, AH, AL, FT)
                    pe.wait_ge(v2_c, pair.value(1))
                    attend_values(first, 0, beta[0], wT, lambda kb: v2tok[:, kb, 0:DH])
                    product(n + 5, AH, AL, FT)
                    attend_values(second, 1, beta[1], wT, lambda kb: v2tok[:, kb, DH:P])
                    pair_features(second, o2)
            pe.wait_ge(y2b_ok, FT)
            with pe.Fori(0, FT // 2) as i:
                for jj in range(2):
                    n = Item(MA + 2 * jj, i, 4)
                    product(n, AH, AL, FT)
                    product(n + 1, BH, BL, FT)
            for n in range(POOLW, MB):
                pe.wait_ge(d_l, 2 * ((n - POOLW) // 2) + 2)
                product(Item(n), BH, BL, 2, k0=2 * ((n - POOLW) // 2))
            with pe.Fori(0, FT // 2) as i:
                for jj in range(2):
                    n = Item(MB + 2 * jj, i, 4)
                    product(n, AH, AL, FT)
                    pe.wait_ge(pw_l, FT)
                    product(n + 1, BH, BL, FT)
            for j in range(FT + 1):
                if j < FT:
                    product(Item(WO2 + j), AH, AL, FT, ready=(mg_l, FT + 1) if j == 0 else None)
                if j:
                    out_transposes(FT + j - 1)

        @block.scalar
        def _(act):
            def high(n, kt):
                r, h = n.slot(2), n.slot(4)
                act.wait_ge(raw_in[r], n.turns(2, 16, 16))
                if n.trip is not None or n.fixed >= 4:
                    act.wait_ge(tile_done, n.value(-3))
                nc.scalar.activation(WH[:, h, 0:kt * P], raw[:, r, 0:kt * P], ACT.Copy).then_inc(h_ready, 1)

            def kt_of(n):
                return weight_source(n)[1]

            def squares(s):
                for t in range(TT):
                    if s or t:
                        act.wait_ge(sumsq, 4 * s + t)
                    if s in (1, 3):
                        act.wait_ge(wo_add, FT * (s // 2 + 1))
                    if s == 2:
                        act.wait_ge(x1_ok, t + 1)
                    nc.scalar.activation(junk, x_tok[:, t, :], ACT.Square,
                                         accum_out=stat[:, 0, t:t + 1]).then_inc(sumsq, 1)
                act.wait_ge(ms_ok, s + 1)
                nc.scalar.activation(stat[:, 2, :], stat[:, 1, :], ACT.Sqrt).then_inc(root, 1)

            def features(layer):
                act.wait_ge(mod_ok, layer + 1)
                m = (mod1, mod2)[layer]
                for f in range(FT):
                    n = FT * layer + f
                    act.wait_ge(ht, n + 1)
                    if f >= 2:
                        act.wait_ge(hl, n - 1)
                    nc.scalar.activation(tmpf[:, f % 2, :], bank(Z0 + f % 2), ACT.Identity, bias=m[:, f:f + 1],
                                         scale=gs[:, layer, f:f + 1]).then_inc(hv, 1)
                    act.wait_ge(hv, n + 1)
                    nc.scalar.activation(AH[:, f, :], tmpf[:, f % 2, :], ACT.Copy).then_inc(hh, 1)

            def copy_out(n, dst):
                act.wait_ge(tile_done, n.value(1))
                nc.scalar.activation(dst, bank(n.slot(2)), ACT.Copy).then_inc(p_free[n.slot(2)], 1)

            def copy_gate(n):
                act.wait_ge(tile_done, n.value(1))
                nc.scalar.activation(gates2, bank(0), ACT.Sigmoid).then_inc(p_free[0], 1)

            def t_copies(hd, wt):
                act.wait_ge(o_ready, hd.value())
                for g, (lo, hi) in enumerate(T_GROUPS):
                    tg = Item(3 * hd.fixed + g, hd.trip, 3 * hd.per)
                    act.wait_ge(t_ready, tg.value(1))
                    nc.scalar.activation(wt[:, lo:hi, :].rearrange("p a b -> p (a b)"),
                                         PS[:, T0 + tg.slot(2), 0:(hi - lo) * P], ACT.Copy).then_inc(t_copied, 1)

            act.wait_ge(cols_ok, 1)
            for k, v in enumerate((V_C1, V_C2)):
                nc.scalar.activation(silc[:, k, :], vcol[:, v:v + FT], ACT.Sigmoid).then_inc(sig_c, 1)
            act.wait_ge(sin_in, 1)
            for k in range(2):
                nc.scalar.activation(pp[:, 12 + k, :], pp[:, 10 + k, :], ACT.Sin).then_inc(sin_ok, 1)
            act.wait_ge(x_in, 16)
            squares(0)
            high(Item(0), FT)
            high(Item(1), FT)
            features(0)
            high(Item(2), FT)
            high(Item(3), FT)
            act.wait_ge(mod_done, 1)
            for r in range(8):
                act.wait_ge(gb_t, r + 1)
                nc.scalar.activation(G1T[:, 2 * r:2 * r + 2, :, :].rearrange("p a b c -> p (a b c)"), bank(T0 + r % 2),
                                     ACT.Copy).then_inc(gb_c, 1)
            for r in range(8):
                act.wait_ge(k_t, r + 1)
                nc.scalar.activation(Kraw[:, 8 * (r // 2) + r % 2:8 * (r // 2) + 8:2, :],
                                     PS[0:GP, Z0 + r % 2, :].rearrange("p (a b) -> p a b", b=P), ACT.Copy).then_inc(k_c, 1)
            act.wait_ge(k_c, 8)
            act.wait_ge(dt_zero, 1)
            for j in range(L):
                d = L - 1 - j
                act.dma_start(Dt[d * GP:(d + 1) * GP, :, j:L, :].rearrange("p a b c -> p a (b c)"),
                              Kraw[:, :, 0:(L - j) * GP]).then_inc(dt_in, 16)
            for n in range(XA, XA + 3):
                copy_out(Item(n), xaT[:, n, :])
            high(Item(XA + 4), FT)
            act.wait_ge(dt_in, 16 * L)
            for f in range(4):
                if f == 1:
                    copy_out(Item(XA + 3), xaT[:, 3, :])
                if f:
                    high(Item(XA + 4 + f), FT)
                act.wait_ge(xt, f + 1)
                if f:
                    act.wait_ge(ut, f)
                for k in range(2):
                    nc.scalar.activation(X[:, :, 4 * k:4 * k + 4, :],
                                         PS[0:NCH, T1 + k, :].rearrange("p (s g c) -> p g s c", s=4, g=L), ACT.Copy).then_inc(xc, 1)
                act.wait_ge(ut, f + 1)
                nc.scalar.activation(U[:, L * f:L * f + L, :].rearrange("p a b -> p (a b)"), bank(T1),
                                     ACT.Copy).then_inc(uc, 1)
                act.wait_ge(but, f + 1)
                nc.scalar.activation(BU[:, 4 * f:4 * f + 4, :, :].rearrange("p a b c -> p (a b c)"), bank(M0),
                                     ACT.Copy).then_inc(buc, 1)
            copy_out(Item(KI), kiw)
            copy_out(Item(KV), kv)
            act.wait_ge(ki_t, 1)
            nc.scalar.activation(wtok[:, :, :], bank(M0).rearrange("p (t f) -> p t f", f=P)[:, :, DH:DH + H1],
                                 ACT.Copy).then_inc(wtok_ok, 1)
            act.dma_start(kiw[DH:P, :], kiw[0:DH, :]).then_inc(ki_dup, 16)
            act.wait_ge(v_t, 1)
            nc.scalar.activation(vtok[:, :, :], bank(M0).rearrange("p (t f) -> p t f", f=P)[:, :, DH:P],
                                 ACT.Copy).then_inc(vtok_ok, 1)
            act.dma_start(kv[DH:P, :], kv[0:DH, :]).then_inc(k_dup, 16)
            for j in range(4):
                if j:
                    act.wait_ge(idx_s, 2 * j)
                copy_out(Item(QI + j), qi_s)
                high(Item(QI + j + 2), FT)
                for h in range(2 * j, 2 * j + 2):
                    act.wait_ge(idx_s, h + 1)
                    if h:
                        act.wait_ge(idx_w, h)
                    for q, c0, b, c in SEGS:
                        if q:
                            last = nc.scalar.activation(rl[:, c0:c0 + (q + 1) * P], PS[:, b, c:c + (q + 1) * P],
                                                        ACT.Relu, scale=IDX_SCALE)
                    last.then_inc(idx_r, 1)
            for f in range(4):
                for half4 in range(2):
                    act.wait_ge(yt, 2 * f + half4 + 1)
                    if f and half4 == 0:
                        act.wait_ge(y2t, f)
                    nc.scalar.activation(
                        Y.rearrange("p i (k h c) -> p i k h c", h=2, c=GP)[:, :, :, half4, :],
                        PS[0:NCH, Z0 + half4, :].rearrange("p (g i c) -> p i g c", g=4, i=L), ACT.Copy).then_inc(yc, 1)
                act.wait_ge(y_v, f + 1)
                nc.scalar.activation(tmpf[:, f % 2, :], tmpf[:, f % 2, :], ACT.Gelu_apprx_tanh).then_inc(gelu_ok, 1)
                act.wait_ge(gelu_ok, f + 1)
                nc.scalar.activation(BH[:, f, :], tmpf[:, f % 2, :], ACT.Copy).then_inc(yh, 1)
            for n in range(ZA, Q1):
                act.wait_ge(tile_done, n + 1)
                if n >= ZA + 2:
                    act.wait_ge(p_free[n % 2], n // 2)
                act.wait_ge(ya_ok, 4)
                nc.scalar.activation(tmpf[:, n % 2, :], bank(n % 2), ACT.Sigmoid).then_inc(gate_sig, 1)
                high(Item(n + 2), FT)
            copy_out(Item(Q1), q_s[:, 0, :])
            high(Item(Q1 + 2), FT)

            def exps(hd):
                act.wait_ge(nmax_ok, hd + 1)
                for q, c0, _, _ in SEGS:
                    seg = lg[hd % 2][:, c0:c0 + (q + 1) * P]
                    last = nc.scalar.activation(seg, seg, ACT.Exp, bias=hs[:, 4 * (hd % 2) + 1, q:q + 1], scale=DH ** -0.5,
                                                accum_out=hs[:, 4 * (hd % 2) + 2, q:q + 1])
                last.then_inc(probs_ok, 1)

            exps(0)
            for hd in range(H1):
                j = hd // 2
                tiles = ((GLU_TILES[j], GLU_TILES[j] + 1) if hd % 2 else Q_TILES[j + 1:j + 2])
                if tiles:
                    high(Item(tiles[0] + 2), kt_of(tiles[0] + 2) if tiles[0] + 2 < GATE else FT)
                if hd < H1 - 1:
                    exps(hd + 1)
                if hd % 2:
                    n = GLU_TILES[j]
                    act.wait_ge(tile_done, n + 2)
                    act.wait_ge(ya2_ok, j)
                    nc.scalar.activation(glu_gate, bank((n + 1) % 2), ACT.Sigmoid,
                                         bias=vcol[:, V_BG + 4 + j:V_BG + 5 + j]).then_inc(p_free[(n + 1) % 2], 1)
                    high(Item(n + 3), kt_of(n + 3) if n + 3 < GATE else FT)
                elif j < 3:
                    copy_out(Item(Q_TILES[j + 1]), q_s[:, (j + 1) % 2, :])
                t_copies(Item(hd), pT)
            act.wait_ge(ya2_ok, 4)
            nc.scalar.activation(BH[:, 0:4, :].rearrange("p a b -> p (a b)"), ya2.rearrange("p a b -> p (a b)"),
                                 ACT.Copy).then_inc(ya2_h, 1)
            with act.Fori(0, FT // 2) as i:
                for jj in range(2):
                    n = Item(GATE + 4 * jj, i, 8)
                    for k in range(4):
                        high(n + k + 2, (4, 4, 8, 8)[k])
                        if k < 2:
                            act.wait_ge(p_free[k], (n + k).turns(2))
                            act.wait_ge(tile_done, (n + k).value(1))
                            nc.scalar.activation(gates[:, k, :], bank(k), ACT.Sigmoid).then_inc(p_free[k], 1)
            act.wait_ge(mg_ok, FT)
            for f in range(FT):
                nc.scalar.activation(AH[:, f, :], merged1[:, f, :], ACT.Copy).then_inc(mg_h, 1)
            act.dma_start(gain, final_g.rearrange("(o n) -> o n", o=1).broadcast_to([P, D])).then_inc(gain_in, 16)

            def out_tile(n, j, m):
                act.wait_ge(tile_done, n + 1)
                if j % FT >= 2:
                    act.wait_ge(wo_t, j - 1)
                nc.scalar.activation(tmpf[:, j % 2, :], bank(n % 2), ACT.Identity,
                                     scale=m[:, 16 + j % FT:17 + j % FT]).then_inc(p_free[n % 2], 1)

            act.wait_ge(mg_l, FT)
            for j in range(FT):
                high(Item(WO + j + 2), FT)
                out_tile(WO + j, j, mod1)
            squares(1)
            squares(2)
            features(1)
            with act.Fori(0, FT // 2) as i:
                for jj in range(2):
                    n, pair = Item(L2 + 6 * jj, i, 12), Item(jj, i, 2)

                    def gates_of(h):
                        hd = Item(H1 + 2 * jj + h, i, 4)
                        act.wait_ge(head2_m, hd.value(1 - H1))
                        act.wait_ge(t_ready, Item(3 * hd.fixed - 3, i, 12).value())
                        act.wait_ge(probs_ok, hd.value(-1))
                        for dst, scale in ((beta[h], DH ** -0.5), (om[h], -DH ** -0.5)):
                            for col, b, width in ((0, Z0, 512), (512, Z1, 512), (1024, Z2, 256)):
                                last = nc.scalar.activation(dst[:, col:col + width], PS[:, b, 0:width], ACT.Sigmoid,
                                                            scale=scale)
                        last.then_inc(z_gates, 1)

                    high(n + 2, FT)
                    act.wait_ge(z_ready, Item(H1 + 2 * jj, i, 4).value())
                    copy_out(n, q2)
                    high(n + 3, FT)
                    copy_out(n + 1, k2)
                    high(n + 4, FT)
                    copy_out(n + 2, v2)
                    gates_of(0)
                    act.wait_ge(v2_t, pair.value(1))
                    act.wait_ge(o_ready, Item(H1 + 2 * jj, i, 4).value())
                    nc.scalar.activation(v2tok.rearrange("p a b -> p (a b)"), bank(M0), ACT.Copy).then_inc(v2_c, 1)
                    high(n + 5, FT)
                    act.wait_ge(tile_done, (n + 3).value(1))
                    nc.scalar.activation(sza2, bank(1), ACT.Sigmoid).then_inc(gate2_sig, 1)
                    gates_of(1)
                    t_copies(Item(H1 + 2 * jj, i, 4), wT)
                    high(n + 6, FT)
                    act.wait_ge(tile_done, (n + 5).value(1))
                    nc.scalar.activation(tmpf[:, 0, :], bank(1), ACT.Sigmoid).then_inc(gate2_sig, 1)
                    t_copies(Item(H1 + 2 * jj + 1, i, 4), wT)
                    high(n + 7, FT)
            with act.Fori(0, FT // 2) as i:
                for jj in range(2):
                    n = Item(MA + 2 * jj, i, 4)
                    high(n + 2, FT)
                    act.wait_ge(p_free[1], n.turns(2))
                    copy_gate(n)
                    high(n + 3, FT)
            act.wait_ge(d_ok, FT)
            for f in range(FT):
                nc.scalar.activation(BH[:, f, :], uT[:, f, :], ACT.Copy).then_inc(d_h, 1)
            for g in range(4):
                n = POOLW + 2 * g
                high(Item(n + 2), kt_of(n + 2) if n + 2 < MB else FT)
                act.wait_ge(tile_done, n + 2)
                for k in range(2):
                    act.wait_ge(pw_l, 2 * g)
                    nc.scalar.activation(wide[:, k, :], bank(k), ACT.Identity,
                                         scale=vcol[:, V_PS + 2 * g + k:V_PS + 2 * g + k + 1]).then_inc(p_free[k], 1)
                high(Item(n + 3), kt_of(n + 3) if n + 3 < MB else FT)
                for k in range(2):
                    act.wait_ge(pw_v, 2 * g + k + 1)
                    nc.scalar.activation(BH[:, 2 * g + k, :], wide[:, k, :], ACT.Copy).then_inc(pw_h, 1)
            with act.Fori(0, FT // 2) as i:
                for jj in range(2):
                    n = Item(MB + 2 * jj, i, 4)
                    high(n + 2, FT)
                    act.wait_ge(p_free[1], n.turns(2))
                    copy_gate(n)
                    high(n + 3, FT)
            act.wait_ge(mg2_ok, FT)
            for f in range(FT):
                nc.scalar.activation(AH[:, f, :], merged2[:, f, :], ACT.Copy).then_inc(mg_h, 1)
            act.dma_start(gain, final_gain_2.rearrange("(o n) -> o n", o=1).broadcast_to([P, D])).then_inc(gain_in, 16)
            for j in range(FT):
                if WO2 + j + 2 < END:
                    high(Item(WO2 + j + 2), FT)
                out_tile(WO2 + j, FT + j, mod2)
            squares(3)

        @block.vector
        def _(dve):
            steps = Steps(dve, dve_s)
            link, do = steps.link, steps.do
            tt, ts, stt = nc.vector.tensor_tensor, nc.vector.tensor_scalar, nc.vector.scalar_tensor_tensor

            def col(k):
                return pp[:, k, :]

            nc.vector.memset(vrow[:, :, :], 0.0).then_inc(rows_zero, 1)
            nc.vector.memset(hs[:, 0, :], 0.0).then_inc(rows_zero, 1)
            link(nc.vector.memset(sc[:, :, :, :], 0.0))
            dve.wait_ge(rows_in, 16 * 12)
            ts(vrow[32:48, 1, :].rearrange("p (g n) -> p g n", g=2), hs[32:48, 0, 0:2].unsqueeze(2).broadcast_to([ST, 2, N]),
               1.0, None, ALU.mult).then_inc(ld_rows, 1)
            dve.wait_ge(cols_t, 1)
            do(nc.vector.tensor_copy(vcol2[:, :], PS[:, M0, P:2 * P]))
            nc.vector.tensor_copy(vcol[:, :], PS[:, M0, 0:P]).then_inc(cols_ok, 1)
            dve.wait_ge(cols_ok, 1)
            steps.settle()
            dve.wait_ge(sig_c, 2)
            for k, v in enumerate((V_C1, V_C2)):
                tt(silc[:, k, :], silc[:, k, :], vcol[:, v:v + FT], ALU.mult).then_inc(silc_ok, 1)

            def scales(s, gains):
                dve.wait_ge(sumsq, 4 * s + 4)
                ts(stat[:, 1, :], stat[:, 0, :], 1.0 / D, EPS, ALU.mult, ALU.add).then_inc(ms_ok, 1)
                dve.wait_ge(root, s + 1)
                link(nc.vector.reciprocal(stat[:, 3, :], stat[:, 2, :]))
                if not gains:
                    for t in range(TT):
                        last = ts(diag[:, t, :], ident[:, :], stat[:, 3, t:t + 1], None, ALU.mult)
                        if t < TT - 1:
                            do(last)
                    last.then_inc(diag_ok, 1)
                else:
                    dve.wait_ge(gain_in, 16 * gains)
                    for t in range(TT):
                        stt(x_tok[:, t, :], x_tok[:, t, :], stat[:, 3, t:t + 1], gain, ALU.mult, ALU.mult)\
                            .then_inc(x1_ok, 1)

            def exponential(out_, in_):
                x_, k_, r_, p_, k1 = (col(n) for n in range(16, 21))
                link(ts(x_, in_, -174.0, 88.0, ALU.max, ALU.min))
                link(ts(k_, x_, 1.0 / math.log(2.0), 12582912.0, ALU.mult, ALU.add))
                link(ts(k_, k_, 12582912.0, None, ALU.subtract))
                link(stt(r_, k_, -0.693359375, x_, ALU.mult, ALU.add))
                link(stt(r_, k_, 2.12194440e-4, r_, ALU.mult, ALU.add))
                link(ts(p_, r_, 1.0 / math.factorial(8), None, ALU.mult))
                for n in range(7, 0, -1):
                    link(stt(p_, p_, 1.0 / math.factorial(n), r_, ALU.add, ALU.mult))
                link(ts(p_, p_, 1.0, None, ALU.add))
                link(ts(k1, k_, -126.0, None, ALU.max))
                link(tt(k_, k_, k1, ALU.subtract))
                for n, k in enumerate((k1, k_)):
                    link(ts(ppi[:, n, :], k, 127.0, None, ALU.add))
                    link(ts(ppi[:, n, :], ppi[:, n, :], 23, None, ALU.logical_shift_left))
                    link(tt(p_, p_, ppi[:, n, :].bitcast(fp32), ALU.mult))
                link(ts(out_, p_, 1.0, None, ALU.mult))

            ar, ai, ld = vcol[:, V_AR:V_AR + ST], vcol2[:, 0:ST], vcol2[:, 32:32 + ST]
            exponential(col(0), ld)
            link(tt(col(1), ar, col(0), ALU.mult))
            exponential(col(2), col(1))
            link(tt(col(3), ai, col(0), ALU.mult))
            C1 = 6.28125
            C2 = round((2 * math.pi - C1) * 2 ** 20) / 2 ** 20
            C3 = 2 * math.pi - C1 - C2
            link(ts(col(4), col(3), 1.0 / (2 * math.pi), 12582912.0, ALU.mult, ALU.add))
            link(ts(col(4), col(4), 12582912.0, None, ALU.subtract))
            for cc in (C1, C2, C3):
                link(stt(col(3), col(4), -cc, col(3), ALU.mult, ALU.add))
            link(ts(col(10), col(3), 3.1415925, -3.1415925, ALU.min, ALU.max))
            ts(col(11), col(10), 0.5, None, ALU.mult).then_inc(sin_in, 1)
            dve.wait_ge(sin_ok, 2)
            link(tt(col(7), col(13), col(13), ALU.mult))
            link(ts(col(7), col(7), -2.0, 1.0, ALU.mult, ALU.add))
            link(tt(col(5), col(2), col(7), ALU.mult))
            link(tt(col(6), col(2), col(12), ALU.mult))
            link(tt(col(16), ar, ar, ALU.mult))
            link(tt(col(17), ai, ai, ALU.mult))
            link(tt(col(16), col(16), col(17), ALU.add))
            link(nc.vector.reciprocal(col(16), col(16)))
            link(ts(col(17), col(5), 1.0, None, ALU.subtract))
            link(tt(col(18), col(17), ar, ALU.mult))
            link(tt(col(19), col(6), ai, ALU.mult))
            link(tt(col(18), col(18), col(19), ALU.add))
            link(tt(col(8), col(18), col(16), ALU.mult))
            link(tt(col(18), col(6), ar, ALU.mult))
            link(tt(col(19), col(17), ai, ALU.mult))
            link(tt(col(18), col(18), col(19), ALU.subtract))
            link(tt(col(9), col(18), col(16), ALU.mult))
            link(ts(col(13), col(6), -1.0, None, ALU.mult))
            link(ts(col(14), col(6), 1.0, None, ALU.mult))
            link(ts(col(15), col(6), -1.0, None, ALU.mult))
            link(ts(col(20), col(9), -1.0, None, ALU.mult))
            link(ts(col(21), col(9), 1.0, None, ALU.mult))

            nc.vector.memset(pp[:, 22, :], 0.0).then_inc(param_ok, 1)
            prod = [prod_c[:, k, :].rearrange("p (a b c) -> p a b c", a=2, b=ST) for k in range(2)]

            def wide_of(v, twice):
                v = v.unsqueeze(1) if twice else v
                return v.unsqueeze(3).broadcast_to([P, 2, ST, GP])

            def complex_times(out_, in_, swapped, re, im):
                link(tt(prod[0], in_, wide_of(re, True), ALU.mult))
                link(tt(prod[1], swapped, wide_of(im, False), ALU.mult))
                link(tt(out_, prod[0], prod[1], ALU.add))

            dve.wait_ge(c_t, 1)
            for part in range(2):
                for half in range(2):
                    v = PS[half * N:(half + 1) * N, Z0 + part, :].rearrange("p (t g c) -> p t g c", g=2, c=GP)
                    link(ts(E[half * N:(half + 1) * N, part, :, 0, :], v[:, :, half, :], 1.0 - 2.0 * part, None, ALU.mult))
            scales(0, 0)

            def add_w_mod(layer, third, rows_, k, first=False):
                sums = (mod_sum1, mod_sum2)[layer][:, third * D:(third + 1) * D]
                if first:
                    return ts(sums, rows_, silc[:, layer, k:k + 1], None, ALU.mult).then_inc(mod_used, 1)
                return stt(sums, rows_, silc[:, layer, k:k + 1] if layer == 0 else k, sums, ALU.mult, ALU.add)\
                    .then_inc(mod_used, 1)

            dve.wait_ge(silc_ok, 2)
            for m in range(NMOD):
                dve.wait_ge(mod1_in[m % 4], 16 * (m // 4 + 1))
                if m >= 3:
                    dve.wait_ge(mod_used, m - 2)
                add_w_mod(0, m % 3, mod_ring1[m % 4], m // 3, first=m < 3)

            def modulations(layer):
                m, base, g = ((mod1, V_BM1, V_G1), (mod2, V_BM2, V_G2))[layer]
                dve.wait_ge(mod_done, layer + 1)
                if layer:
                    tt(m[:, :], PS[:, M0, 256:256 + NMOD], vcol[:, base:base + NMOD], ALU.add).then_inc(mod2_read, 1)
                    dve.wait_ge(mod2_read, 1)
                else:
                    link(tt(m[:, :], PS[:, M0, 256:256 + NMOD], vcol[:, base:base + NMOD], ALU.add))
                stt(gs[:, layer, :], m[:, FT:2 * FT], 1.0, vcol[:, g:g + FT], ALU.add, ALU.mult).then_inc(mod_ok, 1)

            def low_features(layer, f):
                dve.wait_ge(hh, FT * layer + f + 1)
                tt(AL[:, f, :], tmpf[:, f % 2, :], AH[:, f, :].bitcast(fp32), ALU.subtract).then_inc(hl, 1)

            modulations(0)
            for f in range(FT):
                low_features(0, f)
            for k in range(L):
                before = E[:, :, :, k, :]
                complex_times(E[:, :, :, k + 1, :], before, before[:, ::-1, :, :], col(5), pp[:, 14:16, :])
            nc.vector.memset(pp[:, 22, :], 0.0).then_inc(e_ok, 1)
            dve.wait_ge(gb_ok, 1)
            nc.vector.memset(Dt[:, :, :, :], 0.0).then_inc(dt_zero, 1)
            def squared(re, im, re_out, im_out):
                link(tt(col(16), re, re, ALU.mult))
                link(tt(col(17), im, im, ALU.mult))
                link(tt(col(18), re, im, ALU.mult))
                link(tt(re_out, col(16), col(17), ALU.subtract))
                link(ts(im_out, col(18), 2.0, None, ALU.mult))

            squared(col(5), col(6), col(7), col(8))
            squared(col(7), col(8), col(7), col(8))
            squared(col(7), col(8), col(0), col(1))
            for k in range(3):
                squared(col(3 * k), col(3 * k + 1), col(3 * k + 3), col(3 * k + 4))
            for k in range(4):
                link(ts(col(3 * k + 2), col(3 * k + 1), -1.0, None, ALU.mult))

            dve.wait_ge(buc, 4)
            link(nc.vector.memset(score, 0.0))
            for q, c0, _, _ in SEGS:
                do(nc.vector.tensor_copy(score[:, c0 + q * P:c0 + (q + 1) * P], tri1[:, :]))
            steps.settle()
            link(nc.vector.memset(Hs[:, 0, :, :], 0.0))

            by_chunk = BU.rearrange("p t r c -> p r t c")
            states = Hs.rearrange("p c r t -> p r t c")

            def advance(k, out_, in_, add, n):
                re, im = pp[:, 3 * k, :], pp[:, 3 * k + 1:3 * k + 3, :]
                a, b = (tmpf[:, v, 0:2 * ST * n].rearrange("p (r t c) -> p r t c", r=2, t=ST) for v in range(2))
                wide_re = re.unsqueeze(1).unsqueeze(3).broadcast_to([P, 2, ST, n])
                do(tt(a, in_, wide_re, ALU.mult))
                link(tt(b[:, ::-1, :, :], in_, im.unsqueeze(3).broadcast_to([P, 2, ST, n]), ALU.mult))
                link(tt(a, a, b, ALU.add))
                link(tt(out_, a, add, ALU.add))

            LEVELS = 3
            for k in range(LEVELS):
                s_, pairs = 2 ** k, NCH // 2 ** (k + 1)
                for c0 in range(0, pairs, 16):
                    n = min(16, pairs)
                    left = by_chunk[:, :, :, 2 * s_ * c0 + s_ - 1:2 * s_ * (c0 + n) - s_:2 * s_]
                    right = by_chunk[:, :, :, 2 * s_ * c0 + 2 * s_ - 1:2 * s_ * (c0 + n):2 * s_]
                    advance(k, right, left, right, n)
            far = 2 ** LEVELS
            steps.begin_loop()
            with dve.Fori(0, NCH // far) as ch:
                steps.begin_trip(ch, 4)
                now = Hs[:, bass.ds(ch * far, 1), :, :].rearrange("p a r t -> p (a r) t")
                link(tt(sc[:, 0, :, :], now, col(3 * LEVELS).unsqueeze(1).broadcast_to([P, 2, ST]), ALU.mult))
                link(tt(sc[:, 1, ::-1, :], now, pp[:, 3 * LEVELS + 1:3 * LEVELS + 3, :], ALU.mult))
                link(tt(sc[:, 0, :, :], sc[:, 0, :, :], sc[:, 1, :, :], ALU.add))
                link(tt(Hs[:, bass.ds(ch * far + far, 1), :, :].rearrange("p a r t -> p (a r) t"), sc[:, 0, :, :],
                        BU[:, :, :, bass.ds(ch * far + far - 1, 1)].rearrange("p t r a -> p (r a) t"), ALU.add))
            steps.end_loop(NCH // far)
            for k in reversed(range(LEVELS)):
                s_, pairs = 2 ** k, NCH // 2 ** (k + 1)
                for c0 in range(0, pairs, 16):
                    n = min(16, pairs)
                    advance(k, states[:, :, :, 2 * s_ * c0 + s_:2 * s_ * (c0 + n):2 * s_],
                            states[:, :, :, 2 * s_ * c0:2 * s_ * (c0 + n) - s_:2 * s_],
                            by_chunk[:, :, :, 2 * s_ * c0 + s_ - 1:2 * s_ * (c0 + n):2 * s_], n)
            nc.vector.memset(pp[:, 22, :], 0.0).then_inc(scanned, 1)
            for h in range(H1):
                dve.wait_ge(wtok_ok, 1)
                dve.wait_ge(idx_r, h + 1)
                for q, c0, _, _ in SEGS:
                    if q:
                        seg = slice(c0, c0 + (q + 1) * P)
                        last = stt(score[:, seg], rl[:, seg], wtok[:, q, h:h + 1], score[:, seg], ALU.mult, ALU.add)
                        if q > 1:
                            do(last)
                last.then_inc(idx_w, 1)
            dve.wait_ge(idx_w, H1)
            for f in range(4):
                dve.wait_ge(y2t, f + 1)
                if f >= 2:
                    dve.wait_ge(yh, f - 1)
                    dve.wait_ge(ya_ok, f - 1)
                stt(tmpf[:, f % 2, :].rearrange("p (c i) -> p c i", i=L), xaT[:, f, :].rearrange("p (c i) -> p c i", i=L),
                    vcol[:, V_DS + f:V_DS + f + 1], bank(T0).rearrange("p (i c) -> p c i", i=L), ALU.mult, ALU.add)\
                    .then_inc(y_v, 1)
                dve.wait_ge(yh, f + 1)
                tt(BL[:, f, :], tmpf[:, f % 2, :], BH[:, f, :].bitcast(fp32), ALU.subtract).then_inc(ya_ok, 1)

            rounds = [(r, q, c0) for r in range(TOPK // 8) for q, c0, _, _ in SEGS if q]

            def take(r, q, c0):
                seg = slice(c0, c0 + (q + 1) * P)
                src = score[:, seg] if r == 0 else work[:, seg]
                link(nc.vector.max(m8[:, q - 1, :], src))
                link(nc.vector.match_replace(work[:, seg], m8[:, q - 1, :], src, TAKEN))

            for n in range(ZA, Q1):
                for k in range(6):
                    take(*rounds[6 * (n - ZA) + k])
                dve.wait_ge(gate_sig, n - ZA + 1)
                dst = sza[:, n - ZA, :] if n < ZB else szb[:, n - ZB, :]
                tt(dst, bank(n % 2), tmpf[:, n % 2, :], ALU.mult).then_inc(p_free[n % 2], 1)
            for q, c0, _, _ in SEGS:
                if q:
                    seg = slice(c0, c0 + (q + 1) * P)
                    last = ts(score[:, seg], work[:, seg], TAKEN / 2, NEG, ALU.is_gt, ALU.mult)
                    do(last)
            steps.settle()
            amask = score

            def masked(hd):
                k = 4 * (hd % 2)
                dve.wait_ge(z_ready, hd + 1)
                for q, c0, b, cb in SEGS:
                    w = (q + 1) * P
                    last = nc.vector.tensor_tensor_reduce(lg[hd % 2][:, c0:c0 + w], PS[:, b, cb:cb + w],
                                                          amask[:, c0:c0 + w], 1.0, -3e38, ALU.add, ALU.max,
                                                          hs[:, k, q:q + 1])
                    if q != 1:
                        do(last)
                last.then_inc(z_read, 1)
                dve.wait_ge(z_read, hd + 1)
                steps.settle()
                ts(hs[:, k + 1, :], hs[:, k, :], -DH ** -0.5, None, ALU.mult).then_inc(nmax_ok, 1)

            masked(0)
            for j in range(4):
                for h in range(2):
                    hd = 2 * j + h
                    if hd < H1 - 1:
                        masked(hd + 1)
                    if h == 1:
                        n = GLU_TILES[j]
                        dve.wait_ge(p_free[(n + 1) % 2], (n + 1) // 2 + 1)
                        dve.wait_ge(ya2_ok, j)
                        stt(glu_part, bank(n % 2), vcol[:, V_BG + j:V_BG + j + 1], glu_gate, ALU.add, ALU.mult)\
                            .then_inc(p_free[n % 2], 1)
                        dve.wait_ge(p_free[n % 2], n // 2 + 1)
                        tt(ya2[:, j, :], glu_part, sza[:, j, :], ALU.mult).then_inc(ya2_ok, 1)
                    dve.wait_ge(probs_ok, hd + 1)
                    link(nc.vector.reciprocal(hs[:, 4 * h + 3, :], hs[:, 4 * h + 2, :]))
                    dve.wait_ge(o_ready, hd + 1)
                    for q in range(TT):
                        last = ts(o_s[:, q, h * DH:(h + 1) * DH], PS[:, M0, q * DH:(q + 1) * DH],
                                  hs[:, 4 * h + 3, q:q + 1], None, ALU.mult)
                        if q < TT - 1:
                            do(last)
                    last.then_inc(o_copied, 1)
                dve.wait_ge(feats_t, j + 1)
                tt(tmpf[:, 0, :], bank(M0), szb[:, j, :], ALU.mult).then_inc(feats_c, 1)
                dve.wait_ge(feats_c, j + 1)
                link(ts(BH[:, 4 + j, :], tmpf[:, 0, :], 1.0, None, ALU.mult))
                tt(BL[:, 4 + j, :], tmpf[:, 0, :], BH[:, 4 + j, :].bitcast(fp32), ALU.subtract).then_inc(yb_l, 1)
                dve.wait_ge(yb_l, j + 1)
            link(nc.vector.memset(mod_sum2, 0.0))
            dve.wait_ge(ya2_h, 1)
            tt(BL[:, 0:4, :], ya2, BH[:, 0:4, :].bitcast(fp32), ALU.subtract).then_inc(ya2_l, 1)
            with dve.Fori(0, FT // 2) as i:
                for jj in range(2):
                    n = Item(GATE + 4 * jj, i, 8)
                    for third in range(3):
                        dve.wait_ge(mod_in[third], Item(16 * jj, i, 32).value(16))
                        dve.wait_ge(mod_used, Item(NMOD + 3 * jj + third, i, 6).value(-2))
                        add_w_mod(1, third, mod_ring[third],
                                  silc[:, 1, bass.ds(i * 2 + jj, 1)])
                    for k in range(2):
                        dve.wait_ge(p_free[k], (n + k).turns(2, add=1))
                        dve.wait_ge(tile_done, (n + 2 + k).value(1))
                        tt(parts_ab[:, k, :], bank(k), gates[:, k, :], ALU.mult).then_inc(p_free[k], 1)
                    for k in range(2):
                        dve.wait_ge(p_free[k], (n + 2 + k).turns(2, add=1))
                    tt(merged1[:, bass.ds(i * 2 + jj, 1), :].rearrange("p a b -> p (a b)"), parts_ab[:, 0, :],
                       parts_ab[:, 1, :], ALU.add).then_inc(mg_ok, 1)
                    dve.wait_ge(mg_ok, Item(jj, i, 2).value(1))

            def low_merged(layer, m):
                for f in range(FT):
                    dve.wait_ge(mg_h, FT * layer + f + 1)
                    tt(AL[:, f, :], m[:, f, :], AH[:, f, :].bitcast(fp32), ALU.subtract).then_inc(mg_l, 1)

            def add_outputs(layer):
                for j in range(FT):
                    dve.wait_ge(wo_t, FT * layer + j + 1)
                    v = x_tok[:, :, j * P:(j + 1) * P]
                    tt(v, v, bank(T0 + j % 2).rearrange("p (t c) -> p t c", t=TT), ALU.add).then_inc(wo_add, 1)

            low_merged(0, merged1)
            add_outputs(0)
            scales(1, 1)
            modulations(1)
            scales(2, 0)
            for f in range(FT):
                low_features(1, f)
            link(nc.vector.memset(zeros, 0.0))
            link(nc.vector.memset(Pw, 1.0))
            starts = {3: 0, 2: 513, 0: 898, 1: 1027}
            steps.begin_loop()
            with dve.Fori(0, FT // 2) as i:
                steps.begin_trip(i, 2 * (2 * 10 + 1))
                for jj in range(2):
                    n, pair = Item(L2 + 6 * jj, i, 12), Item(jj, i, 2)

                    def masked2(h):
                        hd = Item(H1 + 2 * jj + h, i, 4)
                        dve.wait_ge(z_ready, hd.value(1))
                        for q, _, b, cb in SEGS:
                            v = PS[:, b, cb + q * P:cb + (q + 1) * P]
                            last = tt(v, v, tri2[:, :], ALU.add)
                            if q != 1:
                                do(last)
                        last.then_inc(head2_m, 1)

                    def products(h):
                        hd = Item(H1 + 2 * jj + h, i, 4)
                        dve.wait_ge(z_gates, hd.value(1 - H1))
                        dve.wait_ge(probs_ok, hd.value())
                        for q, c0, _, _ in SEGS:
                            w, s0 = (q + 1) * P, starts[q]
                            do(nc.vector.tensor_tensor_scan(Pw[:, s0:s0 + w][:, ::-1], om[h][:, c0:c0 + w][:, ::-1],
                                                            zeros[:, 0:w], 1.0, ALU.mult, ALU.add))
                        steps.settle()
                        for q, c0, _, _ in SEGS:
                            w, s0 = (q + 1) * P, starts[q]
                            last = tt(beta[h][:, c0:c0 + w], beta[h][:, c0:c0 + w], Pw[:, s0 + 1:s0 + 1 + w], ALU.mult)
                            if q != 1:
                                do(last)
                        last.then_inc(probs_ok, 1)

                    def outputs(h):
                        hd = Item(H1 + 2 * jj + h, i, 4)
                        if h == 0:
                            dve.wait_ge(feats_t, pair.value(4))
                        dve.wait_ge(o_ready, hd.value(1))
                        nc.vector.tensor_copy(o2[:, :, h * DH:(h + 1) * DH],
                                              PS[:, M0, 0:TT * DH].rearrange("p (t c) -> p t c", t=TT))\
                            .then_inc(o_copied, 1)

                    masked2(0)
                    products(0)
                    dve.wait_ge(gate2_sig, Item(2 * jj, i, 4).value(1))
                    tt(sza2, bank(1), sza2, ALU.mult).then_inc(p_free[1], 1)
                    masked2(1)
                    products(1)
                    dve.wait_ge(tile_done, (n + 4).value(1))
                    ts(uT[:, bass.ds(i * 2 + jj, 1), :].rearrange("p a b -> p (a b)"), bank(0), 1.0, None, ALU.mult)\
                        .then_inc(p_free[0], 1)
                    outputs(0)
                    dve.wait_ge(gate2_sig, Item(2 * jj, i, 4).value(2))
                    tt(szb2[:, bass.ds(i * 2 + jj, 1), :].rearrange("p a b -> p (a b)"), bank(1), tmpf[:, 0, :],
                       ALU.mult).then_inc(p_free[1], 1)
                    outputs(1)
                    dve.wait_ge(feats_t, pair.value(5))
                    tt(tmpf[:, 1, :], bank(M0), sza2, ALU.mult).then_inc(feats_c, 1)
                    dve.wait_ge(feats_c, pair.value(5))
                    high = BH[:, bass.ds(i * 2 + jj, 1), :].rearrange("p a b -> p (a b)")
                    link(ts(high, tmpf[:, 1, :], 1.0, None, ALU.mult))
                    tt(BL[:, bass.ds(i * 2 + jj, 1), :].rearrange("p a b -> p (a b)"), tmpf[:, 1, :], high.bitcast(fp32),
                       ALU.subtract).then_inc(y2b_ok, 1)
            steps.end_loop(FT // 2)
            dve.wait_ge(tables, 2)
            steps.begin_loop()
            with dve.Fori(0, FT // 2) as i:
                steps.begin_trip(i, 14)
                for jj in range(2):
                    n = Item(MA + 2 * jj, i, 4)
                    dve.wait_ge(p_free[0], n.turns(2, add=1))
                    dve.wait_ge(tile_done, (n + 1).value(1))
                    tt(part_a[:, bass.ds(i * 2 + jj, 1), :].rearrange("p a b -> p (a b)"), bank(1), gates2, ALU.mult)\
                        .then_inc(p_free[1], 1)
                    u = uT[:, bass.ds(i * 2 + jj, 1), :].rearrange("p a b -> p (a b)")
                    link(ts(padded[:, 0, PAD:PAD + S], u, 1.0, None, ALU.mult))
                    for k in range(4):
                        src = padded[:, k % 2, :]
                        link(stt(padded[:, (k + 1) % 2, PAD:PAD + S], src[:, PAD - 2 ** k:PAD + S - 2 ** k],
                                 shifts[:, bass.ds(i, 1), k:k + 1].rearrange("p a b -> p (a b)"), src[:, PAD:PAD + S],
                                 ALU.mult, ALU.add))
                    total, few = padded[:, 0, PAD:PAD + S], WINDOWS[-1]
                    link(tt(total[:, 0:few], total[:, 0:few],
                            inv_count[:, bass.ds(i, 1), :].rearrange("p a b -> p (a b)"), ALU.mult))
                    link(tt(u[:, 0:few], total[:, 0:few], u[:, 0:few], ALU.subtract))
                    stt(u[:, few:S], total[:, few:S], inv_win[:, bass.ds(i, 1)], u[:, few:S], ALU.mult, ALU.subtract)\
                        .then_inc(d_ok, 1)
                    dve.wait_ge(d_ok, Item(jj, i, 2).value(1))
            steps.end_loop(FT // 2)
            for f in range(FT):
                dve.wait_ge(d_h, f + 1)
                tt(BL[:, f, :], uT[:, f, :], BH[:, f, :].bitcast(fp32), ALU.subtract).then_inc(d_l, 1)
            for f in range(FT):
                dve.wait_ge(p_free[f % 2], (POOLW + f) // 2 + 1)
                tt(wide[:, f % 2, :], wide[:, f % 2, :], szb2[:, f, :], ALU.mult).then_inc(pw_v, 1)
                dve.wait_ge(pw_h, f + 1)
                tt(BL[:, f, :], wide[:, f % 2, :], BH[:, f, :].bitcast(fp32), ALU.subtract).then_inc(pw_l, 1)
            with dve.Fori(0, FT // 2) as i:
                for jj in range(2):
                    n = Item(MB + 2 * jj, i, 4)
                    dve.wait_ge(p_free[0], n.turns(2, add=1))
                    dve.wait_ge(tile_done, (n + 1).value(1))
                    tt(prod2, bank(1), gates2, ALU.mult).then_inc(p_free[1], 1)
                    dve.wait_ge(p_free[1], (n + 1).turns(2, add=1))
                    tt(merged2[:, bass.ds(i * 2 + jj, 1), :].rearrange("p a b -> p (a b)"),
                       part_a[:, bass.ds(i * 2 + jj, 1), :].rearrange("p a b -> p (a b)"), prod2, ALU.add)\
                        .then_inc(mg2_ok, 1)
                    dve.wait_ge(mg2_ok, Item(jj, i, 2).value(1))
            low_merged(1, merged2)
            add_outputs(1)
            scales(3, 2)


_INS = ["x", "c", "norm_g", "w_mod", "b_mod", "w_in", "a_re", "a_im", "b_re", "b_im", "c_re", "c_im", "d_skip",
        "log_dt", "w_glu", "b_glu", "w_a_o", "w_b_o", "w_out", "final_g", "c_2", "norm_gain_2", "w_ada_2", "b_ada_2",
        "w_in_2", "pool_w_2", "pool_scale_2", "w_branch_a_2", "w_branch_b_2", "w_out_2", "final_gain_2"]
_OUTS = [((1, 512, 1024), "float32")]


def kernel(**inputs):
    import numpy as _np
    import concourse.bacc as _bacc
    from concourse import mybir as _mybir
    from concourse.bass_utils import run_bass_kernel_spmd as _run

    nc = _bacc.Bacc("TRN2", target_bir_lowering=False, num_devices=1)
    arrays, args = {}, []
    for name in _INS:
        a = _np.ascontiguousarray(inputs[name])
        arrays[f"in_{name}_dram"] = a
        args.append(nc.dram_tensor(f"in_{name}_dram", a.shape, _mybir.dt.from_np(a.dtype), kind="ExternalInput").ap())
    for i, (shape, dtype) in enumerate(_OUTS):
        dt = _mybir.dt.from_np(_np.dtype(dtype))
        args.append(nc.dram_tensor(f"out_{i}_dram", shape, dt, kind="ExternalOutput").ap())
    hybrid_two_layers(nc, *args)
    r = _run(nc, [arrays], core_ids=[0])
    got = tuple(r.results[0][f"out_{i}_dram"] for i in range(len(_OUTS)))
    return got[0]
```

```python
import concourse.bass as bass
from concourse import mybir
from contextlib import ExitStack
import math


class Item:

    def __init__(self, fixed, trip=None, per=0):
        self.fixed, self.trip, self.per = fixed, trip, per

    def __add__(self, k):
        return Item(self.fixed + k, self.trip, self.per)

    def value(self, add=0):
        return self.fixed + add + (0 if self.trip is None else self.trip * self.per)

    def turns(self, ring, times=1, add=0):
        return (self.fixed // ring) * times + add + (0 if self.trip is None else self.trip * (self.per // ring * times))

    def slot(self, ring):
        return self.fixed % ring


class Steps:

    def __init__(self, engine, sem):
        self.engine, self.sem, self.base, self.k = engine, sem, 0, 0

    def do(self, instruction):
        instruction.then_inc(self.sem, 1)
        self.k += 1

    def settle(self):
        self.engine.wait_ge(self.sem, self.base + self.k)

    def link(self, instruction):
        self.do(instruction)
        self.settle()

    def begin_loop(self):
        self.start, self.k = self.base + self.k, 0

    def begin_trip(self, trip, per):
        self.base, self.k, self.per = self.start + trip * per, 0, per

    def end_loop(self, trips):
        assert self.k == self.per, (self.k, self.per)
        self.base, self.k = self.start + trips * self.per, 0


def hybrid_two_layers(nc, x, c, norm_g, w_mod, b_mod, w_in, a_re, a_im, b_re, b_im, c_re, c_im, d_skip, log_dt,
                      w_glu, b_glu, w_a_o, w_b_o, w_out, final_g, c_2, norm_gain_2, w_ada_2, b_ada_2, w_in_2,
                      pool_w_2, pool_scale_2, w_branch_a_2, w_branch_b_2, w_out_2, final_gain_2, out):
    fp32, fp32r, i32 = mybir.dt.float32, mybir.dt.float32r, mybir.dt.int32
    ALU, ACT, AX = mybir.AluOpType, mybir.ActivationFunctionType, mybir.AxisListType

    P = 128
    S, D = x.shape[1], x.shape[2]
    TT, FT = S // P, D // P
    DH = 64
    G, N, GP = b_re.shape[1], b_re.shape[2], b_re.shape[3]
    ST = G * N // P
    L = P // GP
    NCH = S // L
    TOPK, H1, H2 = 128, 8, 16
    IDX_SCALE = float(H1 * DH) ** -0.5
    EPS = 1e-6
    NEG, TAKEN = -1e30, -3e38
    WINDOWS = (2, 4, 8, 16)

    XA, KI, KV, QI, ZA, ZB, Q1, GATE, WO = 0, 4, 5, 6, 10, 14, 18, 30, 62
    MOD_GATE_AFTER = {21: (0, 1), 23: (2,), 24: (3,), 26: (4,), 27: (5,), 29: (6, 7)}
    Q_TILES, GLU_TILES = (18, 19, 22, 25), (20, 23, 26, 28)
    L2, MA, POOLW, MB, WO2, END = 70, 118, 134, 142, 158, 166
    NMOD = 3 * FT
    C_XA, C_ZA, C_Q, C_K, C_ZB, C_QI, C_KI, C_GA, C_GB = 0, 512, 1024, 1536, 1664, 2176, 2688, 2760, 3784

    def by_rows(w):
        return w.rearrange("(k p) n -> p k n", p=P)

    w_mod1, w_mod2 = by_rows(w_mod[0]), by_rows(w_ada_2[0])
    w_in1, w_in2 = by_rows(w_in[0]), by_rows(w_in_2[0])
    glu_w, ao_w, bo_w, out_w1 = by_rows(w_glu[0]), by_rows(w_a_o[0]), by_rows(w_b_o[0]), by_rows(w_out[0])
    pa_w, pb_w, out_w2 = by_rows(w_branch_a_2[0]), by_rows(w_branch_b_2[0]), by_rows(w_out_2[0])
    pool_w = pool_w_2[0].rearrange("g (k p) n -> p g k n", p=P)
    x_v = x[0].rearrange("(t p) d -> p t d", p=P)
    out_v = out[0].rearrange("(t p) d -> p t d", p=P)

    def rows(v):
        return v.rearrange("(r c) -> r c", c=P)

    ctx = ExitStack()
    with ctx:
        def sb(name, shape, dt=fp32):
            return ctx.enter_context(nc.sbuf_tensor(name, shape, dt))

        def sem(name):
            return ctx.enter_context(nc.semaphore(name))

        x_tok = sb("x_tok", [P, TT, D])
        AH, AL = sb("AH", [P, FT, S], fp32r), sb("AL", [P, FT, S], fp32r)
        BH, BL = sb("BH", [P, FT, S], fp32r), sb("BL", [P, FT, S], fp32r)
        raw = sb("raw", [P, 2, FT * P])
        WH, WL = sb("WH", [P, 4, FT * P], fp32r), sb("WL", [P, 2, FT * P], fp32r)
        tmpf = sb("tmpf", [P, 2, S])
        vcol, vcol2 = sb("vcol", [P, P]), sb("vcol2", [P, P])
        ident = sb("ident", [P, P])
        tri1, tri2 = sb("tri1", [P, P]), sb("tri2", [P, P])
        silc, mod1, mod2, gs = sb("silc", [P, 2, FT]), sb("mod1", [P, NMOD]), sb("mod2", [P, NMOD]), sb("gs", [P, 2, FT])
        stat, diag = sb("stat", [P, 4, TT]), sb("diag", [P, TT, P])
        vtok, wtok, m8 = sb("vtok", [P, TT, DH]), sb("wtok", [P, TT, H1]), sb("m8", [P, 3, 8])
        hs = sb("hs", [P, 8, TT])
        ones = sb("ones", [P, 2])
        arena = sb("arena", [P, 21284])
        pp = sb("pp", [P, 24, ST])
        ppi = sb("ppi", [P, 2, ST], i32)
        sc = sb("sc", [P, 2, 2, ST])
        PS = ctx.enter_context(nc.psum_tensor("PS", [P, 8, 512], fp32))
        Z0, Z1, Z2, T0, T1, M0 = 2, 3, 4, 5, 6, 7

        def at(start, *dims, parts=P):
            n = 1
            for d in dims:
                n *= d
            v = arena[0:parts, start:start + n]
            if len(dims) == 1:
                return v
            names = "abcde"[:len(dims)]
            return v.rearrange(f"p ({' '.join(names)}) -> p {' '.join(names)}",
                               **{k: d for k, d in zip(names, dims)})

        E = at(0, 2, ST, L + 1, GP)
        Cin = at(4608, 2, 4, 2, N)
        vrow = at(6144, 2, P)
        Bin = at(5632, 2, ST, GP)
        prod_b, prod_c = at(6400, 2, 512), at(7424, 2, 512)
        mod_sum1 = at(12832, D)
        mod_row = at(13856, D, parts=1)
        Dt = at(4608, G, L, GP)
        mod_ring1 = [at(8704 + k * D, D) for k in range(4)]
        Kraw = at(8704, G, P, parts=GP)
        U = at(8704, G, NCH)
        X = at(10752, L, L, GP, parts=NCH)
        Hs = at(10752, NCH + 1, 2, ST)
        G1T = at(12832, ST, 2, P)
        GB = at(16928, 2, ST, L, GP)
        xaT = at(16928, 4, S)
        BU = at(18976, ST, 2, NCH)
        Y = at(18976, L, P, parts=NCH)
        kiw, kv, qi_s = at(12832, S), at(13344, S), at(13856, S)
        rl, score = at(14368, 1280), at(15648, 1280)
        work = at(20000, 1280)
        sza, szb = at(0, 4, S), at(2048, 4, S)
        ya2, glu_gate, glu_part = at(16928, 4, S), at(14368, S), at(14880, S)
        mod_sum_gate, mod_ring_gate = at(5376, D), (at(18976, D), at(20000, D))
        q_s, lg = at(6656, 2, S), (at(7680, 1280), at(4096, 1280))
        pT, o_s = at(8960, 10, P), at(10240, TT, P)
        gates, parts_ab = at(12832, 2, S), at(13856, 2, S)
        merged1 = at(16928, FT, S)
        gain = at(0, D)
        norm_parts, norm_scratch = at(D, 2, TT, FT), at(D + 2 * TT * FT, 2, TT, P)
        uT, szb2 = at(0, FT, S), at(4096, FT, S)
        q2, k2, v2, v2tok = at(8192, S), at(8704, S), at(9216, S), at(9728, TT, P)
        beta, om = (at(10240, 1280), at(16900, 1280)), (at(11520, 1280), at(18180, 1280))
        Pw = at(12800, 1284)
        wT, sza2, o2 = at(14084, 10, P), at(15364, S), at(15876, TT, P)
        zeros = at(16388, S)
        mod_sum2, mod_ring = at(6656, 3 * D), (at(10752, D), at(11776, D), at(9728, D))
        shifts, inv_win, inv_count = at(19460, 4, 4), at(19476, 4), at(19480, 4, 16)
        PAD = WINDOWS[-1] // 2
        part_a, merged2 = at(8192, FT, S), at(12288, FT, S)
        wide, gates2, prod2 = at(16384, 2, S), at(17408, S), at(17920, S)
        padded = at(18432 + 1112, 2, PAD + S)
        junk = tmpf[:, :, :].rearrange("p a b -> p (a b)")

        (consts, rows_zero, rows_in, x_in, b_in, c_in, gain_in, cols_t, c_t, gb_t, gb_c, k_t, k_c, silc_ok,
         mod_done, mod_ok, sumsq, root, diag_ok, ht, hv, hh, hl, h_ready, l_ready, tile_done, gb_ok, e_ok,
         dt_zero, dt_in) = [sem(n) for n in (
            "consts rows_zero rows_in x_in b_in c_in gain_in cols_t c_t gb_t gb_c k_t k_c silc_ok "
            "mod_done mod_ok sumsq root diag_ok ht hv hh hl h_ready l_ready tile_done gb_ok e_ok dt_zero "
            "dt_in").split()]
        raw_in = [sem(f"raw_in{i}") for i in range(2)]
        mod1_in = [sem(f"mod1_in{i}") for i in range(4)]
        sq = [sem("sq_x"), sem("sq_y")]
        mod_pe, mod_row_ok = sem("mod_pe"), sem("mod_row_ok")
        scaled, inv_ok, out_dve, out_act = [sem(n) for n in "scaled inv_ok out_dve out_act".split()]
        mod_gate_in = [sem(f"mod_gate_in{i}") for i in range(2)]
        mod_in = [sem(f"mod_in{i}") for i in range(3)]
        p_free = [sem(f"p_free{i}") for i in range(2)]
        dve_s, pool_s = sem("dve_step"), sem("pool_step")
        (xt, xc, ut, uc, but, buc, scanned, yt, yc, y2t, ya_ok, sin_in, sin_ok, cols_ok, gate_sig, param_ok,
         mod_used, tables) = [sem(n) for n in (
            "xt xc ut uc but buc scanned yt yc y2t ya_ok sin_in sin_ok cols_ok gate_sig param_ok mod_used "
            "tables").split()]
        (ki_dup, k_dup, ki_t, wtok_ok, v_t, vtok_ok, idx_s, idx_r, idx_w) = [sem(n) for n in (
            "ki_dup k_dup ki_t wtok_ok v_t vtok_ok idx_s idx_r idx_w").split()]
        (z_ready, z_read, nmax_ok, probs_ok, t_ready, t_copied, o_ready, o_copied, feats_t, feats_c, yb_l,
         ya2_ok, ya2_h, ya2_l, mg_ok, mg_h, mg_l, wo_t, wo_add, out_done, z_gates) = [sem(n) for n in (
            "z_ready z_read nmax_ok probs_ok t_ready t_copied o_ready o_copied feats_t feats_c yb_l "
            "ya2_ok ya2_h ya2_l mg_ok mg_h mg_l wo_t wo_add out_done z_gates").split()]
        (v2_t, v2_c, d_ok, d_h, d_l, pw_v, pw_h, pw_l, y2b_ok, head2_m, ld_rows, mod_sum_read, ms_ok, sig_c,
         y_v, gelu_ok, yh, gate2_sig, mg2_ok, mod_gate) = [sem(n) for n in (
            "v2_t v2_c d_ok d_h d_l pw_v pw_h pw_l y2b_ok head2_m ld_rows mod_sum_read ms_ok sig_c y_v "
            "gelu_ok yh gate2_sig mg2_ok mod_gate").split()]

        def bank(b):
            return PS[:, b, :]

        V_G1, V_BM1, V_C1, V_BG, V_DS, V_C2, V_G2, V_BM2, V_PS, V_AR = 0, 8, 32, 40, 48, 52, 60, 68, 92, 100
        SEGS = ((3, 0, Z0, 0), (2, 512, Z1, 0), (0, 896, Z1, 384), (1, 1024, Z2, 0))
        BLOCKS = [(q, c0 // P + kb, kb) for q, c0, _, _ in SEGS for kb in range(q + 1)]
        T_GROUPS = ((0, 4), (4, 8), (8, 10))

        def weight_source(n):
            def cols(w, col, kt=FT):
                return w[:, 0:kt, col:col + P], kt
            if n < KI:
                return cols(w_in1, C_XA + n * P)
            if n < QI:
                return cols(w_in1, (C_KI, C_K)[n - KI])
            if n < ZA:
                return cols(w_in1, C_QI + (n - QI) * P)
            if n < ZB:
                return cols(w_in1, C_ZA + (n - ZA) * P)
            if n < Q1:
                return cols(w_in1, C_ZB + (n - ZB) * P)
            if n in Q_TILES:
                return cols(w_in1, C_Q + Q_TILES.index(n) * P)
            if n < GATE:
                gate = n not in GLU_TILES
                return cols(glu_w, (GLU_TILES.index(n - gate) + 4 * gate) * P, 4)
            if n < L2:
                return cols(out_w1, (n - WO) * P)
            if n < MA:
                assert False
            if n < MB:
                g, h = (n - POOLW) // 2, (n - POOLW) % 2
                return pool_w[:, g, :, h * P:(h + 1) * P], 2
            return cols(out_w2, (n - WO2) * P)

        block = ctx.enter_context(nc.Block())

        @block.sync
        def _(sp):
            sp.wait_ge(rows_zero, 2)
            for base, v in ((V_G1, norm_g[0]), (V_BM1, b_mod[0]), (V_C1, c[0]), (V_BG, b_glu[0]), (V_DS, d_skip[0]),
                            (V_C2, c_2[0]), (V_G2, norm_gain_2[0]), (V_BM2, b_ada_2[0]), (V_PS, pool_scale_2[0])):
                n = v.shape[0] // P
                sp.dma_start(vrow[base:base + n, 0, :], rows(v)).then_inc(rows_in, 16)
            for part, v in ((0, a_re), (1, a_im)):
                first = V_AR if part == 0 else 0
                sp.dma_start(vrow[first:first + ST, part, :], v[0].rearrange("(t g) n -> t (g n)", g=2)).then_inc(rows_in, 16)
            sp.dma_start(hs[32:48, 0, 0:2], log_dt[0].rearrange("(t g) -> t g", g=2)).then_inc(rows_in, 16)
            for part, v in ((0, c_re), (1, c_im)):
                for dup in range(2):
                    sp.dma_start(Cin[:, part, :, dup, :],
                                 v[0].rearrange("(f g) p n -> (g p) f n", f=4)).then_inc(c_in, 16)
            for part, v in ((0, b_re), (1, b_im)):
                for half in range(2):
                    sp.dma_start(Bin[half * N:(half + 1) * N, part, :, :],
                                 v[0].rearrange("(t g) n p -> g n t p", g=2)[half]).then_inc(b_in, 16)
            sp.dma_start(x_tok[:, :, :], x_v).then_inc(x_in, 16)

            def load(r, src, kt):
                sp.dma_start(raw[:, r.slot(2), 0:kt * P].rearrange("p (k c) -> p k c", c=P), src)\
                    .then_inc(raw_in[r.slot(2)], 16)

            for m in range(2 * FT):
                if m >= 4:
                    sp.wait_ge((mod_used, mod_pe)[m % 2], m // 2 - 1)
                sp.dma_start(mod_ring1[m % 4], w_mod1[:, m // 2, (m % 2) * D:(m % 2 + 1) * D]).then_inc(mod1_in[m % 4], 16)
            for n in range(GATE):
                if n >= 2:
                    sp.wait_ge(l_ready, n - 1)
                load(Item(n), *weight_source(n))
                for k in MOD_GATE_AFTER.get(n, ()):
                    if k == 0:
                        sp.wait_ge(z_read, 1)
                    else:
                        sp.wait_ge(mod_used, FT + max(k - 1, 0))
                    sp.dma_start(mod_ring_gate[k % 2], w_mod1[:, k, 2 * D:3 * D]).then_inc(mod_gate_in[k % 2], 16)
            with sp.Fori(1, FT // 2 + 1) as i:
                for jj in range(2):
                    for k, (w, col, kt) in enumerate(((w_in1, C_GA, 8), (w_in1, C_GB, 8), (ao_w, 0, 4), (bo_w, 0, 4))):
                        n = Item(GATE + 4 * (jj - 2) + k, i, 8)
                        at_col = i * (2 * P) + (col + (jj - 2) * P)
                        sp.wait_ge(l_ready, n.value(-1))
                        load(n, w[:, 0:kt, bass.ds(at_col, P)], kt)
                        if k < 3:
                            m = Item(2 * FT + 3 * (jj - 2) + k, i, 6)
                            at_row = i * 2 + (jj - 2)
                            sp.wait_ge(mod_used, m.value(-2))
                            if k == 2:
                                sp.wait_ge(feats_c, 4)
                            sp.dma_start(mod_ring[k], w_mod2[:, bass.ds(at_row, 1), k * D:(k + 1) * D]
                                         .rearrange("p a n -> p (a n)")).then_inc(mod_in[k], 16)
            for n in range(WO, L2):
                sp.wait_ge(l_ready, n - 1)
                load(Item(n), *weight_source(n))
            with sp.Fori(1, FT // 2 + 1) as i:
                for jj in range(2):
                    for k, s in enumerate((0, 1, 2, 3, 4, 5)):
                        n = Item(L2 + 6 * (jj - 2) + k, i, 12)
                        at_col = i * (2 * P) + (s * D + (jj - 2) * P)
                        sp.wait_ge(l_ready, n.value(-1))
                        load(n, w_in2[:, :, bass.ds(at_col, P)], FT)
            with sp.Fori(1, FT // 2 + 1) as i:
                for jj in range(2):
                    for k, (w, col) in enumerate(((w_in2, 6 * D), (pa_w, 0))):
                        n = Item(MA + 2 * (jj - 2) + k, i, 4)
                        at_col = i * (2 * P) + (col + (jj - 2) * P)
                        sp.wait_ge(l_ready, n.value(-1))
                        load(n, w[:, :, bass.ds(at_col, P)], FT)
            for n in range(POOLW, MB):
                sp.wait_ge(l_ready, n - 1)
                load(Item(n), *weight_source(n))
            with sp.Fori(1, FT // 2 + 1) as i:
                for jj in range(2):
                    for k, (w, col) in enumerate(((w_in2, 7 * D), (pb_w, 0))):
                        n = Item(MB + 2 * (jj - 2) + k, i, 4)
                        at_col = i * (2 * P) + (col + (jj - 2) * P)
                        sp.wait_ge(l_ready, n.value(-1))
                        load(n, w[:, :, bass.ds(at_col, P)], FT)
            for n in range(WO2, END):
                sp.wait_ge(l_ready, n - 1)
                load(Item(n), *weight_source(n))
            for t in range(TT):
                sp.wait_ge((out_dve, out_act)[t % 2], t // 2 + 1)
                sp.dma_start(out_v[:, t, :], x_tok[:, t, :]).then_inc(out_done, 16)
            sp.wait_ge(out_done, 16 * TT)

        @block.gpsimd
        def _(pool):
            steps = Steps(pool, pool_s)
            steps.do(nc.gpsimd.memset(ident[:, :], 0.0))
            steps.do(nc.gpsimd.memset(tri1[:, :], 0.0))
            steps.do(nc.gpsimd.memset(tri2[:, :], 0.0))
            steps.do(nc.gpsimd.memset(wtok[:, :, :], 0.0))
            steps.do(nc.gpsimd.memset(ones[:, :], 1.0))
            steps.settle()
            steps.do(nc.gpsimd.affine_select(out=ident[:, :], in_=ident[:, :], compare_op=ALU.not_equal, fill=1.0, base=0,
                                             pattern=[[-1, P]], channel_multiplier=1))
            steps.do(nc.gpsimd.affine_select(out=tri1[:, :], in_=tri1[:, :], compare_op=ALU.is_ge, fill=NEG, base=0,
                                             pattern=[[-1, P]], channel_multiplier=1))
            steps.do(nc.gpsimd.affine_select(out=tri2[:, :], in_=tri2[:, :], compare_op=ALU.is_gt, fill=NEG, base=0,
                                             pattern=[[-1, P]], channel_multiplier=1))
            steps.settle()
            nc.gpsimd.memset(pp[:, 23, :], 0.0).then_inc(consts, 1)

            def low(n, kt):
                r, h = n.slot(2), n.slot(4)
                pool.wait_ge(h_ready, n.value(1))
                if n.trip is not None or n.fixed >= 2:
                    pool.wait_ge(tile_done, n.value(-1))
                nc.gpsimd.tensor_tensor(WL[:, r, 0:kt * P], raw[:, r, 0:kt * P], WH[:, h, 0:kt * P].bitcast(fp32),
                                        ALU.subtract).then_inc(l_ready, 1)

            pprod = [prod_b[:, k, :].rearrange("p (a b c) -> p a b c", a=2, b=ST) for k in range(2)]

            def times(out_, in_, re, im):
                for o, i, v in ((pprod[0], in_, re.unsqueeze(1)), (pprod[1], in_[:, ::-1, :, :], im)):
                    steps.do(nc.gpsimd.tensor_tensor(o, i, v.unsqueeze(3).broadcast_to([P, 2, ST, GP]), ALU.mult))
                steps.settle()
                steps.link(nc.gpsimd.tensor_tensor(out_, pprod[0], pprod[1], ALU.add))

            pool.wait_ge(param_ok, 1)
            pool.wait_ge(b_in, 64)
            times(GB[:, :, :, 0, :], Bin, pp[:, 8, :], pp[:, 20:22, :])
            for d in range(1, L):
                times(GB[:, :, :, d, :], GB[:, :, :, d - 1, :], pp[:, 5, :], pp[:, 13:15, :])
            nc.gpsimd.memset(pp[:, 23, :], 0.0).then_inc(gb_ok, 1)

            for n in range(GATE):
                low(Item(n), weight_source(n)[1])
            with pool.Fori(0, FT // 2) as i:
                for k in range(8):
                    low(Item(GATE + k, i, 8), 8 if k % 4 < 2 else 4)
            for n in range(WO, L2):
                low(Item(n), FT)
            pool.wait_ge(mg_l, FT)
            steps.do(nc.gpsimd.memset(shifts, 1.0))
            for g, win in enumerate(WINDOWS):
                steps.do(nc.gpsimd.memset(inv_win[:, g:g + 1], 1.0 / win))
                steps.do(nc.gpsimd.memset(inv_count[:, g, :], 1.0 / win))
            steps.settle()
            for g in range(3):
                steps.do(nc.gpsimd.memset(shifts[:, g, g + 1:4], 0.0))
            for t in range(WINDOWS[-1] - 1):
                first = next(g for g, win in enumerate(WINDOWS) if win > t)
                steps.do(nc.gpsimd.memset(inv_count[:, first:4, t], 1.0 / (t + 1)))
            steps.settle()
            for k in range(2):
                nc.gpsimd.memset(padded[:, k, 0:PAD], 0.0).then_inc(tables, 1)
            with pool.Fori(0, FT // 2) as i:
                for k in range(12):
                    low(Item(L2 + k, i, 12), FT)
            with pool.Fori(0, FT // 2) as i:
                for k in range(4):
                    low(Item(MA + k, i, 4), FT)
            for n in range(POOLW, MB):
                low(Item(n), 2)
            with pool.Fori(0, FT // 2) as i:
                for k in range(4):
                    low(Item(MB + k, i, 4), FT)
            for n in range(WO2, END):
                low(Item(n), FT)

        @block.tensor
        def _(pe):
            def product(n, hi, lo, kt, k0=0, ready=None):
                s = n.slot(2)
                pe.wait_ge(l_ready, n.value(1))
                if n.trip is not None or n.fixed >= 2:
                    pe.wait_ge(p_free[s], n.turns(2))
                for k in range(kt):
                    if ready:
                        pe.wait_ge(ready[0], ready[1] + k)
                    w_hi, w_lo = WH[:, n.slot(4), k * P:(k + 1) * P], WL[:, s, k * P:(k + 1) * P]
                    nc.tensor.matmul(bank(s), w_hi, hi[:, k0 + k, :], start=(k == 0), stop=False)
                    nc.tensor.matmul(bank(s), w_hi, lo[:, k0 + k, :], start=False, stop=False)
                    last = nc.tensor.matmul(bank(s), w_lo, hi[:, k0 + k, :], start=False, stop=(k == kt - 1))
                last.then_inc(tile_done, 1)

            def taken_out(n):
                pe.wait_ge(p_free[n.slot(2)], n.turns(2, add=1))

            def modulation(used, sums, b, col, n):
                pe.wait_ge(mod_used, used)
                for m in range(n):
                    last = nc.tensor.matmul(PS[:, b, col + m:col + m + 1], sums[:, m * P:(m + 1) * P], ones[:, 0:1],
                                            start=True, stop=True)
                last.then_inc(mod_done, 1)

            def normed_features(layer, between=None):
                pe.wait_ge(diag_ok, layer + 1)
                for f in range(FT):
                    if f >= 2:
                        pe.wait_ge(hv, FT * layer + f - 1)
                    for t in range(TT):
                        last = nc.tensor.matmul(PS[:, Z0 + f % 2, t * P:(t + 1) * P], x_tok[:, t, f * P:(f + 1) * P],
                                                diag[:, t, :], start=True, stop=True)
                    last.then_inc(ht, 1)
                    if between:
                        between(f)

            def attend_scores(hd, base_q, base_k, h):
                for q, _, b, c in SEGS:
                    last = nc.tensor.matmul(PS[:, b, c:c + (q + 1) * P], base_q[h * DH:(h + 1) * DH, q * P:(q + 1) * P],
                                            base_k[h * DH:(h + 1) * DH, 0:(q + 1) * P], start=True, stop=True)
                last.then_inc(z_ready, 1)

            def attend_values(hd, h, probs, wt, vals):
                pe.wait_ge(probs_ok, hd.value(1))
                for g, (lo, hi) in enumerate(T_GROUPS):
                    if hd.trip is not None or 3 * hd.fixed + g >= 2:
                        pe.wait_ge(t_copied, Item(3 * hd.fixed + g, hd.trip, 3 * hd.per).value(-1))
                    b = T0 + (3 * hd.fixed + g) % 2
                    for n in range(lo, hi):
                        last = nc.tensor.transpose(PS[:, b, (n - lo) * P:(n - lo + 1) * P], probs[:, n * P:(n + 1) * P],
                                                   ident[:, :])
                    last.then_inc(t_ready, 1)
                if hd.trip is not None or hd.fixed >= 1:
                    pe.wait_ge(o_copied, hd.value())
                pe.wait_ge(t_copied, Item(3 * hd.fixed, hd.trip, 3 * hd.per).value(3))
                for q, n, kb in BLOCKS:
                    last = nc.tensor.matmul(PS[:, M0, q * DH:(q + 1) * DH], wt[:, n, :], vals(kb),
                                            start=(kb == 0), stop=(kb == q))
                last.then_inc(o_ready, 1)

            def pair_features(hd, o):
                pe.wait_ge(o_copied, hd.value(1))
                for t in range(TT):
                    last = nc.tensor.transpose(PS[:, M0, t * P:(t + 1) * P], o[:, t, :], ident[:, :])
                last.then_inc(feats_t, 1)

            def out_transposes(j):
                n = Item((WO if j < FT else WO2 - FT) + j)
                taken_out(n)
                if j >= 2:
                    pe.wait_ge(wo_add, j - 1)
                for t in range(TT):
                    last = nc.tensor.transpose(PS[:, T0 + j % 2, t * P:(t + 1) * P], tmpf[:, j % 2, t * P:(t + 1) * P],
                                               ident[:, :])
                last.then_inc(wo_t, 1)

            pe.wait_ge(consts, 1)
            pe.wait_ge(rows_in, 16 * 11)
            pe.wait_ge(ld_rows, 1)
            for part in range(2):
                last = nc.tensor.transpose(PS[:, M0, part * P:(part + 1) * P], vrow[:, part, :], ident[:, :])
            last.then_inc(cols_t, 1)
            pe.wait_ge(c_in, 64)
            for part in range(2):
                for f in range(4):
                    last = nc.tensor.transpose(PS[:, Z0 + part, f * P:(f + 1) * P],
                                               Cin[:, part, f, :, :].rearrange("p a b -> p (a b)"), ident[:, :])
            last.then_inc(c_t, 1)
            pe.wait_ge(cols_ok, 1)
            pe.wait_ge(silc_ok, 2)
            for k in range(FT):
                m = 2 * k + 1
                pe.wait_ge(mod1_in[m % 4], 16 * (m // 4 + 1))
                for half in range(2):
                    last = nc.tensor.matmul(PS[0:1, T0 + half, :], silc[:, 0, k:k + 1],
                                            mod_ring1[m % 4][:, half * 512:(half + 1) * 512],
                                            start=(k == 0), stop=(k == FT - 1))
                last.then_inc(mod_pe, 1)
            pe.wait_ge(mod_row_ok, 1)
            for m in range(FT):
                nc.tensor.matmul(PS[:, M0, 256 + FT + m:257 + FT + m], mod_row[:, m * P:(m + 1) * P], ones[0:1, 0:1],
                                 start=True, stop=True)
            modulation(FT, mod_sum1, M0, 256, FT)

            def scan_matrices(r):
                if r == 0:
                    pe.wait_ge(gb_ok, 1)
                    pe.wait_ge(e_ok, 1)
                if r >= 2:
                    pe.wait_ge(gb_c, r - 1)
                for k in range(4):
                    t, ri = 2 * r + k // 2, k % 2
                    last = nc.tensor.transpose(PS[:, r % 2, k * P:(k + 1) * P],
                                               GB[:, ri, t, :, :].rearrange("p a b -> p (a b)"), ident[:, :])
                last.then_inc(gb_t, 1)
                if r >= 2:
                    pe.wait_ge(k_c, r - 1)
                for k in range(4):
                    t, half = 4 * (r // 2) + k, (r % 2) * N
                    for ri in range(2):
                        last = nc.tensor.matmul(PS[0:GP, T0 + r % 2, k * P:(k + 1) * P], GB[half:half + N, ri, t, 0, :],
                                                E[half:half + N, ri, t, 0:L, :].rearrange("p a b -> p (a b)"),
                                                start=(ri == 0), stop=(ri == 1))
                last.then_inc(k_t, 1)

            normed_features(0, scan_matrices)
            pe.wait_ge(hl, FT)
            pe.wait_ge(gb_c, FT)
            for n in (XA, XA + 1):
                product(Item(n), AH, AL, FT)

            product(Item(XA + 2), AH, AL, FT)
            for f in range(4):
                if f:
                    product(Item(XA + 2 + f), AH, AL, FT)
                taken_out(Item(XA + f))
                if f >= 1:
                    pe.wait_ge(uc, f)
                    pe.wait_ge(buc, f)
                steps_of = xaT[:, f, :].rearrange("p (c j) -> p c j", j=L)
                for s in range(L):
                    last = nc.tensor.transpose(PS[0:NCH, T1 + s // 4, (s % 4) * P:(s % 4 + 1) * P],
                                               steps_of[:, :, L - 1 - s], ident[:, :])
                last.then_inc(xt, 1)
                pe.wait_ge(xc, 2 * f + 2)
                for g in range(L):
                    last = nc.tensor.transpose(PS[:, T1, g * NCH:(g + 1) * NCH], X[:, g, :, :].rearrange("p a b -> p (a b)"),
                                               ident[0:NCH, 0:NCH])
                last.then_inc(ut, 1)
                pe.wait_ge(uc, f + 1)
                for t in range(4):
                    for ri in range(2):
                        for half in range(2):
                            last = nc.tensor.matmul(
                                PS[half * N:(half + 1) * N, M0, (2 * t + ri) * NCH:(2 * t + ri + 1) * NCH],
                                G1T[:, 4 * f + t, ri, half * N:(half + 1) * N], U[:, 2 * (4 * f + t) + half, :],
                                start=True, stop=True)
                last.then_inc(but, 1)
            pe.wait_ge(buc, 4)
            taken_out(Item(KI))
            for t in range(TT):
                last = nc.tensor.transpose(PS[:, M0, t * P:(t + 1) * P], kiw[:, t * P:(t + 1) * P], ident[:, :])
            last.then_inc(ki_t, 1)
            product(Item(QI), AH, AL, FT)
            taken_out(Item(KV))
            pe.wait_ge(wtok_ok, 1)
            for t in range(TT):
                last = nc.tensor.transpose(PS[:, M0, t * P:(t + 1) * P], kv[:, t * P:(t + 1) * P], ident[:, :])
            last.then_inc(v_t, 1)
            pe.wait_ge(ki_dup, 16)
            for j in range(4):
                if j:
                    product(Item(QI + j), AH, AL, FT)
                taken_out(Item(QI + j))
                for h in range(2):
                    if 2 * j + h:
                        pe.wait_ge(idx_r, 2 * j + h)
                    for q, _, b, c in SEGS:
                        if q:
                            last = nc.tensor.matmul(PS[:, b, c:c + (q + 1) * P],
                                                    qi_s[h * DH:(h + 1) * DH, q * P:(q + 1) * P],
                                                    kiw[h * DH:(h + 1) * DH, 0:(q + 1) * P], start=True, stop=True)
                    last.then_inc(idx_s, 1)
            pe.wait_ge(scanned, 1)
            pe.wait_ge(dt_in, 128)
            pe.wait_ge(idx_r, H1)
            for f in range(4):
                for half4 in range(2):
                    if f:
                        pe.wait_ge(yc, 2 * f + half4 - 1)
                    for k in range(4):
                        t, half = 4 * f + k, half4 * N
                        g = 2 * t + half4
                        o = PS[0:NCH, Z0 + half4, k * P:(k + 1) * P]
                        for ri in range(2):
                            nc.tensor.matmul(o, Hs[half:half + N, 0:NCH, ri, t],
                                             E[half:half + N, ri, t, 1:L + 1, :].rearrange("p a b -> p (a b)"),
                                             start=(ri == 0), stop=False)
                        last = nc.tensor.matmul(o, U[:, g, :], Dt[:, g, :, :].rearrange("p a b -> p (a b)"),
                                                start=False, stop=True)
                    last.then_inc(yt, 1)
                pe.wait_ge(yc, 2 * f + 2)
                if f:
                    pe.wait_ge(y_v, f)
                for s in range(L):
                    last = nc.tensor.transpose(PS[:, T0, s * NCH:(s + 1) * NCH], Y[:, s, :], ident[0:NCH, 0:NCH])
                last.then_inc(y2t, 1)
            for n in range(ZA, Q1):
                product(Item(n), AH, AL, FT)
            product(Item(Q1), AH, AL, FT)
            pe.wait_ge(ya_ok, 4)
            pe.wait_ge(k_dup, 16)
            taken_out(Item(Q1))
            attend_scores(Item(0), q_s[:, 0, :], kv, 0)
            for j in range(4):
                for h in range(2):
                    hd = Item(2 * j + h)
                    if hd.fixed < H1 - 1:
                        if h == 1:
                            taken_out(Item(Q_TILES[j + 1]))
                        pe.wait_ge(z_read, hd.fixed + 1)
                        attend_scores(hd + 1, q_s[:, (hd.fixed + 1) // 2 % 2, :], kv, 1 - h)
                    if h == 1:
                        product(Item(GLU_TILES[j]), BH, BL, 4)
                        product(Item(GLU_TILES[j] + 1), BH, BL, 4)
                    elif j < 3:
                        product(Item(Q_TILES[j + 1]), AH, AL, FT)
                    pe.wait_ge(feats_c, j)
                    attend_values(hd, h, lg[h], pT, lambda kb: vtok[:, kb, :])
                pair_features(Item(2 * j + 1), o_s)
            pe.wait_ge(z_read, H1)
            modulation(2 * FT, mod_sum_gate, Z0, 0, FT)
            with pe.Fori(0, FT // 2) as i:
                for jj in range(2):
                    n = Item(GATE + 4 * jj, i, 8)
                    product(n, AH, AL, FT)
                    product(n + 1, AH, AL, FT)
                    pe.wait_ge(ya2_l, 1)
                    product(n + 2, BH, BL, 4)
                    pe.wait_ge(yb_l, 4)
                    product(n + 3, BH, BL, 4, k0=4)
            for j in range(FT + 1):
                if j < FT:
                    product(Item(WO + j), AH, AL, FT, ready=(mg_l, 1) if j == 0 else None)
                if j == 1:
                    pe.wait_ge(feats_c, 4)
                    modulation(2 * FT + NMOD, mod_sum2, M0, 256, NMOD)
                if j:
                    out_transposes(j - 1)

            pe.wait_ge(mod_sum_read, 2)
            normed_features(1)
            pe.wait_ge(hl, 2 * FT)
            with pe.Fori(0, FT // 2) as i:
                for jj in range(2):
                    n = Item(L2 + 6 * jj, i, 12)
                    pair = Item(jj, i, 2)
                    first, second = Item(H1 + 2 * jj, i, 4), Item(H1 + 2 * jj + 1, i, 4)
                    for k in range(3):
                        product(n + k, AH, AL, FT)
                    taken_out(n)
                    taken_out(n + 1)
                    attend_scores(first, q2, k2, 0)
                    taken_out(n + 2)
                    pe.wait_ge(feats_c, pair.value(4))
                    for t in range(TT):
                        last = nc.tensor.transpose(PS[:, M0, t * P:(t + 1) * P], v2[:, t * P:(t + 1) * P], ident[:, :])
                    last.then_inc(v2_t, 1)
                    product(n + 3, AH, AL, FT)
                    pe.wait_ge(z_gates, first.value(1 - H1))
                    attend_scores(second, q2, k2, 1)
                    product(n + 4, AH, AL, FT)
                    pe.wait_ge(v2_c, pair.value(1))
                    attend_values(first, 0, beta[0], wT, lambda kb: v2tok[:, kb, 0:DH])
                    product(n + 5, AH, AL, FT)
                    attend_values(second, 1, beta[1], wT, lambda kb: v2tok[:, kb, DH:P])
                    pair_features(second, o2)
            pe.wait_ge(y2b_ok, FT)
            with pe.Fori(0, FT // 2) as i:
                for jj in range(2):
                    n = Item(MA + 2 * jj, i, 4)
                    product(n, AH, AL, FT)
                    product(n + 1, BH, BL, FT)
            for n in range(POOLW, MB):
                pe.wait_ge(d_l, 2 * ((n - POOLW) // 2) + 2)
                product(Item(n), BH, BL, 2, k0=2 * ((n - POOLW) // 2))
            with pe.Fori(0, FT // 2) as i:
                for jj in range(2):
                    n = Item(MB + 2 * jj, i, 4)
                    product(n, AH, AL, FT)
                    pe.wait_ge(pw_l, FT)
                    product(n + 1, BH, BL, FT)
            for j in range(FT + 1):
                if j < FT:
                    product(Item(WO2 + j), AH, AL, FT, ready=(mg_l, FT + 1) if j == 0 else None)
                if j:
                    out_transposes(FT + j - 1)

        @block.scalar
        def _(act):
            def high(n, kt):
                r, h = n.slot(2), n.slot(4)
                act.wait_ge(raw_in[r], n.turns(2, 16, 16))
                if n.trip is not None or n.fixed >= 4:
                    act.wait_ge(tile_done, n.value(-3))
                nc.scalar.activation(WH[:, h, 0:kt * P], raw[:, r, 0:kt * P], ACT.Copy).then_inc(h_ready, 1)

            def kt_of(n):
                return weight_source(n)[1]

            def squares():
                for t in range(TT):
                    if t:
                        act.wait_ge(sumsq, t)
                    nc.scalar.activation(junk, x_tok[:, t, :], ACT.Square,
                                         accum_out=stat[:, 0, t:t + 1]).then_inc(sumsq, 1)
                act.wait_ge(ms_ok, 1)
                nc.scalar.activation(stat[:, 2, :], stat[:, 1, :], ACT.Sqrt).then_inc(root, 1)

            def squares_of(layer, part, j):
                act.wait_ge((wo_add, scaled)[part], FT * layer + j + 1)
                if FT * layer + j:
                    act.wait_ge(sq[part], TT * (FT * layer * (1 - part) + j))
                for t in range(TT):
                    nc.scalar.activation(norm_scratch[:, part, t, :], x_tok[:, t, j * P:(j + 1) * P], ACT.Square,
                                         accum_out=norm_parts[:, part, t, j:j + 1]).then_inc(sq[part], 1)

            def features(layer, between=None):
                act.wait_ge(mod_ok, layer + 1)
                m = (mod1, mod2)[layer]
                for f in range(FT):
                    n = FT * layer + f
                    act.wait_ge(ht, n + 1)
                    if f >= 2:
                        act.wait_ge(hl, n - 1)
                    nc.scalar.activation(tmpf[:, f % 2, :], bank(Z0 + f % 2), ACT.Identity, bias=m[:, f:f + 1],
                                         scale=gs[:, layer, f:f + 1]).then_inc(hv, 1)
                    act.wait_ge(hv, n + 1)
                    nc.scalar.activation(AH[:, f, :], tmpf[:, f % 2, :], ACT.Copy).then_inc(hh, 1)
                    if between:
                        between(f)

            def copy_out(n, dst):
                act.wait_ge(tile_done, n.value(1))
                nc.scalar.activation(dst, bank(n.slot(2)), ACT.Copy).then_inc(p_free[n.slot(2)], 1)

            def copy_gate(n):
                act.wait_ge(tile_done, n.value(1))
                nc.scalar.activation(gates2, bank(0), ACT.Sigmoid).then_inc(p_free[0], 1)

            def t_copies(hd, wt):
                act.wait_ge(o_ready, hd.value())
                for g, (lo, hi) in enumerate(T_GROUPS):
                    tg = Item(3 * hd.fixed + g, hd.trip, 3 * hd.per)
                    act.wait_ge(t_ready, tg.value(1))
                    nc.scalar.activation(wt[:, lo:hi, :].rearrange("p a b -> p (a b)"),
                                         PS[:, T0 + tg.slot(2), 0:(hi - lo) * P], ACT.Copy).then_inc(t_copied, 1)

            act.wait_ge(cols_ok, 1)
            for k, v in enumerate((V_C1, V_C2)):
                nc.scalar.activation(silc[:, k, :], vcol[:, v:v + FT], ACT.Sigmoid).then_inc(sig_c, 1)
            act.wait_ge(sin_in, 1)
            for k in range(2):
                nc.scalar.activation(pp[:, 12 + k, :], pp[:, 10 + k, :], ACT.Sin).then_inc(sin_ok, 1)
            act.wait_ge(x_in, 16)
            squares()
            high(Item(0), FT)
            high(Item(1), FT)
            act.wait_ge(mod_pe, FT)
            nc.scalar.activation(mod_row, PS[0:1, T0:T1 + 1, :].rearrange("p a b -> p (a b)"), ACT.Copy)\
                .then_inc(mod_row_ok, 1)
            act.wait_ge(mod_done, 1)

            def copy_scan_matrices(r):
                act.wait_ge(gb_t, r + 1)
                nc.scalar.activation(G1T[:, 2 * r:2 * r + 2, :, :].rearrange("p a b c -> p (a b c)"), bank(r % 2),
                                     ACT.Copy).then_inc(gb_c, 1)
                act.wait_ge(k_t, r + 1)
                nc.scalar.activation(Kraw[:, 8 * (r // 2) + r % 2:8 * (r // 2) + 8:2, :],
                                     PS[0:GP, T0 + r % 2, :].rearrange("p (a b) -> p a b", b=P), ACT.Copy).then_inc(k_c, 1)

            features(0, copy_scan_matrices)
            act.wait_ge(k_c, 8)
            act.wait_ge(dt_zero, 1)
            act.wait_ge(k_c, 8)
            act.wait_ge(dt_zero, 1)
            for j in range(L):
                d = L - 1 - j
                act.dma_start(Dt[d * GP:(d + 1) * GP, :, j:L, :].rearrange("p a b c -> p a (b c)"),
                              Kraw[:, :, 0:(L - j) * GP]).then_inc(dt_in, 16)
            high(Item(2), FT)
            high(Item(3), FT)
            copy_out(Item(XA), xaT[:, XA, :])
            copy_out(Item(XA + 1), xaT[:, XA + 1, :])
            copy_out(Item(XA + 2), xaT[:, XA + 2, :])
            high(Item(XA + 4), FT)
            act.wait_ge(dt_in, 16 * L)
            for f in range(4):
                if f == 1:
                    copy_out(Item(XA + 3), xaT[:, 3, :])
                if f:
                    high(Item(XA + 4 + f), FT)
                act.wait_ge(xt, f + 1)
                if f:
                    act.wait_ge(ut, f)
                for k in range(2):
                    nc.scalar.activation(X[:, :, 4 * k:4 * k + 4, :],
                                         PS[0:NCH, T1 + k, :].rearrange("p (s g c) -> p g s c", s=4, g=L), ACT.Copy).then_inc(xc, 1)
                act.wait_ge(ut, f + 1)
                nc.scalar.activation(U[:, L * f:L * f + L, :].rearrange("p a b -> p (a b)"), bank(T1),
                                     ACT.Copy).then_inc(uc, 1)
                act.wait_ge(but, f + 1)
                nc.scalar.activation(BU[:, 4 * f:4 * f + 4, :, :].rearrange("p a b c -> p (a b c)"), bank(M0),
                                     ACT.Copy).then_inc(buc, 1)
            copy_out(Item(KI), kiw)
            copy_out(Item(KV), kv)
            act.wait_ge(ki_t, 1)
            nc.scalar.activation(wtok[:, :, :], bank(M0).rearrange("p (t f) -> p t f", f=P)[:, :, DH:DH + H1],
                                 ACT.Copy).then_inc(wtok_ok, 1)
            act.dma_start(kiw[DH:P, :], kiw[0:DH, :]).then_inc(ki_dup, 16)
            act.wait_ge(v_t, 1)
            nc.scalar.activation(vtok[:, :, :], bank(M0).rearrange("p (t f) -> p t f", f=P)[:, :, DH:P],
                                 ACT.Copy).then_inc(vtok_ok, 1)
            act.dma_start(kv[DH:P, :], kv[0:DH, :]).then_inc(k_dup, 16)
            for j in range(4):
                if j:
                    act.wait_ge(idx_s, 2 * j)
                copy_out(Item(QI + j), qi_s)
                high(Item(QI + j + 2), FT)
                for h in range(2 * j, 2 * j + 2):
                    act.wait_ge(idx_s, h + 1)
                    if h:
                        act.wait_ge(idx_w, h)
                    for q, c0, b, c in SEGS:
                        if q:
                            last = nc.scalar.activation(rl[:, c0:c0 + (q + 1) * P], PS[:, b, c:c + (q + 1) * P],
                                                        ACT.Relu, scale=IDX_SCALE)
                    last.then_inc(idx_r, 1)
            for f in range(4):
                for half4 in range(2):
                    act.wait_ge(yt, 2 * f + half4 + 1)
                    if f and half4 == 0:
                        act.wait_ge(y2t, f)
                    nc.scalar.activation(
                        Y.rearrange("p i (k h c) -> p i k h c", h=2, c=GP)[:, :, :, half4, :],
                        PS[0:NCH, Z0 + half4, :].rearrange("p (g i c) -> p i g c", g=4, i=L), ACT.Copy).then_inc(yc, 1)
                act.wait_ge(y_v, f + 1)
                nc.scalar.activation(tmpf[:, f % 2, :], tmpf[:, f % 2, :], ACT.Gelu_apprx_tanh).then_inc(gelu_ok, 1)
                act.wait_ge(gelu_ok, f + 1)
                nc.scalar.activation(BH[:, f, :], tmpf[:, f % 2, :], ACT.Copy).then_inc(yh, 1)
            for n in range(ZA, Q1):
                act.wait_ge(tile_done, n + 1)
                if n >= ZA + 2:
                    act.wait_ge(p_free[n % 2], n // 2)
                act.wait_ge(ya_ok, 4)
                nc.scalar.activation(tmpf[:, n % 2, :], bank(n % 2), ACT.Sigmoid).then_inc(gate_sig, 1)
                high(Item(n + 2), FT)
            copy_out(Item(Q1), q_s[:, 0, :])
            high(Item(Q1 + 2), FT)

            def exps(hd):
                act.wait_ge(nmax_ok, hd + 1)
                for q, c0, _, _ in SEGS:
                    seg = lg[hd % 2][:, c0:c0 + (q + 1) * P]
                    last = nc.scalar.activation(seg, seg, ACT.Exp, bias=hs[:, 4 * (hd % 2) + 1, q:q + 1], scale=DH ** -0.5,
                                                accum_out=hs[:, 4 * (hd % 2) + 2, q:q + 1])
                last.then_inc(probs_ok, 1)

            exps(0)
            for hd in range(H1):
                j = hd // 2
                tiles = ((GLU_TILES[j], GLU_TILES[j] + 1) if hd % 2 else Q_TILES[j + 1:j + 2])
                if tiles:
                    high(Item(tiles[0] + 2), kt_of(tiles[0] + 2) if tiles[0] + 2 < GATE else FT)
                if hd < H1 - 1:
                    exps(hd + 1)
                if hd % 2:
                    n = GLU_TILES[j]
                    act.wait_ge(tile_done, n + 2)
                    act.wait_ge(ya2_ok, j)
                    nc.scalar.activation(glu_gate, bank((n + 1) % 2), ACT.Sigmoid,
                                         bias=vcol[:, V_BG + 4 + j:V_BG + 5 + j]).then_inc(p_free[(n + 1) % 2], 1)
                    high(Item(n + 3), kt_of(n + 3) if n + 3 < GATE else FT)
                elif j < 3:
                    copy_out(Item(Q_TILES[j + 1]), q_s[:, (j + 1) % 2, :])
                t_copies(Item(hd), pT)
            act.wait_ge(ya2_ok, 4)
            nc.scalar.activation(BH[:, 0:4, :].rearrange("p a b -> p (a b)"), ya2.rearrange("p a b -> p (a b)"),
                                 ACT.Copy).then_inc(ya2_h, 1)
            with act.Fori(0, FT // 2) as i:
                for jj in range(2):
                    n = Item(GATE + 4 * jj, i, 8)
                    for k in range(4):
                        high(n + k + 2, (4, 4, 8, 8)[k])
                        if k < 2:
                            act.wait_ge(p_free[k], (n + k).turns(2))
                            act.wait_ge(tile_done, (n + k).value(1))
                            nc.scalar.activation(gates[:, k, :], bank(k), ACT.Sigmoid).then_inc(p_free[k], 1)
            act.wait_ge(mg_ok, FT)
            for f in range(FT):
                nc.scalar.activation(AH[:, f, :], merged1[:, f, :], ACT.Copy).then_inc(mg_h, 1)
            act.dma_start(gain, final_g.rearrange("(o n) -> o n", o=1).broadcast_to([P, D])).then_inc(gain_in, 16)

            def out_tile(n, j, m):
                act.wait_ge(tile_done, n + 1)
                if j % FT >= 2:
                    act.wait_ge(wo_t, j - 1)
                nc.scalar.activation(tmpf[:, j % 2, :], bank(n % 2), ACT.Identity,
                                     scale=m[:, 16 + j % FT:17 + j % FT]).then_inc(p_free[n % 2], 1)

            act.wait_ge(mg_l, FT)
            act.wait_ge(mod_gate, 1)
            for j in range(FT):
                high(Item(WO + j + 2), FT)
                out_tile(WO + j, j, mod1)
                if j >= 1:
                    squares_of(0, 0, j - 1)
                if j >= 2:
                    squares_of(0, 1, j - 2)
            squares_of(0, 0, FT - 1)
            squares_of(0, 1, FT - 2)
            squares_of(0, 1, FT - 1)
            act.wait_ge(ms_ok, 2)
            nc.scalar.activation(stat[:, 2:4, :], stat[:, 0:2, :], ACT.Sqrt).then_inc(root, 1)
            features(1)
            with act.Fori(0, FT // 2) as i:
                for jj in range(2):
                    n, pair = Item(L2 + 6 * jj, i, 12), Item(jj, i, 2)

                    def gates_of(h):
                        hd = Item(H1 + 2 * jj + h, i, 4)
                        act.wait_ge(head2_m, hd.value(1 - H1))
                        act.wait_ge(t_ready, Item(3 * hd.fixed - 3, i, 12).value())
                        act.wait_ge(probs_ok, hd.value(-1))
                        for dst, scale in ((beta[h], DH ** -0.5), (om[h], -DH ** -0.5)):
                            for col, b, width in ((0, Z0, 512), (512, Z1, 512), (1024, Z2, 256)):
                                last = nc.scalar.activation(dst[:, col:col + width], PS[:, b, 0:width], ACT.Sigmoid,
                                                            scale=scale)
                        last.then_inc(z_gates, 1)

                    high(n + 2, FT)
                    act.wait_ge(z_ready, Item(H1 + 2 * jj, i, 4).value())
                    copy_out(n, q2)
                    high(n + 3, FT)
                    copy_out(n + 1, k2)
                    high(n + 4, FT)
                    copy_out(n + 2, v2)
                    gates_of(0)
                    act.wait_ge(v2_t, pair.value(1))
                    act.wait_ge(o_ready, Item(H1 + 2 * jj, i, 4).value())
                    nc.scalar.activation(v2tok.rearrange("p a b -> p (a b)"), bank(M0), ACT.Copy).then_inc(v2_c, 1)
                    high(n + 5, FT)
                    act.wait_ge(tile_done, (n + 3).value(1))
                    nc.scalar.activation(sza2, bank(1), ACT.Sigmoid).then_inc(gate2_sig, 1)
                    gates_of(1)
                    t_copies(Item(H1 + 2 * jj, i, 4), wT)
                    high(n + 6, FT)
                    act.wait_ge(tile_done, (n + 5).value(1))
                    nc.scalar.activation(tmpf[:, 0, :], bank(1), ACT.Sigmoid).then_inc(gate2_sig, 1)
                    t_copies(Item(H1 + 2 * jj + 1, i, 4), wT)
                    high(n + 7, FT)
            with act.Fori(0, FT // 2) as i:
                for jj in range(2):
                    n = Item(MA + 2 * jj, i, 4)
                    high(n + 2, FT)
                    act.wait_ge(p_free[1], n.turns(2))
                    copy_gate(n)
                    high(n + 3, FT)
            act.wait_ge(d_ok, FT)
            act.wait_ge(tile_done, POOLW)
            for f in range(FT):
                nc.scalar.activation(BH[:, f, :], uT[:, f, :], ACT.Copy).then_inc(d_h, 1)
            for g in range(4):
                n = POOLW + 2 * g
                high(Item(n + 2), kt_of(n + 2) if n + 2 < MB else FT)
                act.wait_ge(tile_done, n + 2)
                for k in range(2):
                    act.wait_ge(pw_l, 2 * g)
                    nc.scalar.activation(wide[:, k, :], bank(k), ACT.Identity,
                                         scale=vcol[:, V_PS + 2 * g + k:V_PS + 2 * g + k + 1]).then_inc(p_free[k], 1)
                high(Item(n + 3), kt_of(n + 3) if n + 3 < MB else FT)
                for k in range(2):
                    act.wait_ge(pw_v, 2 * g + k + 1)
                    nc.scalar.activation(BH[:, 2 * g + k, :], wide[:, k, :], ACT.Copy).then_inc(pw_h, 1)
            with act.Fori(0, FT // 2) as i:
                for jj in range(2):
                    n = Item(MB + 2 * jj, i, 4)
                    high(n + 2, FT)
                    act.wait_ge(p_free[1], n.turns(2))
                    copy_gate(n)
                    high(n + 3, FT)
            act.wait_ge(mg2_ok, FT)
            for f in range(FT):
                nc.scalar.activation(AH[:, f, :], merged2[:, f, :], ACT.Copy).then_inc(mg_h, 1)
            act.dma_start(gain, final_gain_2.rearrange("(o n) -> o n", o=1).broadcast_to([P, D])).then_inc(gain_in, 16)
            for j in range(FT):
                if WO2 + j + 2 < END:
                    high(Item(WO2 + j + 2), FT)
                out_tile(WO2 + j, FT + j, mod2)
                if j >= 1:
                    squares_of(1, 0, j - 1)
            squares_of(1, 0, FT - 1)
            act.wait_ge(ms_ok, 3)
            nc.scalar.activation(stat[:, 2, :], stat[:, 0, :], ACT.Sqrt).then_inc(root, 1)
            act.wait_ge(inv_ok, 1)
            act.wait_ge(scaled, 2 * FT)
            for t in range(1, TT, 2):
                nc.scalar.activation(x_tok[:, t, :], x_tok[:, t, :], ACT.Identity, scale=stat[:, 0, t:t + 1])\
                    .then_inc(out_act, 1)

        @block.vector
        def _(dve):
            steps = Steps(dve, dve_s)
            link, do = steps.link, steps.do
            tt, ts, stt = nc.vector.tensor_tensor, nc.vector.tensor_scalar, nc.vector.scalar_tensor_tensor

            def col(k):
                return pp[:, k, :]

            nc.vector.memset(vrow[:, :, :], 0.0).then_inc(rows_zero, 1)
            nc.vector.memset(hs[:, 0, :], 0.0).then_inc(rows_zero, 1)
            link(nc.vector.memset(sc[:, :, :, :], 0.0))
            dve.wait_ge(rows_in, 16 * 12)
            ts(vrow[32:48, 1, :].rearrange("p (g n) -> p g n", g=2), hs[32:48, 0, 0:2].unsqueeze(2).broadcast_to([ST, 2, N]),
               1.0, None, ALU.mult).then_inc(ld_rows, 1)
            dve.wait_ge(cols_t, 1)
            do(nc.vector.tensor_copy(vcol2[:, :], PS[:, M0, P:2 * P]))
            nc.vector.tensor_copy(vcol[:, :], PS[:, M0, 0:P]).then_inc(cols_ok, 1)
            dve.wait_ge(cols_ok, 1)
            steps.settle()
            dve.wait_ge(sig_c, 2)
            for k, v in enumerate((V_C1, V_C2)):
                tt(silc[:, k, :], silc[:, k, :], vcol[:, v:v + FT], ALU.mult).then_inc(silc_ok, 1)

            def diagonals(inv):
                for t in range(TT):
                    last = ts(diag[:, t, :], ident[:, :], inv[:, t:t + 1], None, ALU.mult)
                    if t < TT - 1:
                        do(last)
                last.then_inc(diag_ok, 1)

            def exponential(out_, in_):
                x_, k_, r_, p_, k1 = (col(n) for n in range(16, 21))
                link(ts(x_, in_, -174.0, 88.0, ALU.max, ALU.min))
                link(ts(k_, x_, 1.0 / math.log(2.0), 12582912.0, ALU.mult, ALU.add))
                link(ts(k_, k_, 12582912.0, None, ALU.subtract))
                link(stt(r_, k_, -0.693359375, x_, ALU.mult, ALU.add))
                link(stt(r_, k_, 2.12194440e-4, r_, ALU.mult, ALU.add))
                link(ts(p_, r_, 1.0 / math.factorial(8), None, ALU.mult))
                for n in range(7, 0, -1):
                    link(stt(p_, p_, 1.0 / math.factorial(n), r_, ALU.add, ALU.mult))
                link(ts(p_, p_, 1.0, None, ALU.add))
                link(ts(k1, k_, -126.0, None, ALU.max))
                link(tt(k_, k_, k1, ALU.subtract))
                for n, k in enumerate((k1, k_)):
                    link(ts(ppi[:, n, :], k, 127.0, None, ALU.add))
                    link(ts(ppi[:, n, :], ppi[:, n, :], 23, None, ALU.logical_shift_left))
                    link(tt(p_, p_, ppi[:, n, :].bitcast(fp32), ALU.mult))
                link(ts(out_, p_, 1.0, None, ALU.mult))

            ar, ai, ld = vcol[:, V_AR:V_AR + ST], vcol2[:, 0:ST], vcol2[:, 32:32 + ST]
            exponential(col(0), ld)
            link(tt(col(1), ar, col(0), ALU.mult))
            exponential(col(2), col(1))
            link(tt(col(3), ai, col(0), ALU.mult))
            C1 = 6.28125
            C2 = round((2 * math.pi - C1) * 2 ** 20) / 2 ** 20
            C3 = 2 * math.pi - C1 - C2
            link(ts(col(4), col(3), 1.0 / (2 * math.pi), 12582912.0, ALU.mult, ALU.add))
            link(ts(col(4), col(4), 12582912.0, None, ALU.subtract))
            for cc in (C1, C2, C3):
                link(stt(col(3), col(4), -cc, col(3), ALU.mult, ALU.add))
            link(ts(col(10), col(3), 3.1415925, -3.1415925, ALU.min, ALU.max))
            ts(col(11), col(10), 0.5, None, ALU.mult).then_inc(sin_in, 1)
            dve.wait_ge(sin_ok, 2)
            link(tt(col(7), col(13), col(13), ALU.mult))
            link(ts(col(7), col(7), -2.0, 1.0, ALU.mult, ALU.add))
            link(tt(col(5), col(2), col(7), ALU.mult))
            link(tt(col(6), col(2), col(12), ALU.mult))
            link(tt(col(16), ar, ar, ALU.mult))
            link(tt(col(17), ai, ai, ALU.mult))
            link(tt(col(16), col(16), col(17), ALU.add))
            link(nc.vector.reciprocal(col(16), col(16)))
            link(ts(col(17), col(5), 1.0, None, ALU.subtract))
            link(tt(col(18), col(17), ar, ALU.mult))
            link(tt(col(19), col(6), ai, ALU.mult))
            link(tt(col(18), col(18), col(19), ALU.add))
            link(tt(col(8), col(18), col(16), ALU.mult))
            link(tt(col(18), col(6), ar, ALU.mult))
            link(tt(col(19), col(17), ai, ALU.mult))
            link(tt(col(18), col(18), col(19), ALU.subtract))
            link(tt(col(9), col(18), col(16), ALU.mult))
            link(ts(col(13), col(6), -1.0, None, ALU.mult))
            link(ts(col(14), col(6), 1.0, None, ALU.mult))
            link(ts(col(15), col(6), -1.0, None, ALU.mult))
            link(ts(col(20), col(9), -1.0, None, ALU.mult))
            link(ts(col(21), col(9), 1.0, None, ALU.mult))

            nc.vector.memset(pp[:, 22, :], 0.0).then_inc(param_ok, 1)
            prod = [prod_c[:, k, :].rearrange("p (a b c) -> p a b c", a=2, b=ST) for k in range(2)]

            def wide_of(v, twice):
                v = v.unsqueeze(1) if twice else v
                return v.unsqueeze(3).broadcast_to([P, 2, ST, GP])

            def complex_times(out_, in_, swapped, re, im):
                link(tt(prod[0], in_, wide_of(re, True), ALU.mult))
                link(tt(prod[1], swapped, wide_of(im, False), ALU.mult))
                link(tt(out_, prod[0], prod[1], ALU.add))

            dve.wait_ge(c_t, 1)
            for part in range(2):
                for half in range(2):
                    v = PS[half * N:(half + 1) * N, Z0 + part, :].rearrange("p (t g c) -> p t g c", g=2, c=GP)
                    link(ts(E[half * N:(half + 1) * N, part, :, 0, :], v[:, :, half, :], 1.0 - 2.0 * part, None, ALU.mult))
            dve.wait_ge(sumsq, TT)
            ts(stat[:, 1, :], stat[:, 0, :], 1.0 / D, EPS, ALU.mult, ALU.add).then_inc(ms_ok, 1)
            dve.wait_ge(root, 1)
            link(nc.vector.reciprocal(stat[:, 3, :], stat[:, 2, :]))
            diagonals(stat[:, 3, :])

            def add_w_mod(layer, sums, rows_, silu_c, first=False):
                if first:
                    ts(sums, rows_, silu_c, None, ALU.mult).then_inc(mod_used, 1)
                else:
                    stt(sums, rows_, silu_c, sums, ALU.mult, ALU.add).then_inc(mod_used, 1)

            dve.wait_ge(silc_ok, 2)
            for k in range(FT):
                m = 2 * k
                dve.wait_ge(mod1_in[m % 4], 16 * (m // 4 + 1))
                if k:
                    dve.wait_ge(mod_used, k)
                add_w_mod(0, mod_sum1, mod_ring1[m % 4], silc[:, 0, k:k + 1], k == 0)
                before = E[:, :, :, k, :]
                complex_times(E[:, :, :, k + 1, :], before, before[:, ::-1, :, :], col(5), pp[:, 14:16, :])

            def modulations(layer):
                m, base, g, n = ((mod1, V_BM1, V_G1, 2 * FT), (mod2, V_BM2, V_G2, NMOD))[layer]
                dve.wait_ge(mod_done, 2 * layer + 1)
                tt(m[:, 0:n], PS[:, M0, 256:256 + n], vcol[:, base:base + n], ALU.add).then_inc(mod_sum_read, 1)
                dve.wait_ge(mod_sum_read, layer + 1)
                stt(gs[:, layer, :], m[:, FT:2 * FT], 1.0, vcol[:, g:g + FT], ALU.add, ALU.mult).then_inc(mod_ok, 1)

            def low_features(layer, f):
                dve.wait_ge(hh, FT * layer + f + 1)
                tt(AL[:, f, :], tmpf[:, f % 2, :], AH[:, f, :].bitcast(fp32), ALU.subtract).then_inc(hl, 1)

            nc.vector.memset(pp[:, 22, :], 0.0).then_inc(e_ok, 1)
            modulations(0)
            for f in range(FT):
                low_features(0, f)
            dve.wait_ge(gb_ok, 1)
            nc.vector.memset(Dt[:, :, :, :], 0.0).then_inc(dt_zero, 1)
            def squared(re, im, re_out, im_out):
                link(tt(col(16), re, re, ALU.mult))
                link(tt(col(17), im, im, ALU.mult))
                link(tt(col(18), re, im, ALU.mult))
                link(tt(re_out, col(16), col(17), ALU.subtract))
                link(ts(im_out, col(18), 2.0, None, ALU.mult))

            squared(col(5), col(6), col(7), col(8))
            squared(col(7), col(8), col(7), col(8))
            squared(col(7), col(8), col(0), col(1))
            for k in range(3):
                squared(col(3 * k), col(3 * k + 1), col(3 * k + 3), col(3 * k + 4))
            for k in range(4):
                link(ts(col(3 * k + 2), col(3 * k + 1), -1.0, None, ALU.mult))

            by_chunk = BU.rearrange("p t r c -> p r t c")
            states = Hs.rearrange("p c r t -> p r t c")

            def advance(k, out_, in_, add, t0, tiles, n):
                re, im = pp[:, 3 * k, t0:t0 + tiles], pp[:, 3 * k + 1:3 * k + 3, t0:t0 + tiles]
                a, b = (tmpf[:, v, 0:2 * tiles * n].rearrange("p (r t c) -> p r t c", r=2, t=tiles) for v in range(2))
                do(tt(a, in_, re.unsqueeze(1).unsqueeze(3).broadcast_to([P, 2, tiles, n]), ALU.mult))
                link(tt(b[:, ::-1, :, :], in_, im.unsqueeze(3).broadcast_to([P, 2, tiles, n]), ALU.mult))
                link(tt(a, a, b, ALU.add))
                link(tt(out_, a, add, ALU.add))

            LEVELS = 3
            for f in range(4):
                dve.wait_ge(buc, f + 1)
                for k in range(LEVELS):
                    s_, n = 2 ** k, NCH // 2 ** (k + 1)
                    those = by_chunk[:, :, 4 * f:4 * f + 4, :]
                    advance(k, those[:, :, :, 2 * s_ - 1:NCH:2 * s_], those[:, :, :, s_ - 1:NCH - s_:2 * s_],
                            those[:, :, :, 2 * s_ - 1:NCH:2 * s_], 4 * f, 4, n)
            link(nc.vector.memset(score, 0.0))
            for q, c0, _, _ in SEGS:
                do(nc.vector.tensor_copy(score[:, c0 + q * P:c0 + (q + 1) * P], tri1[:, :]))
            steps.settle()
            link(nc.vector.memset(Hs[:, 0, :, :], 0.0))

            def accumulate(h):
                dve.wait_ge(wtok_ok, 1)
                dve.wait_ge(idx_r, h + 1)
                if h:
                    dve.wait_ge(idx_w, h)
                for q, c0, _, _ in SEGS:
                    if q:
                        seg = slice(c0, c0 + (q + 1) * P)
                        last = stt(score[:, seg], rl[:, seg], wtok[:, q, h:h + 1], score[:, seg], ALU.mult, ALU.add)
                        if q > 1:
                            do(last)
                last.then_inc(idx_w, 1)

            far = 2 ** LEVELS
            steps.begin_loop()
            with dve.Fori(0, NCH // far) as ch:
                steps.begin_trip(ch, 4)
                now = Hs[:, bass.ds(ch * far, 1), :, :].rearrange("p a r t -> p (a r) t")
                link(tt(sc[:, 0, :, :], now, col(3 * LEVELS).unsqueeze(1).broadcast_to([P, 2, ST]), ALU.mult))
                link(tt(sc[:, 1, ::-1, :], now, pp[:, 3 * LEVELS + 1:3 * LEVELS + 3, :], ALU.mult))
                link(tt(sc[:, 0, :, :], sc[:, 0, :, :], sc[:, 1, :, :], ALU.add))
                link(tt(Hs[:, bass.ds(ch * far + far, 1), :, :].rearrange("p a r t -> p (a r) t"), sc[:, 0, :, :],
                        BU[:, :, :, bass.ds(ch * far + far - 1, 1)].rearrange("p t r a -> p (r a) t"), ALU.add))
            steps.end_loop(NCH // far)
            for k in reversed(range(LEVELS)):
                accumulate(LEVELS - 1 - k)
                s_, pairs = 2 ** k, NCH // 2 ** (k + 1)
                for c0 in range(0, pairs, 16):
                    n = min(16, pairs)
                    advance(k, states[:, :, :, 2 * s_ * c0 + s_:2 * s_ * (c0 + n):2 * s_],
                            states[:, :, :, 2 * s_ * c0:2 * s_ * (c0 + n) - s_:2 * s_],
                            by_chunk[:, :, :, 2 * s_ * c0 + s_ - 1:2 * s_ * (c0 + n):2 * s_], 0, ST, n)
            nc.vector.memset(pp[:, 22, :], 0.0).then_inc(scanned, 1)
            for h in range(LEVELS, H1):
                accumulate(h)
            dve.wait_ge(idx_w, H1)

            rounds = [(r, q, c0) for r in range(TOPK // 8) for q, c0, _, _ in SEGS if q]

            def take(r, q, c0):
                seg = slice(c0, c0 + (q + 1) * P)
                src = score[:, seg] if r == 0 else work[:, seg]
                link(nc.vector.max(m8[:, q - 1, :], src))
                link(nc.vector.match_replace(work[:, seg], m8[:, q - 1, :], src, TAKEN))

            for f in range(4):
                for k in range(6):
                    take(*rounds[6 * f + k])
                dve.wait_ge(y2t, f + 1)
                if f >= 2:
                    dve.wait_ge(yh, f - 1)
                    dve.wait_ge(ya_ok, f - 1)
                stt(tmpf[:, f % 2, :].rearrange("p (c i) -> p c i", i=L), xaT[:, f, :].rearrange("p (c i) -> p c i", i=L),
                    vcol[:, V_DS + f:V_DS + f + 1], bank(T0).rearrange("p (i c) -> p c i", i=L), ALU.mult, ALU.add)\
                    .then_inc(y_v, 1)
                dve.wait_ge(yh, f + 1)
                tt(BL[:, f, :], tmpf[:, f % 2, :], BH[:, f, :].bitcast(fp32), ALU.subtract).then_inc(ya_ok, 1)

            for n in range(ZA, Q1):
                for k in range(3):
                    take(*rounds[24 + 3 * (n - ZA) + k])
                dve.wait_ge(gate_sig, n - ZA + 1)
                dst = sza[:, n - ZA, :] if n < ZB else szb[:, n - ZB, :]
                tt(dst, bank(n % 2), tmpf[:, n % 2, :], ALU.mult).then_inc(p_free[n % 2], 1)
            for q, c0, _, _ in SEGS:
                if q:
                    seg = slice(c0, c0 + (q + 1) * P)
                    last = ts(score[:, seg], work[:, seg], TAKEN / 2, NEG, ALU.is_gt, ALU.mult)
                    do(last)
            steps.settle()
            amask = score

            def masked(hd):
                k = 4 * (hd % 2)
                dve.wait_ge(z_ready, hd + 1)
                for q, c0, b, cb in SEGS:
                    w = (q + 1) * P
                    last = nc.vector.tensor_tensor_reduce(lg[hd % 2][:, c0:c0 + w], PS[:, b, cb:cb + w],
                                                          amask[:, c0:c0 + w], 1.0, -3e38, ALU.add, ALU.max,
                                                          hs[:, k, q:q + 1])
                    if q != 1:
                        do(last)
                last.then_inc(z_read, 1)
                dve.wait_ge(z_read, hd + 1)
                steps.settle()
                ts(hs[:, k + 1, :], hs[:, k, :], -DH ** -0.5, None, ALU.mult).then_inc(nmax_ok, 1)

            masked(0)
            for j in range(4):
                for h in range(2):
                    hd = 2 * j + h
                    if hd < H1 - 1:
                        masked(hd + 1)
                    if h == 1:
                        n = GLU_TILES[j]
                        dve.wait_ge(p_free[(n + 1) % 2], (n + 1) // 2 + 1)
                        dve.wait_ge(ya2_ok, j)
                        stt(glu_part, bank(n % 2), vcol[:, V_BG + j:V_BG + j + 1], glu_gate, ALU.add, ALU.mult)\
                            .then_inc(p_free[n % 2], 1)
                        dve.wait_ge(p_free[n % 2], n // 2 + 1)
                        tt(ya2[:, j, :], glu_part, sza[:, j, :], ALU.mult).then_inc(ya2_ok, 1)
                    dve.wait_ge(probs_ok, hd + 1)
                    link(nc.vector.reciprocal(hs[:, 4 * h + 3, :], hs[:, 4 * h + 2, :]))
                    dve.wait_ge(o_ready, hd + 1)
                    for q in range(TT):
                        last = ts(o_s[:, q, h * DH:(h + 1) * DH], PS[:, M0, q * DH:(q + 1) * DH],
                                  hs[:, 4 * h + 3, q:q + 1], None, ALU.mult)
                        if q < TT - 1:
                            do(last)
                    last.then_inc(o_copied, 1)
                    dve.wait_ge(mod_gate_in[h], 16 * (j + 1))
                    if hd:
                        dve.wait_ge(mod_used, FT + hd)
                    add_w_mod(0, mod_sum_gate, mod_ring_gate[h], silc[:, 0, hd:hd + 1], hd == 0)
                dve.wait_ge(feats_t, j + 1)
                tt(tmpf[:, 0, :], bank(M0), szb[:, j, :], ALU.mult).then_inc(feats_c, 1)
                dve.wait_ge(feats_c, j + 1)
                link(ts(BH[:, 4 + j, :], tmpf[:, 0, :], 1.0, None, ALU.mult))
                tt(BL[:, 4 + j, :], tmpf[:, 0, :], BH[:, 4 + j, :].bitcast(fp32), ALU.subtract).then_inc(yb_l, 1)
                dve.wait_ge(yb_l, j + 1)
            link(nc.vector.memset(mod_sum2, 0.0))
            dve.wait_ge(mod_done, 2)
            tt(mod1[:, 2 * FT:NMOD], PS[:, Z0, 0:FT], vcol[:, V_BM1 + 2 * FT:V_BM1 + NMOD], ALU.add).then_inc(mod_gate, 1)
            dve.wait_ge(ya2_h, 1)
            tt(BL[:, 0:4, :], ya2, BH[:, 0:4, :].bitcast(fp32), ALU.subtract).then_inc(ya2_l, 1)
            with dve.Fori(0, FT // 2) as i:
                for jj in range(2):
                    n = Item(GATE + 4 * jj, i, 8)
                    for third in range(3):
                        dve.wait_ge(mod_in[third], Item(16 * jj, i, 32).value(16))
                        dve.wait_ge(mod_used, Item(2 * FT + 3 * jj + third, i, 6).value(-2))
                        add_w_mod(1, mod_sum2[:, third * D:(third + 1) * D], mod_ring[third],
                                  silc[:, 1, bass.ds(i * 2 + jj, 1)])
                    for k in range(2):
                        dve.wait_ge(p_free[k], (n + k).turns(2, add=1))
                        dve.wait_ge(tile_done, (n + 2 + k).value(1))
                        tt(parts_ab[:, k, :], bank(k), gates[:, k, :], ALU.mult).then_inc(p_free[k], 1)
                    for k in range(2):
                        dve.wait_ge(p_free[k], (n + 2 + k).turns(2, add=1))
                    tt(merged1[:, bass.ds(i * 2 + jj, 1), :].rearrange("p a b -> p (a b)"), parts_ab[:, 0, :],
                       parts_ab[:, 1, :], ALU.add).then_inc(mg_ok, 1)
                    dve.wait_ge(mg_ok, Item(jj, i, 2).value(1))

            def low_merged(layer, m):
                for f in range(FT):
                    dve.wait_ge(mg_h, FT * layer + f + 1)
                    tt(AL[:, f, :], m[:, f, :], AH[:, f, :].bitcast(fp32), ALU.subtract).then_inc(mg_l, 1)

            def times_gain(layer, j):
                dve.wait_ge(sq[0], TT * (FT * layer + j + 1))
                v = x_tok[:, :, j * P:(j + 1) * P]
                tt(v, v, gain[:, j * P:(j + 1) * P].unsqueeze(1).broadcast_to([P, TT, P]), ALU.mult).then_inc(scaled, 1)

            def add_outputs(layer):
                dve.wait_ge(gain_in, 16 * (layer + 1))
                for j in range(FT):
                    dve.wait_ge(wo_t, FT * layer + j + 1)
                    v = x_tok[:, :, j * P:(j + 1) * P]
                    tt(v, v, bank(T0 + j % 2).rearrange("p (t c) -> p t c", t=TT), ALU.add).then_inc(wo_add, 1)
                    if layer == 0 and j == 2:
                        modulations(1)
                    if j:
                        times_gain(layer, j - 1)

            low_merged(0, merged1)
            add_outputs(0)
            times_gain(0, FT - 1)
            for part in range(2):
                dve.wait_ge(sq[part], TT * FT)
            link(nc.vector.tensor_reduce(stat[:, 0:2, :], norm_parts, AX.X, ALU.add))
            link(ts(stat[:, 0, :], stat[:, 0, :], 1.0 / D, EPS, ALU.mult, ALU.add))
            link(ts(stat[:, 1, :], stat[:, 1, :], 1.0 / D, None, ALU.mult))
            stt(stat[:, 1, :], stat[:, 0, :], EPS, stat[:, 1, :], ALU.mult, ALU.add).then_inc(ms_ok, 1)
            dve.wait_ge(root, 2)
            link(nc.vector.reciprocal(stat[:, 0:2, :], stat[:, 2:4, :]))
            diagonals(stat[:, 1, :])
            for f in range(FT):
                low_features(1, f)
            for t in range(TT):
                do(ts(x_tok[:, t, :], x_tok[:, t, :], stat[:, 0, t:t + 1], None, ALU.mult))
            steps.settle()
            link(nc.vector.memset(zeros, 0.0))
            link(nc.vector.memset(Pw, 1.0))
            starts = {3: 0, 2: 513, 0: 898, 1: 1027}
            steps.begin_loop()
            with dve.Fori(0, FT // 2) as i:
                steps.begin_trip(i, 2 * (2 * 10 + 1))
                for jj in range(2):
                    n, pair = Item(L2 + 6 * jj, i, 12), Item(jj, i, 2)

                    def masked2(h):
                        hd = Item(H1 + 2 * jj + h, i, 4)
                        dve.wait_ge(z_ready, hd.value(1))
                        for q, _, b, cb in SEGS:
                            v = PS[:, b, cb + q * P:cb + (q + 1) * P]
                            last = tt(v, v, tri2[:, :], ALU.add)
                            if q != 1:
                                do(last)
                        last.then_inc(head2_m, 1)

                    def products(h):
                        hd = Item(H1 + 2 * jj + h, i, 4)
                        dve.wait_ge(z_gates, hd.value(1 - H1))
                        dve.wait_ge(probs_ok, hd.value())
                        for q, c0, _, _ in SEGS:
                            w, s0 = (q + 1) * P, starts[q]
                            do(nc.vector.tensor_tensor_scan(Pw[:, s0:s0 + w][:, ::-1], om[h][:, c0:c0 + w][:, ::-1],
                                                            zeros[:, 0:w], 1.0, ALU.mult, ALU.add))
                        steps.settle()
                        for q, c0, _, _ in SEGS:
                            w, s0 = (q + 1) * P, starts[q]
                            last = tt(beta[h][:, c0:c0 + w], beta[h][:, c0:c0 + w], Pw[:, s0 + 1:s0 + 1 + w], ALU.mult)
                            if q != 1:
                                do(last)
                        last.then_inc(probs_ok, 1)

                    def outputs(h):
                        hd = Item(H1 + 2 * jj + h, i, 4)
                        if h == 0:
                            dve.wait_ge(feats_t, pair.value(4))
                        dve.wait_ge(o_ready, hd.value(1))
                        nc.vector.tensor_copy(o2[:, :, h * DH:(h + 1) * DH],
                                              PS[:, M0, 0:TT * DH].rearrange("p (t c) -> p t c", t=TT))\
                            .then_inc(o_copied, 1)

                    masked2(0)
                    products(0)
                    dve.wait_ge(gate2_sig, Item(2 * jj, i, 4).value(1))
                    tt(sza2, bank(1), sza2, ALU.mult).then_inc(p_free[1], 1)
                    masked2(1)
                    products(1)
                    dve.wait_ge(tile_done, (n + 4).value(1))
                    ts(uT[:, bass.ds(i * 2 + jj, 1), :].rearrange("p a b -> p (a b)"), bank(0), 1.0, None, ALU.mult)\
                        .then_inc(p_free[0], 1)
                    outputs(0)
                    dve.wait_ge(gate2_sig, Item(2 * jj, i, 4).value(2))
                    tt(szb2[:, bass.ds(i * 2 + jj, 1), :].rearrange("p a b -> p (a b)"), bank(1), tmpf[:, 0, :],
                       ALU.mult).then_inc(p_free[1], 1)
                    outputs(1)
                    dve.wait_ge(feats_t, pair.value(5))
                    tt(tmpf[:, 1, :], bank(M0), sza2, ALU.mult).then_inc(feats_c, 1)
                    dve.wait_ge(feats_c, pair.value(5))
                    high = BH[:, bass.ds(i * 2 + jj, 1), :].rearrange("p a b -> p (a b)")
                    link(ts(high, tmpf[:, 1, :], 1.0, None, ALU.mult))
                    tt(BL[:, bass.ds(i * 2 + jj, 1), :].rearrange("p a b -> p (a b)"), tmpf[:, 1, :], high.bitcast(fp32),
                       ALU.subtract).then_inc(y2b_ok, 1)
            steps.end_loop(FT // 2)
            dve.wait_ge(tables, 2)
            steps.begin_loop()
            with dve.Fori(0, FT // 2) as i:
                steps.begin_trip(i, 14)
                for jj in range(2):
                    n = Item(MA + 2 * jj, i, 4)
                    u = uT[:, bass.ds(i * 2 + jj, 1), :].rearrange("p a b -> p (a b)")
                    link(ts(padded[:, 0, PAD:PAD + S], u, 1.0, None, ALU.mult))
                    for k in range(4):
                        src = padded[:, k % 2, :]
                        link(stt(padded[:, (k + 1) % 2, PAD:PAD + S], src[:, PAD - 2 ** k:PAD + S - 2 ** k],
                                 shifts[:, bass.ds(i, 1), k:k + 1].rearrange("p a b -> p (a b)"), src[:, PAD:PAD + S],
                                 ALU.mult, ALU.add))
                    total, few = padded[:, 0, PAD:PAD + S], WINDOWS[-1]
                    link(tt(total[:, 0:few], total[:, 0:few],
                            inv_count[:, bass.ds(i, 1), :].rearrange("p a b -> p (a b)"), ALU.mult))
                    link(tt(u[:, 0:few], total[:, 0:few], u[:, 0:few], ALU.subtract))
                    stt(u[:, few:S], total[:, few:S], inv_win[:, bass.ds(i, 1)], u[:, few:S], ALU.mult, ALU.subtract)\
                        .then_inc(d_ok, 1)
                    dve.wait_ge(d_ok, Item(jj, i, 2).value(1))
                    dve.wait_ge(p_free[0], n.turns(2, add=1))
                    dve.wait_ge(tile_done, (n + 1).value(1))
                    tt(part_a[:, bass.ds(i * 2 + jj, 1), :].rearrange("p a b -> p (a b)"), bank(1), gates2, ALU.mult)\
                        .then_inc(p_free[1], 1)
            steps.end_loop(FT // 2)
            for f in range(FT):
                dve.wait_ge(d_h, f + 1)
                tt(BL[:, f, :], uT[:, f, :], BH[:, f, :].bitcast(fp32), ALU.subtract).then_inc(d_l, 1)
            for f in range(FT):
                dve.wait_ge(p_free[f % 2], (POOLW + f) // 2 + 1)
                tt(wide[:, f % 2, :], wide[:, f % 2, :], szb2[:, f, :], ALU.mult).then_inc(pw_v, 1)
                dve.wait_ge(pw_h, f + 1)
                tt(BL[:, f, :], wide[:, f % 2, :], BH[:, f, :].bitcast(fp32), ALU.subtract).then_inc(pw_l, 1)
            with dve.Fori(0, FT // 2) as i:
                for jj in range(2):
                    n = Item(MB + 2 * jj, i, 4)
                    dve.wait_ge(p_free[0], n.turns(2, add=1))
                    dve.wait_ge(tile_done, (n + 1).value(1))
                    tt(prod2, bank(1), gates2, ALU.mult).then_inc(p_free[1], 1)
                    dve.wait_ge(p_free[1], (n + 1).turns(2, add=1))
                    tt(merged2[:, bass.ds(i * 2 + jj, 1), :].rearrange("p a b -> p (a b)"),
                       part_a[:, bass.ds(i * 2 + jj, 1), :].rearrange("p a b -> p (a b)"), prod2, ALU.add)\
                        .then_inc(mg2_ok, 1)
                    dve.wait_ge(mg2_ok, Item(jj, i, 2).value(1))
            low_merged(1, merged2)
            add_outputs(1)
            dve.wait_ge(sq[0], 2 * TT * FT)
            link(nc.vector.tensor_reduce(stat[:, 0:1, :], norm_parts[:, 0:1, :, :], AX.X, ALU.add))
            ts(stat[:, 0, :], stat[:, 0, :], 1.0 / D, EPS, ALU.mult, ALU.add).then_inc(ms_ok, 1)
            times_gain(1, FT - 1)
            dve.wait_ge(root, 3)
            nc.vector.reciprocal(stat[:, 0, :], stat[:, 2, :]).then_inc(inv_ok, 1)
            dve.wait_ge(inv_ok, 1)
            dve.wait_ge(scaled, 2 * FT)
            for t in range(0, TT, 2):
                ts(x_tok[:, t, :], x_tok[:, t, :], stat[:, 0, t:t + 1], None, ALU.mult).then_inc(out_dve, 1)


_INS = ["x", "c", "norm_g", "w_mod", "b_mod", "w_in", "a_re", "a_im", "b_re", "b_im", "c_re", "c_im", "d_skip",
        "log_dt", "w_glu", "b_glu", "w_a_o", "w_b_o", "w_out", "final_g", "c_2", "norm_gain_2", "w_ada_2", "b_ada_2",
        "w_in_2", "pool_w_2", "pool_scale_2", "w_branch_a_2", "w_branch_b_2", "w_out_2", "final_gain_2"]
_OUTS = [((1, 512, 1024), "float32")]


def kernel(**inputs):
    import numpy as _np
    import concourse.bacc as _bacc
    from concourse import mybir as _mybir
    from concourse.bass_utils import run_bass_kernel_spmd as _run

    nc = _bacc.Bacc("TRN2", target_bir_lowering=False, num_devices=1)
    arrays, args = {}, []
    for name in _INS:
        a = _np.ascontiguousarray(inputs[name])
        arrays[f"in_{name}_dram"] = a
        args.append(nc.dram_tensor(f"in_{name}_dram", a.shape, _mybir.dt.from_np(a.dtype), kind="ExternalInput").ap())
    for i, (shape, dtype) in enumerate(_OUTS):
        dt = _mybir.dt.from_np(_np.dtype(dtype))
        args.append(nc.dram_tensor(f"out_{i}_dram", shape, dt, kind="ExternalOutput").ap())
    hybrid_two_layers(nc, *args)
    r = _run(nc, [arrays], core_ids=[0])
    got = tuple(r.results[0][f"out_{i}_dram"] for i in range(len(_OUTS)))
    return got[0]
```
